# Optimizing a Trainium2 kernel written in Bass

```python
import math
import jax, jax.numpy as jnp
from jax import lax
import numpy as np

D_MODEL = 1024
BATCH = 1
SEQ = 256
DEPTH = 2
DEC_BATCH = 8
DEC_SEQ = 8
PAST_LEN = 2048
PAGE_SIZE = 128

N_PAIRS = DEPTH // 2
D_A = D_MODEL // 2
CONV_A = 31
D_INNER = D_MODEL
SSM_HEADDIM = 64
SSM_HEADS = D_INNER // SSM_HEADDIM
SSM_GROUPS = 2
SSM_STATE = 128
SSM_CONV = 4
CONV_DIM = D_INNER + 2 * SSM_GROUPS * SSM_STATE
SSD_CHUNK = 128
HEAD_DIM = 64
N_HEADS = (D_MODEL // 2) // HEAD_DIM
N_KV = 2
ROT_DIM = HEAD_DIM // 4
ROPE_THETA = 500000.0
IDX_HEADS = 4
IDX_DIM = 64
TOPK_MAX = 256
Q_BLOCK = 128
D_D = D_MODEL // 2
CONV_D = 3
D_FF = 2816
N_EXPERTS = 8
TOP_K = 2
EPS = 1e-6
NEG = -1e30

E_SPLIT = [D_A, D_A, D_INNER, CONV_DIM, SSM_HEADS]
O_SPLIT = [N_HEADS * HEAD_DIM, N_KV * HEAD_DIM, N_KV * HEAD_DIM, IDX_HEADS * IDX_DIM, IDX_DIM, IDX_HEADS, D_D, D_D, D_D]
E_IN = sum(E_SPLIT)
O_IN = sum(O_SPLIT)
E_MIX = D_A + D_INNER
O_MIX = N_HEADS * HEAD_DIM + D_D

kernel_name = 'hybrid_conformer_ssd_dsa_decoder_step'

F32 = jnp.float32

def split_cols(z, sizes):
    offs = np.cumsum(sizes)[:-1].tolist()
    return jnp.split(z, offs, axis=-1)

def rms_norm(x, g):
    xf = x.astype(F32)
    y = xf * lax.rsqrt(jnp.mean(xf * xf, axis=-1, keepdims=True) + EPS)
    return (y * g.astype(F32)).astype(x.dtype)

def layer_norm(x, g, b):
    xf = x.astype(F32)
    mu = jnp.mean(xf, axis=-1, keepdims=True)
    var = jnp.mean(jnp.square(xf - mu), axis=-1, keepdims=True)
    return ((xf - mu) * lax.rsqrt(var + EPS) * g.astype(F32) + b.astype(F32)).astype(x.dtype)

def rope(x, pos):
    half = ROT_DIM // 2
    inv = ROPE_THETA ** (-jnp.arange(half, dtype=F32) / half)
    ang = pos.astype(F32)[:, None] * inv[None, :]
    cos = jnp.cos(ang)[None, :, None, :]
    sin = jnp.sin(ang)[None, :, None, :]
    xr = x[..., :ROT_DIM].astype(F32)
    x1, x2 = xr[..., :half], xr[..., half:]
    rot = jnp.concatenate([x1 * cos - x2 * sin, x1 * sin + x2 * cos], axis=-1).astype(x.dtype)
    return jnp.concatenate([rot, x[..., ROT_DIM:]], axis=-1)

def causal_dw_conv(x, prev, w, bias=None):
    k_w = w.shape[0]
    xp = jnp.concatenate([prev.astype(x.dtype), x], axis=1)
    y = lax.conv_general_dilated(xp, w[:, None, :].astype(x.dtype), window_strides=(1,), padding='VALID',
                                 dimension_numbers=('NWC', 'WIO', 'NWC'), feature_group_count=x.shape[-1])
    if bias is not None:
        y = y + bias.astype(x.dtype)
    return y, xp[:, xp.shape[1] - (k_w - 1):]

def ssd_scan(x, dt, a, bm, cm, h0, chunk):
    b, L, H, P = x.shape
    G, N = bm.shape[2], bm.shape[3]
    R = H // G
    nc = L // chunk
    xc = x.astype(F32).reshape(b, nc, chunk, G, R, P)
    dtc = dt.astype(F32).reshape(b, nc, chunk, G, R)
    bc = bm.astype(F32).reshape(b, nc, chunk, G, N)
    cc = cm.astype(F32).reshape(b, nc, chunk, G, N)
    a_cum = jnp.cumsum(dtc * a.reshape(G, R), axis=2)
    causal = jnp.tril(jnp.ones((chunk, chunk), bool))[None, None, :, :, None, None]
    seg = a_cum[:, :, :, None] - a_cum[:, :, None, :]
    decay = jnp.where(causal, jnp.exp(jnp.where(causal, seg, 0.0)), 0.0)
    cb = jnp.einsum('bctgn,bcsgn->bctsg', cc, bc)
    wts = cb[..., None] * decay * dtc[:, :, None]
    y = jnp.einsum('bctsgr,bcsgrp->bctgrp', wts, xc)
    to_end = jnp.exp(a_cum[:, :, -1:] - a_cum) * dtc
    states = jnp.einsum('bclgr,bclgrp,bclgn->bcgrpn', to_end, xc, bc)
    chunk_decay = jnp.exp(a_cum[:, :, -1])

    def step(h, inp):
        s, d = inp
        return h * d[..., None, None] + s, h

    h_init = h0.astype(F32).reshape(b, G, R, P, N)
    h_last, h_start = lax.scan(step, h_init, (jnp.moveaxis(states, 1, 0), jnp.moveaxis(chunk_decay, 1, 0)))
    h_start = jnp.moveaxis(h_start, 0, 1)
    y = y + jnp.einsum('bctgn,bcgrpn,bctgr->bctgrp', cc, h_start, jnp.exp(a_cum))
    return y.reshape(b, L, H, P), h_last.reshape(b, H, P, N)

def even_mixer(h, conv_a_prev, ssm_prev, conv_b_prev, chunk, w_in, conv_a_w, conv_a_b, ln_a_g, ln_a_b,
               conv_b_w, conv_b_b, dt_bias, a_log, d_skip, ssm_norm, w_out):
    b, L, _ = h.shape
    a_val, a_gate, z, xbc, dt_raw = split_cols(h @ w_in, E_SPLIT)
    u = a_val * jax.nn.sigmoid(a_gate)
    ua, conv_a_new = causal_dw_conv(u, conv_a_prev, conv_a_w, conv_a_b)
    ya = jax.nn.silu(layer_norm(ua, ln_a_g, ln_a_b))
    xbc_c, conv_b_new = causal_dw_conv(xbc, conv_b_prev, conv_b_w, conv_b_b)
    xs, bm, cm = split_cols(jax.nn.silu(xbc_c), [D_INNER, SSM_GROUPS * SSM_STATE, SSM_GROUPS * SSM_STATE])
    dt = jax.nn.softplus(dt_raw.astype(F32) + dt_bias.astype(F32))
    a = -jnp.exp(a_log.astype(F32))
    xh = xs.reshape(b, L, SSM_HEADS, SSM_HEADDIM)
    y, ssm_new = ssd_scan(xh, dt, a, bm.reshape(b, L, SSM_GROUPS, SSM_STATE),
                          cm.reshape(b, L, SSM_GROUPS, SSM_STATE), ssm_prev, chunk)
    y = y + d_skip.astype(F32)[:, None] * xh.astype(F32)
    y = y.reshape(b, L, D_INNER) * jax.nn.silu(z.astype(F32))
    y = y.reshape(b, L, SSM_GROUPS, D_INNER // SSM_GROUPS)
    y = y * lax.rsqrt(jnp.mean(y * y, axis=-1, keepdims=True) + EPS)
    yb = (y.reshape(b, L, D_INNER) * ssm_norm.astype(F32)).astype(h.dtype)
    out = jnp.concatenate([ya, yb], axis=-1) @ w_out
    return out, conv_a_new, ssm_new.astype(ssm_prev.dtype), conv_b_new

def odd_project(h, pos, w_in, q_norm, k_norm, kidx_g, kidx_b):
    b, L, _ = h.shape
    q, k, v, qi, ki, wi, din, bg, cg = split_cols(h @ w_in, O_SPLIT)
    q = rope(rms_norm(q.reshape(b, L, N_HEADS, HEAD_DIM), q_norm), pos)
    k = rope(rms_norm(k.reshape(b, L, N_KV, HEAD_DIM), k_norm), pos)
    v = v.reshape(b, L, N_KV, HEAD_DIM)
    qi = rope(qi.reshape(b, L, IDX_HEADS, IDX_DIM), pos)
    ki = rope(layer_norm(ki, kidx_g, kidx_b)[:, :, None, :], pos)[:, :, 0, :]
    wi = wi * (IDX_HEADS ** -0.5 * IDX_DIM ** -0.5)
    return q, k, v, qi, ki, wi, din, bg, cg

def indexer_scores(qi, wi, ki):
    dots = jnp.einsum('bthd,bsd->bhts', qi, ki).astype(F32)
    return jnp.einsum('bhts,bth->bts', jax.nn.relu(dots), wi.astype(F32))

def sparse_attend(q, k_sel, v_sel, valid):
    b, t = q.shape[:2]
    qg = q.reshape(b, t, N_KV, N_HEADS // N_KV, HEAD_DIM)
    s = jnp.einsum('btgrd,btkgd->btgrk', qg, k_sel).astype(F32) * (HEAD_DIM ** -0.5)
    s = jnp.where(valid[:, :, None, None, :], s, NEG)
    pr = jax.nn.softmax(s, axis=-1).astype(v_sel.dtype)
    o = jnp.einsum('btgrk,btkgd->btgrd', pr, v_sel)
    return o.reshape(b, t, N_HEADS * HEAD_DIM)

def prompt_dsa(q, k, v, qi, ki, wi):
    b, s_len = q.shape[:2]
    topk = min(TOPK_MAX, s_len // 4)
    nb = s_len // Q_BLOCK
    key_pos = jnp.arange(s_len)
    bi = jnp.arange(b)[:, None, None]

    def blk(arr):
        return arr.reshape((b, nb, Q_BLOCK) + arr.shape[2:]).swapaxes(0, 1)

    def one(args):
        qb, qib, wib, start = args
        qpos = start + jnp.arange(Q_BLOCK)
        sc = indexer_scores(qib, wib, ki)
        sc = jnp.where((key_pos[None, :] <= qpos[:, None])[None], sc, NEG)
        _, idx = lax.top_k(sc, topk)
        valid = idx <= qpos[None, :, None]
        return sparse_attend(qb, k[bi, idx], v[bi, idx], valid)

    starts = jnp.arange(nb, dtype=jnp.int32) * Q_BLOCK
    out = lax.map(one, (blk(q), blk(qi), blk(wi), starts))
    return out.swapaxes(0, 1).reshape(b, s_len, N_HEADS * HEAD_DIM)

def sample_dsa(q, k, v, qi, ki, wi, cache_k, cache_v, cache_kidx, page_table):
    bd, t_len = q.shape[:2]
    past = page_table.shape[1] * PAGE_SIZE
    total = past + t_len
    topk = min(TOPK_MAX, total // 4)
    ki_past = cache_kidx[page_table].reshape(bd, past, IDX_DIM)
    ki_all = jnp.concatenate([ki_past.astype(ki.dtype), ki], axis=1)
    qpos = past + jnp.arange(t_len)
    sc = indexer_scores(qi, wi, ki_all)
    sc = jnp.where((jnp.arange(total)[None, :] <= qpos[:, None])[None], sc, NEG)
    _, idx = lax.top_k(sc, topk)
    bi = jnp.arange(bd)[:, None, None]
    from_past = (idx < past)[..., None, None]
    pidx = jnp.minimum(idx, past - 1)
    page = page_table[bi, pidx // PAGE_SIZE]
    off = pidx % PAGE_SIZE
    nidx = jnp.clip(idx - past, 0, t_len - 1)
    k_sel = jnp.where(from_past, cache_k[page, off].astype(k.dtype), k[bi, nidx])
    v_sel = jnp.where(from_past, cache_v[page, off].astype(v.dtype), v[bi, nidx])
    valid = idx <= qpos[None, :, None]
    return sparse_attend(q, k_sel, v_sel, valid)

def short_conv_mixer(din, bg, cg, prev, conv_w):
    y, new_buf = causal_dw_conv(cg * din, prev, conv_w)
    return bg * y, new_buf

def swiglu(h, w_gate, w_up, w_down):
    return (jax.nn.silu(h @ w_gate) * (h @ w_up)) @ w_down

def moe_swiglu(h, w_router, b_router, we_gate, we_up, we_down):
    logits = (h @ w_router).astype(F32) + b_router.astype(F32)
    top_v, top_i = lax.top_k(logits, TOP_K)
    gates = jax.nn.softmax(top_v, axis=-1)
    comb = jnp.sum(jax.nn.one_hot(top_i, N_EXPERTS, dtype=F32) * gates[..., None], axis=-2)
    out = jnp.zeros(h.shape, F32)
    for e in range(N_EXPERTS):
        out = out + comb[..., e:e + 1] * swiglu(h, we_gate[e], we_up[e], we_down[e]).astype(F32)
    return out.astype(h.dtype)

def setup_inputs(seed: int = 0) -> dict:
    key = jax.random.key(seed)
    keys = jax.random.split(key, 64)
    ctr = [0]

    def nk():
        ctr[0] += 1
        return keys[ctr[0] - 1]

    def nrm(shape, scale):
        return scale * jax.random.normal(nk(), shape, F32)

    def gain(shape):
        return 1.0 + nrm(shape, 0.02)

    NP = N_PAIRS
    n_pages = PAST_LEN // PAGE_SIZE
    n_used = DEC_BATCH * n_pages
    n_pool = (5 * n_used + 3) // 4
    perm = jax.random.permutation(nk(), n_pool)
    page_table = perm[:n_used].reshape(DEC_BATCH, n_pages).astype(jnp.int32)
    dt0 = jnp.exp(jax.random.uniform(nk(), (NP, SSM_HEADS), F32, math.log(1e-3), math.log(1e-1)))
    dt_bias = dt0 + jnp.log(-jnp.expm1(-dt0))
    a_log = jnp.log(jax.random.uniform(nk(), (NP, SSM_HEADS), F32, 1.0, 16.0))
    return {
        'x_prompt': nrm((BATCH, SEQ, D_MODEL), 1.0),
        'x_sample': nrm((DEC_BATCH, DEC_SEQ, D_MODEL), 1.0),
        'state_conv_a': nrm((NP, DEC_BATCH, CONV_A - 1, D_A), 0.5),
        'state_ssm': nrm((NP, DEC_BATCH, SSM_HEADS, SSM_HEADDIM, SSM_STATE), 0.1),
        'state_conv_b': nrm((NP, DEC_BATCH, SSM_CONV - 1, CONV_DIM), 0.5),
        'cache_k': nrm((NP, n_pool, PAGE_SIZE, N_KV, HEAD_DIM), 1.0),
        'cache_v': nrm((NP, n_pool, PAGE_SIZE, N_KV, HEAD_DIM), 1.0),
        'cache_kidx': nrm((NP, n_pool, PAGE_SIZE, IDX_DIM), 1.0),
        'state_conv_d': nrm((NP, DEC_BATCH, CONV_D - 1, D_D), 0.5),
        'page_table': page_table,
        'e_norm_mix': gain((NP, D_MODEL)),
        'e_w_in': nrm((NP, D_MODEL, E_IN), D_MODEL ** -0.5),
        'e_conv_a_w': nrm((NP, CONV_A, D_A), CONV_A ** -0.5),
        'e_conv_a_b': nrm((NP, D_A), 0.02),
        'e_ln_a_g': gain((NP, D_A)),
        'e_ln_a_b': nrm((NP, D_A), 0.02),
        'e_conv_b_w': nrm((NP, SSM_CONV, CONV_DIM), SSM_CONV ** -0.5),
        'e_conv_b_b': nrm((NP, CONV_DIM), 0.02),
        'e_dt_bias': dt_bias,
        'e_a_log': a_log,
        'e_d_skip': 1.0 + nrm((NP, SSM_HEADS), 0.1),
        'e_ssm_norm': gain((NP, D_INNER)),
        'e_w_out': nrm((NP, E_MIX, D_MODEL), E_MIX ** -0.5),
        'e_norm_ffn': gain((NP, D_MODEL)),
        'e_w_gate': nrm((NP, D_MODEL, D_FF), D_MODEL ** -0.5),
        'e_w_up': nrm((NP, D_MODEL, D_FF), D_MODEL ** -0.5),
        'e_w_down': nrm((NP, D_FF, D_MODEL), D_FF ** -0.5),
        'o_norm_mix': gain((NP, D_MODEL)),
        'o_w_in': nrm((NP, D_MODEL, O_IN), D_MODEL ** -0.5),
        'o_q_norm': gain((NP, HEAD_DIM)),
        'o_k_norm': gain((NP, HEAD_DIM)),
        'o_kidx_g': gain((NP, IDX_DIM)),
        'o_kidx_b': nrm((NP, IDX_DIM), 0.02),
        'o_conv_d_w': nrm((NP, CONV_D, D_D), CONV_D ** -0.5),
        'o_w_out': nrm((NP, O_MIX, D_MODEL), O_MIX ** -0.5),
        'o_norm_ffn': gain((NP, D_MODEL)),
        'o_w_router': nrm((NP, D_MODEL, N_EXPERTS), D_MODEL ** -0.5),
        'o_b_router': nrm((NP, N_EXPERTS), 0.01),
        'o_we_gate': nrm((NP, N_EXPERTS, D_MODEL, D_FF), D_MODEL ** -0.5),
        'o_we_up': nrm((NP, N_EXPERTS, D_MODEL, D_FF), D_MODEL ** -0.5),
        'o_we_down': nrm((NP, N_EXPERTS, D_FF, D_MODEL), D_FF ** -0.5),
    }

def reference(x_prompt, x_sample, state_conv_a, state_ssm, state_conv_b, cache_k, cache_v, cache_kidx, state_conv_d,
              page_table, e_norm_mix, e_w_in, e_conv_a_w, e_conv_a_b, e_ln_a_g, e_ln_a_b, e_conv_b_w, e_conv_b_b,
              e_dt_bias, e_a_log, e_d_skip, e_ssm_norm, e_w_out, e_norm_ffn, e_w_gate, e_w_up, e_w_down,
              o_norm_mix, o_w_in, o_q_norm, o_k_norm, o_kidx_g, o_kidx_b, o_conv_d_w, o_w_out, o_norm_ffn,
              o_w_router, o_b_router, o_we_gate, o_we_up, o_we_down):
    bp, s_len = x_prompt.shape[:2]
    bd, t_len = x_sample.shape[:2]
    past = page_table.shape[1] * PAGE_SIZE
    pos_p = jnp.arange(s_len)
    pos_s = past + jnp.arange(t_len)
    xp, xs = x_prompt, x_sample
    p_ca, p_ssm, p_cb, p_k, p_v, p_ki, p_cd = [], [], [], [], [], [], []
    s_ca, s_ssm, s_cb, s_k, s_v, s_ki, s_cd = [], [], [], [], [], [], []
    for layer in range(DEPTH):
        i = layer // 2
        if layer % 2 == 0:
            ew = (e_w_in[i], e_conv_a_w[i], e_conv_a_b[i], e_ln_a_g[i], e_ln_a_b[i], e_conv_b_w[i], e_conv_b_b[i],
                  e_dt_bias[i], e_a_log[i], e_d_skip[i], e_ssm_norm[i], e_w_out[i])
            mp, ca, sm, cb = even_mixer(rms_norm(xp, e_norm_mix[i]),
                                        jnp.zeros((bp, CONV_A - 1, D_A), xp.dtype),
                                        jnp.zeros((bp, SSM_HEADS, SSM_HEADDIM, SSM_STATE), xp.dtype),
                                        jnp.zeros((bp, SSM_CONV - 1, CONV_DIM), xp.dtype),
                                        min(SSD_CHUNK, s_len), *ew)
            xp = xp + mp
            p_ca.append(ca); p_ssm.append(sm); p_cb.append(cb)
            ms, ca, sm, cb = even_mixer(rms_norm(xs, e_norm_mix[i]), state_conv_a[i], state_ssm[i],
                                        state_conv_b[i], t_len, *ew)
            xs = xs + ms
            s_ca.append(ca); s_ssm.append(sm); s_cb.append(cb)
            xp = xp + swiglu(rms_norm(xp, e_norm_ffn[i]), e_w_gate[i], e_w_up[i], e_w_down[i])
            xs = xs + swiglu(rms_norm(xs, e_norm_ffn[i]), e_w_gate[i], e_w_up[i], e_w_down[i])
        else:
            ow = (o_w_in[i], o_q_norm[i], o_k_norm[i], o_kidx_g[i], o_kidx_b[i])
            q, k, v, qi, ki, wi, din, bg, cg = odd_project(rms_norm(xp, o_norm_mix[i]), pos_p, *ow)
            att = prompt_dsa(q, k, v, qi, ki, wi)
            dm, cd = short_conv_mixer(din, bg, cg, jnp.zeros((bp, CONV_D - 1, D_D), xp.dtype), o_conv_d_w[i])
            xp = xp + jnp.concatenate([att, dm], axis=-1) @ o_w_out[i]
            p_k.append(k); p_v.append(v); p_ki.append(ki); p_cd.append(cd)
            q, k, v, qi, ki, wi, din, bg, cg = odd_project(rms_norm(xs, o_norm_mix[i]), pos_s, *ow)
            att = sample_dsa(q, k, v, qi, ki, wi, cache_k[i], cache_v[i], cache_kidx[i], page_table)
            dm, cd = short_conv_mixer(din, bg, cg, state_conv_d[i], o_conv_d_w[i])
            xs = xs + jnp.concatenate([att, dm], axis=-1) @ o_w_out[i]
            s_k.append(k); s_v.append(v); s_ki.append(ki); s_cd.append(cd)
            xp = xp + moe_swiglu(rms_norm(xp, o_norm_ffn[i]), o_w_router[i], o_b_router[i],
                                 o_we_gate[i], o_we_up[i], o_we_down[i])
            xs = xs + moe_swiglu(rms_norm(xs, o_norm_ffn[i]), o_w_router[i], o_b_router[i],
                                 o_we_gate[i], o_we_up[i], o_we_down[i])
    return (xp, xs,
            jnp.stack(p_ca), jnp.stack(p_ssm), jnp.stack(p_cb), jnp.stack(p_k), jnp.stack(p_v), jnp.stack(p_ki), jnp.stack(p_cd),
            jnp.stack(s_ca), jnp.stack(s_ssm), jnp.stack(s_cb), jnp.stack(s_k), jnp.stack(s_v), jnp.stack(s_ki), jnp.stack(s_cd))


_drawn_inputs = setup_inputs


def setup_inputs(seed=0):
    import zlib

    import numpy as np

    out = dict(_drawn_inputs(seed))
    spreads = {}
    factors = {'o_q_norm': 10.702, 'o_kidx_g': 3.631, 'o_kidx_b': 2.928, 'o_b_router': 3.513}
    for name, (base, spread) in spreads.items():
        noise = np.random.default_rng([zlib.crc32(name.encode()), seed]).standard_normal(out[name].shape)
        drawn = base * np.exp(spread * noise) if base else spread * noise
        out[name] = __import__('jax').numpy.asarray(drawn.astype(out[name].dtype))
    for name, factor in factors.items():
        out[name] = (out[name] * factor).astype(out[name].dtype)
    return out
```

```python
from contextlib import ExitStack

import concourse.bass as bass
from concourse import mybir
from concourse.alu_op_type import AluOpType as ALU

F32 = mybir.dt.float32
I32 = mybir.dt.int32
U32 = mybir.dt.uint32
ACT = mybir.ActivationFunctionType
AX = mybir.AxisListType.X
ds = bass.ds

P = 128
D = 1024
KD = D // P
SEQ = 256
NB = 8
NT = 8
NS = NB * NT
T = SEQ + NS
TILES = [(0, 0, P), (1, P, P), (2, 2 * P, NS)]
DA = 512
CA = DA // P
WA = 31
XC = 12
WB = 4
NH = 16
HP = 64
NG = 2
NST = 128
DFF = 2816
FS = 256
NSTEP = DFF // FS
NE = 8
PAST = 2048
PAGE = 128
N_POOL = 160
NPG = PAST // PAGE
KEYS = PAST + NT
TOPP = 64
TOPS = 256
EPS = 1e-6
NEG = -1e30
TAKEN = -3e38
CAP = 128
NOVER = 2 * T // CAP - 1
NQ = 8
HD = 64
E_IN = 2 * DA + D + XC * P + NH
O_IN = 512 + 128 + 128 + 256 + 64 + 4 + 3 * DA

CONST = {}
_at = 0
for _n, _w in (("ident", 128), ("ones", 128), ("tri_p", 128), ("tri_s", 64), ("last_s", 64), ("mask_p", 128),
               ("mask_s", 64), ("causal", 512), ("new_ok", 8), ("new_neg", 8), ("cos", 24), ("sin", 24),
               ("batch", 8), ("slots", 128), ("half", 3), ("head_row", 16 * 128)):
    CONST[_n] = (_at, _w)
    _at += _w
NCONST = _at


def constants():
    import numpy as np
    c = np.zeros((P, NCONST), np.float32)

    def put(name, a):
        o, w = CONST[name]
        a = np.asarray(a, np.float32).reshape(a.shape[0], -1)
        c[:a.shape[0], o:o + a.shape[1]] = a

    i = np.arange(P)
    j = np.arange(NS)
    put("ident", np.eye(P))
    put("ones", np.ones((P, P)))
    put("tri_p", i[:, None] <= i[None, :])
    same = (j[:, None] // NT) == (j[None, :] // NT)
    put("tri_s", same & (j[:, None] <= j[None, :]))
    put("last_s", same)
    put("mask_p", np.where(i[:, None] <= i[None, :], 0, NEG))
    put("mask_s", np.where(same & (j[:, None] <= j[None, :]), 0, NEG))
    key = np.arange(SEQ)
    put("causal", np.stack([np.where(key[None] <= (i + t * P)[:, None], 0, NEG) for t in range(2)], 1))
    ok = (np.arange(NT)[None] <= (j % NT)[:, None])
    put("new_ok", ok)
    put("new_neg", np.where(ok, 0, NEG))
    half = 8
    inv = np.float32(500000.0) ** (-np.arange(half, dtype=np.float32) / np.float32(half))
    pos = np.zeros((P, 3), np.float32)
    pos[:, 0], pos[:, 1] = i, i + P
    pos[:NS, 2] = PAST + j % NT
    ang = (pos[:, :, None] * inv[None, None].astype(np.float32)).astype(np.float32)
    put("cos", np.cos(ang))
    put("sin", np.sin(ang))
    put("batch", (j[:, None] // NT) == np.arange(NB)[None])
    put("slots", np.broadcast_to(i[None], (P, P)))
    put("half", np.full((P, 3), -0.5))
    put("head_row", np.repeat(np.eye(NH, dtype=np.float32)[:, :, None], P, 2))
    return c


RING = 0
SLOT = 4096
STEP = 8 * FS * 2 + 2 * D
NSLOT = 4
TAIL = RING + 4 * SLOT
FIXED = RING + NSLOT * STEP


class Own:

    def __init__(self, eng, semaphore):
        self.eng, self.semaphore, self.n = eng, semaphore, 0

    def mark(self, ins):
        ins.then_inc(self.semaphore, 1)
        self.n += 1

    def wait(self, behind=0):
        if self.n > behind:
            self.eng.wait_ge(self.semaphore, self.n - behind)

    def link(self, ins):
        self.mark(ins)
        self.wait()


def step_program(nc, inp, out):
    with ExitStack() as ctx:
        arena = ctx.enter_context(nc.sbuf_tensor("arena", [P, 53000], F32))
        psum = ctx.enter_context(nc.psum_tensor("psum", [P, 8 * 512], F32))
        sems = {}

        def sem(name):
            if name not in sems:
                sems[name] = ctx.enter_context(nc.semaphore(name))
            return sems[name]

        where = [FIXED]

        def at(off, *dims):
            n = 1
            for d in dims:
                n *= d
            v = arena[:, off:off + n]
            if len(dims) == 2:
                v = v.rearrange("p (a b) -> p a b", a=dims[0])
            elif len(dims) == 3:
                v = v.rearrange("p (a b c) -> p a b c", a=dims[0], b=dims[1])
            elif len(dims) == 4:
                v = v.rearrange("p (a b c d) -> p a b c d", a=dims[0], b=dims[1], c=dims[2])
            return v

        def new(*dims):
            n = 1
            for d in dims:
                n *= d
            v = at(where[0], *dims)
            where[0] += n
            assert where[0] <= 53000, where[0]
            return v

        def bank(i, *dims):
            v = psum[:, 512 * i:512 * i + 512]
            if dims:
                n = 1
                for d in dims:
                    n *= d
                v = psum[:, 512 * i:512 * i + n]
                if len(dims) == 2:
                    v = v.rearrange("p (a b) -> p a b", a=dims[0])
                elif len(dims) == 3:
                    v = v.rearrange("p (a b c) -> p a b c", a=dims[0], b=dims[1])
            return v

        const = new(NCONST)
        K = {n: const[:, o:o + w] for n, (o, w) in CONST.items()}
        ident = K["ident"]
        ones = K["ones"]
        causal = K["causal"].rearrange("p (a b) -> p a b", a=2)
        cos = K["cos"].rearrange("p (a b) -> p a b", a=3)
        sin = K["sin"].rearrange("p (a b) -> p a b", a=3)
        head_row = K["head_row"].rearrange("p (a b) -> p a b", a=NH)
        HEAD_ROW = FIXED + CONST["head_row"][0]
        x = new(3, D)
        HT = where[0]
        hT = new(KD, T)
        vecA = new(CA, 37)
        vecB = new(XC, 5)
        vecD = new(KD, 5)
        rows = {}
        for n, w in (("e_dt_bias", 16), ("e_a_log", 16), ("e_d_skip", 16), ("o_q_norm", 64), ("o_k_norm", 64),
                     ("o_kidx_g", 64), ("o_kidx_b", 64), ("o_b_router", 8)):
            rows[n] = new(w)
        w_dt = new(KD, NH)
        w_router = new(KD, NE)
        pages = new(P)
        ss = new(3)
        ms = new(3)
        rstd = new(3)
        FREE = where[0]

        u_p = new(CA, WA - 1 + SEQ)
        u_s = new(CA, NB, WA - 1 + NT)
        ua = new(CA, T)
        mixT = new(CA + KD, T)
        XBC = where[0]
        xbc_p = new(XC, WB - 1 + SEQ)
        xbc_s = new(XC, NB, WB - 1 + NT)
        Z = where[0]
        z = new(3, D)
        XT = where[0]
        x_tok = new(3, D)
        xn = at(Z, 3, D)
        param_rows = at(XT, 3 * D)
        xbcT = at(TAIL, XC, T)
        b_tok = at(TAIL + XC * T, 3, NG * NST)
        TMP = TAIL + XC * T + 3 * NG * NST
        xdt = at(TMP, NH, HP)
        xw = at(TMP + D, NH, HP)
        y = at(TMP + 2 * D, NH, HP)
        b_one = at(TMP + 3 * D, 2, NG * NST)
        assert TMP + 3 * D + 512 <= FIXED
        decay = at(FREE, NH, P)
        state_a = at(TMP, 2, DA)
        state_b = at(TMP + D, XC * P)
        squares = at(TMP, CA, T)
        small = [at(TMP + 1280 + 320 * i, T) for i in range(3)]
        h_old = [at(XBC + D * i, KD, P) for i in range(2)]
        h_new = [at(XBC + 2 * D + D * i, KD, P) for i in range(2)]
        h_oldT = at(TAIL, D)
        p_state = at(TAIL, D)
        dA_rows = at(TAIL + D, D)
        c_pad = at(FREE + 4 * 286 + 4 * 8 * 38, NG, NB, NS)
        raw_dt = new(3, NH)
        dts, dA, dt_abs, dt_log = new(3, NH), new(3, NH), new(3, NH), new(3, NH)
        negcum, w_end, e_cum, e_last, neg_a, w_arg = [new(NH) for _ in range(6)]
        decs = new(KD, NB)
        u_last = at(TMP + 2 * D, CA, NS)
        xbc_last = at(TMP + 2 * D + CA * NS, XC, NB * 3)
        tail_us, tail_up, tail_xp = at(XT, 512), at(XT + 512, 512), at(XT + 1024, XC * P)
        tail_xs = mixT[:, CA:CA + 5, :].rearrange("p a b -> p (a b)")[:, 0:XC * P]
        cumT = at(TMP + 3 * D, P)
        gs, gms, grs = new(2), new(2), new(2)

        silu_t = at(FREE, 2, T)
        ff = at(FREE + 2 * T, 4, T)

        def slot(s):
            o = RING + s * STEP
            return at(o, KD, FS), at(o + KD * FS, KD, FS), at(o + 2 * KD * FS, 2, D)

        where[0] = FREE
        qT = new(4, T)
        kkT = new(2, T)
        qiT = new(4, T)
        mix1T = new(KD, T)
        v_new = new(NB, P)
        q_blk = new(NB, 64)
        WORK = where[0]
        work_s = new(KEYS)
        bias_p = new(2, SEQ)
        rep = new(4, P)
        qi_b = new(NB, 32)
        ws = new(2, NS)
        best = new(8)
        mx, nmx, sums, rsum = new(8), new(8), new(8), new(8)
        qk_ss, qk_ms, qk_rs = new(30), new(30), new(30)
        ki_s, ki_v, ki_ms, ki_rs = new(3), new(3), new(3), new(3)
        rope_t = [at(WORK + 240 * i, 3, 10, 8) for i in range(4)]
        v_tok = new(3, P)
        w_idx = new(3, 4)
        ZB = where[0]
        tok = new(3, 1092)
        q_tok = new(3, 4, P)
        qi_tok = new(3, 4, P)
        ki_tok = new(3, P)
        cd_p = at(WORK - NB * 64 - NB * P, CA, 2 + SEQ)
        cd_last = at(WORK - NB * 64 - NB * P + CA * (2 + SEQ), CA, 16)
        cd_s = at(WORK + 960, CA, NB, 2 + NT)
        state_d = at(WORK + 960 + 320, DA)
        tail_dp, tail_ds = at(ZB + 3 * 1092 + 3 * 4 * P, DA), at(ZB + 3 * 1092 + 3 * 4 * P + DA, DA)
        squares1 = at(ZB + 3 * 1092, 3, 640)
        din_t = at(ZB + 3 * 1092, CA, T)
        where[0] = ZB
        relu_s = [new(KEYS) for _ in range(2)]
        relu_p = at(ZB, 4, SEQ)
        sc_p = at(ZB + 4 * SEQ, 2, SEQ)
        kidx = [at(RING + 3 * 4096 + 1024 * i, NPG, HD) for i in range(2)]
        kidxT = [at(RING + 3 * 4096 + 2048 + 1024 * i, NPG // 2, P) for i in range(2)]
        B3 = ZB
        probs = at(B3, KEYS)
        k_pages = [at(B3 + KEYS, NPG, P), at(HEAD_ROW, NPG, P)]
        k_T = at(RING + 4 * SLOT, PAST)
        v_pages = [at(RING + 3 * 4096 + 2048 * i, NPG, P) for i in range(2)]
        probsT = at(HT, 17, P)
        probs_p = at(B3, 8, SEQ)
        probs_pT = at(HT, 8, 2, P)

        sel = at(FREE, 3, NE, CAP)
        moe_silu = at(FREE + 3 * NE * CAP, 2, CAP)
        moe_ff = at(FREE + 3 * NE * CAP + 2 * CAP, 4, CAP)
        MH = FREE + 3 * NE * CAP + 6 * CAP
        moe_h = at(MH, NE, KD, CAP)
        moe_y = at(MH, NE, D)
        xn3 = at(MH + NE * D, 3, D)
        selT = at(HT, NE, T)
        where[0] = MH + NE * D + 3 * D
        logits, routed, gate, rank = new(3, NE), new(3, NE), new(3, NE), new(3, NE)
        top, first, second = new(3, 8), new(3, NE), new(3, NE)
        top_i = new(3, 8).bitcast(U32)
        top_f = new(3, 8)
        counts, more, before = new(NE), [new(NE), new(NE)], new(NE)
        upto = [new(16), new(16)]
        over_e, over_at, over_rank = new(NOVER + 1), new(NOVER), new(3, 1)
        over_i = new(NOVER + 1).bitcast(I32)
        gap, e_gap, g_one, g_two = new(3), new(3), new(3), new(3)
        pieces1 = [(5, 512, 512), (0, 1024, 68), (1, 0, 512), (2, 1092, 512), (3, 2116, 512), (4, 1604, 512)]

        def piece1(p):
            return at(RING + p * SLOT, KD, 512)

        RSTD = [1, 6, 7, 10]

        ONCE = {
            "vector": ["dt_abs_ready", "dA_ready", "ua_centred", "ua_normed", "c_pad_ready", "dA_rows_ready",
                       "tok_cleared", "ki_centred", "din_free", "cd_last_ready", "conv_d_ready", "q_packed",
                       "sc_p_taken", "work_s_ready", "rep_ready", "bias_s_ready", "routed_ready", "gap_ready", "over_ready"
                       ],
            "scalar": ["dt_log_ready", "squares_ready", "decs_ready", "qk_squared", "ki_squared", "ws_ready",
                       "e_gap_ready"],
            "tensor": ["paramsT_mm", "dt_mm", "tails_mm", "mean_mm", "var_mm", "inter_mm", "dA_sum_mm", "stateT1_mm",
                       "wsT_mm", "isum_mm", "logits_mm", "rank_mm"],
        }
        done = {engine: 0 for engine in ONCE}

        def reached(name):
            for engine, names in ONCE.items():
                if name in names:
                    return sem(engine + "_reached"), names.index(name) + 1

        def reaches(name):
            for engine, names in ONCE.items():
                if name in names:
                    assert names[done[engine]] == name, name
                    done[engine] += 1
                    return sem(engine + "_reached"), 1

        def while_overflow(eng, body):
            eng.wait_ge(*reached("over_ready"))
            n = eng.value_load(over_i[0:1, NOVER:NOVER + 1], min_val=0, max_val=NOVER)
            with eng.Fori(0, NOVER) as w:
                with eng.If(w < n):
                    body(w)

        block = ctx.enter_context(nc.Block())

        pieces0 = [("e_w_in", 0, 8, 512 * i, 512) for i in range(2)] + \
                  [("e_w_in", 0, 8, 2048 + 512 * i, 512) for i in range(3)] + \
                  [("e_w_in", 0, 8, 1024 + 512 * i, 512) for i in range(2)] + \
                  [("e_w_out", k, n, 512 * h, 512) for h in range(2) for k, n in ((0, 8), (8, 4))]

        used0 = [("val_mm", 4), ("gate_mm", 4), ("xbc_mm", 4), ("xbc_mm", 8), ("xbc_mm", 12), ("z_mm", 6), ("z_mm", 6),
                 ("mix_out_mm", 1), ("mix_out_mm", 4), ("mix_out_mm", 5), ("mix_out_mm", 8)]

        def piece(n):
            return at(RING + (n % 4) * SLOT, 8, 512)

        @block.sync
        def _(sp):
            sp.dma_start(pages.bitcast(I32)[0:1, :], inp["page_table"].rearrange("b j -> (b j)").unsqueeze(0)
                         ).then_inc(sem("pages_in"), 16)
            sp.wait_ge(sem("pages_in"), 16)
            for i, (t, t0, n) in enumerate(TILES):
                src = inp["x_prompt"][0, t0:t0 + n, :] if t < 2 else inp["x_sample"].rearrange("b t d -> (b t) d")
                sp.dma_start(x[0:n, t, :], src).then_inc(sem("x_in"), 16)
            for n, (name, k0, nk, c0, nc_) in enumerate(pieces0):
                if n >= 4:
                    sp.wait_ge(sem(used0[n - 4][0]), used0[n - 4][1])
                sp.dma_start(piece(n)[:, 0:nk, 0:nc_],
                             inp[name][0, k0 * P:(k0 + nk) * P, c0:c0 + nc_].rearrange("(k p) n -> p k n", p=P)
                             ).then_inc(sem(f"piece{n % 4}"), 16)

            def ff_step(names, e, j):
                g, u, dn = slot(j % NSLOT)
                for dst, name, rows_ in ((g, names[0], False), (u, names[1], False), (dn, names[2], True)):
                    w = inp[name][0] if e is None else inp[name][0, e]
                    if e is not None and not isinstance(e, int):
                        w = inp[name][0, ds(e, 1)]
                        src = (w[:, j * FS:(j + 1) * FS, :].rearrange("e (k p) n -> p (e k) n", p=P) if rows_ else
                               w[:, :, j * FS:(j + 1) * FS].rearrange("e (k p) n -> p (e k) n", p=P))
                    else:
                        src = (w[j * FS:(j + 1) * FS, :].rearrange("(k p) n -> p k n", p=P) if rows_ else
                               w[:, j * FS:(j + 1) * FS].rearrange("(k p) n -> p k n", p=P))
                    sp.dma_start(dst, src).then_inc(sem(f"weights{j % NSLOT}"), 16)

            for j in range(NSTEP):
                if j < NSLOT:
                    sp.wait_ge(sem("mix_out_mm"), 5 if j == 0 else 8)
                else:
                    sp.wait_ge(sem("ff_used"), j - 3)
                ff_step(("e_w_gate", "e_w_up", "e_w_down"), None, j)
            for (p, c0, nc_), last in zip(pieces1, (8, 9, 10, 10, 11, 11)):
                sp.wait_ge(sem("ff_used"), last)
                sp.dma_start(piece1(p)[:, :, 0:nc_], inp["o_w_in"][0, :, c0:c0 + nc_].rearrange("(k p) n -> p k n", p=P)
                             ).then_inc(sem(f"piece{p}"), 16)
            sp.wait_ge(sem("cg_mm"), CA)
            for b in range(NB):
                if b >= 2:
                    sp.wait_ge(sem("kidxT_mm"), 2 * (b - 1))
                with sp.Fori(0, NPG) as j:
                    page = sp.value_load(pages.bitcast(I32)[0:1, ds(j + b * NPG, 1)], min_val=0, max_val=N_POOL - 1)
                    sp.dma_start(kidx[b % 2][:, ds(j, 1), :], inp["cache_kidx"][0, ds(page, 1)].rearrange("a p d -> p a d")
                                 ).then_inc(sem(f"kidx{b % 2}"), 16)
            def w_out1(h, p):
                w = inp["o_w_out"][0, :, 512 * h:512 * h + 512]
                dst = piece1(p)
                for g in range(2):
                    sp.dma_start(dst[64 * g:64 * g + 64, 0:4, :],
                                 w[256 * g:256 * g + 256, :].rearrange("(r d) n -> d r n", d=HD)).then_inc(sem(f"out{h}"), 16)
                sp.dma_start(dst[:, 4:8, :], w[512:, :].rearrange("(k p) n -> p k n", p=P)).then_inc(sem(f"out{h}"), 16)

            sp.wait_ge(sem("tok_mm"), 3)
            w_out1(0, 5)
            moe_w = ("o_we_gate", "o_we_up", "o_we_down")
            sp.wait_ge(sem("din_mm"), CA)
            ff_step(moe_w, 0, 0)
            ff_step(moe_w, 0, 1)
            sp.wait_ge(*reached("isum_mm"))
            sp.wait_ge(sem("pt_prompt_mm"), 8)
            for b in range(NB):
                if b >= 2:
                    sp.wait_ge(sem("kT_mm"), 4 * (b - 1))
                    sp.wait_ge(sem("pv_mm"), b - 1)
                with sp.Fori(0, NPG) as j:
                    page = sp.value_load(pages.bitcast(I32)[0:1, ds(j + b * NPG, 1)], min_val=0, max_val=N_POOL - 1)
                    sp.dma_start(k_pages[b % 2][:, ds(j, 1), :],
                                 inp["cache_k"][0, ds(page, 1)].rearrange("a p g d -> p a (g d)")
                                 ).then_inc(sem(f"kidx{b % 2}"), 16)
                    sp.dma_start(v_pages[b % 2][:, ds(j, 1), :],
                                 inp["cache_v"][0, ds(page, 1)].rearrange("a p g d -> p a (g d)")
                                 ).then_inc(sem(f"v_in{b % 2}"), 16)
            sp.wait_ge(sem("pv_mm"), NB)
            w_out1(1, 4)
            sp.wait_ge(sem("out1_mm"), 6)
            ff_step(moe_w, 0, 2)
            ff_step(moe_w, 0, 3)
            with sp.Fori(0, NE - 1) as e:
                for j in range(4, NSTEP):
                    sp.wait_ge(sem("ff_used"), e * NSTEP + NSTEP + j - 3)
                    ff_step(moe_w, e, j)
                for j, last in zip(range(4), (9, 10, 11, 8)):
                    sp.wait_ge(sem("ff_used"), e * NSTEP + NSTEP + last)
                    if last == NSTEP:
                        sp.wait_ge(sem("moe_down_mm"), e + 1)
                    ff_step(moe_w, e + 1, j)
            for j in range(4, NSTEP):
                sp.wait_ge(sem("ff_used"), NE * NSTEP + j - 3)
                ff_step(moe_w, NE - 1, j)

            def overflow(w):
                e = sp.value_load(over_i[0:1, ds(w, 1)], min_val=0, max_val=NE - 1)
                sp.wait_ge(sem("moe_down_mm"), w + NE)
                for j in range(NSTEP):
                    if j >= NSLOT:
                        sp.wait_ge(sem("ff_used"), w * NSTEP + NE * NSTEP + NSTEP + j - 3)
                    ff_step(moe_w, e, j)

            while_overflow(sp, overflow)

        @block.gpsimd
        def _(pool):
            def load(dst, src, signal):
                pool.dma_start(dst, src).then_inc(sem(signal), 16)

            load(const, inp["constants"], "const_in")
            pr = param_rows
            load(pr[0:31, 0:512], inp["e_conv_a_w"][0], "params_in")
            load(pr[31:32, 0:512], inp["e_conv_a_b"], "params_in")
            load(pr[32:33, 0:512], inp["e_ln_a_g"], "params_in")
            load(pr[33:34, 0:512], inp["e_ln_a_b"], "params_in")
            load(pr[34:37, 0:512], inp["o_conv_d_w"][0], "params_in")
            load(pr[0:4, 512:2048], inp["e_conv_b_w"][0], "params_in")
            load(pr[4:5, 512:2048], inp["e_conv_b_b"], "params_in")
            for i, n in enumerate(("e_norm_mix", "e_norm_ffn", "e_ssm_norm", "o_norm_mix", "o_norm_ffn")):
                load(pr[i:i + 1, 2048:3072], inp[n], "params_in")
            sa = inp["state_conv_a"][0].rearrange("(h b) t c -> h (b t) c", h=2)
            for h in range(2):
                load(state_a[0:120, h, :], sa[h], "states_in")
            load(state_b[0:24, :], inp["state_conv_b"][0].rearrange("b t c -> (b t) c"), "states_in")
            for n in rows:
                load(rows[n], inp[n][0].partition_broadcast(P), "rows_in")
            load(w_dt, inp["e_w_in"][0, :, E_IN - NH:E_IN].rearrange("(k p) n -> p k n", p=P), "rows_in")
            load(w_router, inp["o_w_router"][0].rearrange("(k p) n -> p k n", p=P), "rows_in")
            load(out["s_conv_a"][0, :, 0:WA - 1 - NT, :], inp["state_conv_a"][0, :, NT:WA - 1, :], "stored")

            def rsqrt(dst, src, n, count):
                pool.wait_ge(sem("ms_ready"), count)
                pool.tensor_tensor(dst, src, K["half"][:, 0:1].to_broadcast([P, n]) if n > 3 else K["half"][:, 0:n],
                                   ALU.pow).then_inc(sem("rstd_ready"), 1)

            pool.wait_ge(sem("const_in"), 16)
            rsqrt(rstd, ms, 3, 1)
            rsqrt(small[2], small[1], T, 2)
            pool.wait_ge(sem("tails_ready"), 8)
            for b in range(NB):
                load(out["s_conv_a"][0, b, WA - 1 - NT:WA - 1, :], tail_us[b * NT:b * NT + NT, :], "tails_stored")
            load(out["p_conv_a"][0, 0], tail_up[0:30, :], "tails_stored")
            load(out["p_conv_b"][0, 0], tail_xp[0:3, :], "tails_stored")
            load(out["s_conv_b"][0].rearrange("b t c -> (b t) c"), tail_xs[0:24, :], "tails_stored")
            ssm_in = inp["state_ssm"][0].rearrange("b (c h) p n -> b (h p) c n", h=2)
            ssm_out = out["s_ssm"][0].rearrange("b (c h) p n -> b (h p) c n", h=2)
            pool.wait_ge(sem("conv_b_ready"), XC)
            for b in range(2):
                load(h_old[b], ssm_in[b], f"h_old{b}")
            for i in range(3):
                rsqrt(grs, gms, 2, 3 + i)
                if i == 1:
                    pool.wait_ge(sem("p_ssm_ready"), 2)
                    load(out["p_ssm"][0, 0].rearrange("(c h) p n -> (h p) c n", h=2), h_new[0], "p_ssm_stored")
                    for b in range(NB):
                        pool.wait_ge(sem("h_new_ready"), KD * (b + 1))
                        load(ssm_out[b], h_new[b % 2], f"h_stored{b % 2}")
                        if b + 2 < NB:
                            pool.wait_ge(sem("h_oldT_mm"), 2 * b + 2)
                            load(h_old[b % 2], ssm_in[b + 2], f"h_old{b % 2}")
            rsqrt(rstd, ms, 3, RSTD[1])
            pool.wait_ge(sem("ff_used"), NSTEP)
            load(state_d[0:16, :], inp["state_conv_d"][0].rearrange("b t c -> (b t) c"), "state_d_in")
            rsqrt(rstd, ms, 3, 7)
            rsqrt(ki_rs, ki_ms, 3, 8)
            rsqrt(qk_rs, qk_ms, 30, 9)
            pool.wait_ge(sem("rot_ready"), 2)
            for i, t0, n in TILES:
                for a, b, name in ((512, 640, "k"), (640, 768, "v"), (1024, 1088, "kidx")):
                    dst = (out["p_" + name][0, 0, t0:t0 + n] if i < 2 else
                           out["s_" + name][0].rearrange("b t ... -> (b t) ...") if name == "kidx" else
                           out["s_" + name][0].rearrange("b t g d -> (b t) g d"))
                    if name != "kidx":
                        dst = dst.rearrange("t g d -> t (g d)")
                    load(dst, tok[0:n, i, a:b], "kv_stored")
            pool.wait_ge(*reached("conv_d_ready"))
            pool.wait_ge(sem("tails1_mm"), 2)
            for b in range(NB):
                load(v_new[0:NT, b, :], v_tok[b * NT:b * NT + NT, 2, :], "v_new_in")
            pool.wait_ge(sem("tails1_ready"), 2)
            load(out["p_conv_d"][0, 0], tail_dp[0:2, :], "tails1_stored")
            load(out["s_conv_d"][0].rearrange("b t c -> (b t) c"), tail_ds[0:16, :], "tails1_stored")
            rsqrt(rstd, ms, 3, 10)
            pool.wait_ge(sem("y_out_ready"), 6)
            while_overflow(pool, lambda w: pool.wait_ge(sem("y_out_ready"), 6 * w + 12))
            load(out["y_prompt"][0].rearrange("(a p) d -> p a d", p=P), x[:, 0:2, :], "y_stored")
            load(out["y_sample"].rearrange("b t d -> (b t) d"), x[0:64, 2, :], "y_stored")
            pool.wait_ge(sem("y_stored"), 32)
            pool.wait_ge(sem("h_stored0"), 64)
            pool.wait_ge(sem("h_stored1"), 64)
            pool.wait_ge(sem("stored"), 16)
            pool.wait_ge(sem("kv_stored"), 16 * 9)
            pool.wait_ge(sem("tails1_stored"), 32)

        @block.scalar
        def _(act):
            own = Own(act, sem("act_step"))

            def norm(k, xn=xn):
                for i, t0, n in TILES:
                    act.activation(xn[0:n, i, :], x[0:n, i, :], ACT.Square,
                                   accum_out=ss[0:n, i:i + 1]).then_inc(sem("ss_ready"), 1)

            def copy(dst, src, signal):
                act.activation(dst, src, ACT.Copy).then_inc(sem(signal), 1)

            act.wait_ge(sem("x_in"), 48)
            act.wait_ge(sem("cleared"), 2)
            norm(0)
            act.wait_ge(sem("rows_in"), 16 * 10)
            own.link(act.activation(neg_a, rows["e_a_log"], ACT.Exp))
            own.link(act.activation(neg_a, neg_a, ACT.Copy, scale=-1.0))
            act.wait_ge(*reached("paramsT_mm"))
            copy(vecA.rearrange("p a b -> p (a b)"), bank(6)[:, 0:148], "params_ready")
            copy(vecB.rearrange("p a b -> p (a b)"), bank(6)[:, 148:208], "params_ready")
            copy(vecD.rearrange("p a b -> p (a b)"), bank(6)[:, 208:248], "params_ready")
            act.wait_ge(sem("stateT_mm"), 1)
            copy(xbc_s[:, :, :, 0:3], bank(7)[:, 0:288].rearrange("p (c b t) -> p c b t", c=XC, b=NB), "halo_ready")
            for h in range(2):
                act.wait_ge(sem("stateT_mm"), 2 + h)
                for c in range(CA):
                    copy(u_s[:, c, 4 * h:4 * h + 4, 0:30],
                         bank(6 + h)[:, 120 * c:120 * c + 120].rearrange("p (b t) -> p b t", b=4), "halo_ready")
            for c in range(CA):
                act.wait_ge(sem("gate_mm"), c + 1)
                act.activation(ua[:, c, :], bank(4 + c)[:, 0:T], ACT.Sigmoid).then_inc(sem("sig_ready"), 1)
            for c in range(XC):
                act.wait_ge(sem("xbc_mm"), c + 1)
                act.activation(xbc_p[:, c, 3:], bank(c % 8)[:, 0:SEQ], ACT.Copy)
                copy(xbc_s[:, c, :, 3:], bank(c % 8)[:, SEQ:T].rearrange("p (b t) -> p b t", b=NB), "xbc_ready")
            act.wait_ge(*reached("dt_mm"))
            for i, t0, n in TILES:
                copy(raw_dt[0:n, i, :], bank(4)[0:n, 16 * i:16 * i + 16], "dt_raw_ready")
            act.wait_ge(sem("u_ready"), CA)
            act.wait_ge(sem("xbc_ready"), XC)
            copy(u_last.rearrange("p c (b t) -> p c b t", b=NB), u_s[:, :, :, 30:38], "last_ready")
            copy(xbc_last.rearrange("p c (b t) -> p c b t", b=NB), xbc_s[:, :, :, 8:11], "last_ready")
            for g in range(6):
                i, h = g // 2, g % 2
                n = TILES[i][2]
                act.wait_ge(sem("z_mm"), g + 1)
                act.activation(z[0:n, i, 512 * h:512 * h + 512], bank((13 + g) % 8)[0:n, :],
                               ACT.Silu).then_inc(sem("z_ready"), 1)
            act.wait_ge(*reached("tails_mm"))
            copy(tail_us[0:64, :], bank(3)[0:64, :], "tails_ready")
            copy(tail_up[0:30, :], bank(4)[0:30, :], "tails_ready")
            for j in range(3):
                copy(tail_xp[0:3, 512 * j:512 * j + 512], bank(5 + j)[0:3, :], "tails_ready")
                copy(tail_xs[0:24, 512 * j:512 * j + 512], bank(j)[0:24, :], "tails_ready")
            act.wait_ge(*reached("dt_abs_ready"))
            own.link(act.activation(dt_log, dt_abs, ACT.Exp, scale=-1.0))
            act.activation(dt_log, dt_log, ACT.Ln, bias=1.0).then_inc(*reaches("dt_log_ready"))
            for c in range(XC):
                act.wait_ge(sem("conv_b_ready"), c + 1)
                act.activation(xbcT[:, c, :], xbcT[:, c, :], ACT.Silu).then_inc(sem("xbcT_ready"), 1)
            act.wait_ge(*reached("ua_centred"))
            act.activation(squares, ua, ACT.Square).then_inc(*reaches("squares_ready"))
            act.wait_ge(*reached("ua_normed"))
            for c in range(CA):
                act.activation(mixT[:, c, :], ua[:, c, :], ACT.Silu, scale=vecA[:, c, 32:33],
                               bias=vecA[:, c, 33:34]).then_inc(sem("ya_ready"), 1)
            act.wait_ge(sem("tails_stored"), 16 * 11)
            for g in range(9):
                i, k = g // 3, g % 3
                n = TILES[i][2]
                act.wait_ge(sem("xT_mm"), g + 1)
                src = bank([5, 6, 7, 0, 1, 2][g % 6])
                if k < 2:
                    copy(x_tok[0:n, i, 512 * k:512 * k + 512], src[0:n, :], "x_tok_ready")
                else:
                    copy(b_tok[0:n, i, :], src[0:n, 0:256], "x_tok_ready")
            for i, t0, n in TILES:
                act.wait_ge(sem("cumT_ready"), i + 1)
                own.mark(act.activation(e_cum[0:n], bank(0)[0:n, 0:16], ACT.Exp))
                own.mark(act.activation(w_end[0:n], w_arg[0:n], ACT.Exp))
                act.activation(e_last[0:n], bank(0)[0:n, 16:32], ACT.Exp).then_inc(sem("scan_exps_ready"), 1)
                for q in range(4):
                    act.wait_ge(sem("arow_mm"), 4 * i + q + 1)
                    for h in range(4 * q, 4 * q + 4):
                        ins = act.activation(decay[0:n, h, 0:n], bank(2 + q)[0:n, (h % 4) * n:(h % 4) * n + n],
                                             ACT.Exp, bias=negcum[0:n, h:h + 1])
                    ins.then_inc(sem("decay_ready"), 1)
                if i == 1:
                    for g in range(2):
                        act.wait_ge(sem("p_ssmT_mm"), g + 1)
                        copy(h_new[0][:, 4 * g:4 * g + 4, :], bank(4 + g, 4, P), "p_ssm_ready")
                if i == 2:
                    act.wait_ge(*reached("dA_sum_mm"))
                    act.activation(decs, bank(0)[:, 0:64].rearrange("p (c b) -> p c b", c=KD),
                                   ACT.Exp).then_inc(*reaches("decs_ready"))
                    for b in range(NB):
                        if b == 0:
                            act.wait_ge(sem("p_ssmT_mm"), 2)
                        for g in range(2):
                            act.wait_ge(sem("h_oldT_mm"), 2 * b + g + 1)
                            if b:
                                act.wait_ge(sem("inter_acc"), 2 * b - 1 + g)
                            copy(h_oldT[:, 512 * g:512 * g + 512], bank(4 + g), "h_oldT_ready")
                act.wait_ge(sem("y_ready"), i + 1)
                for g in range(2):
                    act.activation(xdt[0:n, 8 * g:8 * g + 8, :], y[0:n, 8 * g:8 * g + 8, :], ACT.Square,
                                   accum_out=gs[0:n, g:g + 1]).then_inc(sem("gs_ready"), 1)
            act.wait_ge(sem("x_ready"), 6)
            norm(1)

            def silu(dst, src, gate_mm, done, value):
                act.wait_ge(sem(gate_mm), value)
                act.activation(dst, src, ACT.Silu).then_inc(sem(done), 1)

            for m in range(2 * NSTEP):
                if m >= 2:
                    act.wait_ge(sem("ff_ready"), m - 1)
                silu(silu_t[:, m % 2, :], bank(6)[:, 0:T], "ff_gate_mm", "ff_silu", m + 1)
            act.wait_ge(sem("x_ready"), 12)
            norm(2)
            act.wait_ge(*reached("tok_cleared"))
            for g in range(7):
                act.wait_ge(sem("tok_mm"), min(g + 1, 4) if g < 4 else g + 1)
                if g < 3:
                    n = TILES[g][2]
                    copy(tok[0:n, g, 512:1024], bank(g)[0:n, :], "tok_ready")
                elif g == 3:
                    copy(tok[:, 0:2, 1024:1092], bank(3, 2, 68), "tok_ready")
                    copy(tok[0:NS, 2, 1024:1092], bank(3)[0:NS, 136:204], "tok_ready")
                else:
                    n = TILES[g - 4][2]
                    copy(tok[0:n, g - 4, 0:512], bank(g)[0:n, :], "tok_ready")
            act.wait_ge(sem("tok_ready"), 8)
            act.activation(squares1, tok[:, :, 0:640], ACT.Square).then_inc(*reaches("qk_squared"))
            act.wait_ge(*reached("ki_centred"))
            act.activation(rope_t[0].rearrange("p a b c -> p a (b c)")[:, :, 0:64], tok[:, :, 1024:1088],
                           ACT.Square).then_inc(*reaches("ki_squared"))
            copy(v_tok, tok[:, :, 640:768], "v_ready")
            act.activation(w_idx, tok[:, :, 1088:1092], ACT.Copy,
                           scale=4 ** -0.5 * HD ** -0.5).then_inc(sem("v_ready"), 1)
            for g in range(9):
                i, k = g // 3, g % 3
                t0, n = TILES[i][1:]
                act.wait_ge(sem("rotT_mm"), g + 1)
                dst = (qT, qiT, kkT)[k]
                m = 4 if k < 2 else 2
                copy(dst[:, :, t0:t0 + n], bank(4 + k, m, n), "rotT_ready")
            act.wait_ge(*reached("stateT1_mm"))
            copy(cd_s[:, :, :, 0:2], bank(7)[:, 0:64].rearrange("p (c b t) -> p c b t", c=CA, b=NB), "halo1_ready")
            act.wait_ge(*reached("din_free"))
            for c in range(CA):
                act.wait_ge(sem("din_mm"), c + 1)
                copy(din_t[:, c, :], bank(c)[:, 0:T], "din_ready")
            act.wait_ge(sem("tails1_mm"), 2)
            copy(tail_dp[0:2, :], bank(7)[0:2, :], "tails1_ready")
            copy(tail_ds[0:16, :], bank(4)[0:16, :], "tails1_ready")
            for i in range(2):
                act.wait_ge(sem("idx_p_mm"), i + 1)
                act.wait_ge(sem("sc_p_ready"), i) if i else act.wait_ge(sem("tails1_stored"), 32)
                act.activation(relu_p.rearrange("p a b -> p (a b)"), psum[:, 1024 * i:1024 * i + 1024],
                               ACT.Relu).then_inc(sem("relu_p_ready"), 1)
            act.wait_ge(sem("kv_stored"), 16 * 9)
            act.wait_ge(*reached("sc_p_taken"))
            for b in range(NB):
                for g in range(2):
                    act.wait_ge(sem("kidxT_mm"), 2 * b + g + 1)
                    if b >= 2:
                        act.wait_ge(sem("dots_mm"), b - 1)
                    copy(kidxT[b % 2][:, 4 * g:4 * g + 4, :], bank(5 + g, 4, P), "kidxT_ready")
                if b % 4 == 3:
                    act.wait_ge(sem("dots_mm"), b + 1)
                    for odd in range(2):
                        act.activation(relu_s[b // 4][:, 0:PAST].rearrange("p (a o k) -> p a o k", o=2, k=P)[:, :, odd, :],
                                       psum[:, 1024 * odd:1024 * odd + 1024].rearrange("p (a k) -> p a k", k=P), ACT.Relu)
                    act.activation(relu_s[b // 4][:, PAST:], bank(4)[:, 0:NT], ACT.Relu).then_inc(sem("relu_s_ready"), 1)
            act.wait_ge(*reached("wsT_mm"))
            act.activation(ws, bank(7, 2, NS), ACT.Copy).then_inc(*reaches("ws_ready"))
            for i in range(2):
                act.wait_ge(sem("nmx_p_ready"), i + 1)
                for h in range(8):
                    ins = act.activation(probs_p[:, h, :], probs_p[:, h, :], ACT.Exp, bias=nmx[:, h:h + 1],
                                         scale=HD ** -0.5, accum_out=sums[:, h:h + 1])
                ins.then_inc(sem("exp_p_ready"), 1)
                for g in range(4):
                    act.wait_ge(sem("pt_prompt_mm"), 4 * i + g + 1)
                    copy(probs_pT[:, 2 * g:2 * g + 2], bank(4 + g % 2, 2, 2, P), "pt_prompt_ready")
                act.wait_ge(sem("pv_p_mm"), i + 1)
                copy(mix1T[:, 0:4, P * i:P * i + P], bank(7, 4, P), "att_ready")
            for b in range(NB):
                for g in range(4):
                    act.wait_ge(sem("kT_mm"), 4 * b + g + 1)
                    if b:
                        act.wait_ge(sem("s_mm"), b)
                    copy(k_T[:, 512 * g:512 * g + 512], bank(5 + g % 2), "kT_ready")
                if b % 2:
                    q = b // 2
                    act.wait_ge(sem("nmx_ready"), q + 1)
                    if q:
                        act.wait_ge(sem("pt_mm"), 5 * q)
                    act.activation(probs, psum[:, 0:KEYS], ACT.Exp, bias=nmx[:, 0:1], scale=HD ** -0.5,
                                   accum_out=sums[:, 0:1]).then_inc(sem("exp_ready"), 1)
                    for g in range(5):
                        act.wait_ge(sem("pt_mm"), 5 * q + g + 1)
                        if q:
                            act.wait_ge(sem("pv_mm"), 2 * q)
                        if g < 4:
                            copy(probsT[:, 4 * g:4 * g + 4, :], bank(5 + g % 2, 4, P), "pt_ready")
                        else:
                            copy(probsT[0:NT, 16, :], bank(5)[0:NT, 0:P], "pt_ready")
            act.wait_ge(sem("x_ready"), 18)
            norm(3, xn3)
            act.wait_ge(*reached("gap_ready"))
            act.activation(e_gap, gap, ACT.Exp).then_inc(*reaches("e_gap_ready"))
            for e in range(NE):
                act.wait_ge(sem("selT_mm"), e + 1)
                copy(selT[:, e, :], bank(4 + e % 2)[:, 0:T], "selT_ready")

            def expert(n, y_out):
                for m in range(2 * NSTEP):
                    act.wait_ge(sem("ff_ready"), n * 2 * NSTEP + 2 * NSTEP + m - 1)
                    silu(moe_silu[:, m % 2, :], bank(2 + 2 * (m % 2))[:, 0:CAP], "ff_gate_mm", "ff_silu",
                         n * 2 * NSTEP + 2 * NSTEP + m + 1)
                act.wait_ge(sem("moe_down_mm"), n + 1)
                act.activation(y_out, bank(1).unsqueeze(1), ACT.Copy).then_inc(sem("moe_y1"), 1)

            with act.Fori(0, NE) as e:
                expert(e, moe_y[:, ds(e, 1), 512:1024])

            def overflow(w):
                n = w + NE
                act.wait_ge(sem("selT_mm"), n + 1)
                copy(selT[:, 0, :], bank(4)[:, 0:T], "selT_ready")
                expert(n, moe_y[:, 1:2, 512:1024])

            while_overflow(act, overflow)

        @block.tensor
        def _(pe):
            def mm(dst, w, m, start, stop):
                return pe.matmul(dst, w, m, start=start, stop=stop)

            def norm(k, xn=xn):
                for i, t0, n in TILES:
                    pe.wait_ge(sem("xn_ready"), 3 * k + i + 1)
                    for g in range(2):
                        for c in range(4):
                            ins = pe.transpose(bank(2 * i + g, 4, n)[:, c, :],
                                               xn[0:n, i, (4 * g + c) * P:(4 * g + c + 1) * P], ident[0:n, 0:n])
                        ins.then_inc(sem("xnT_mm"), 1)

            pe.wait_ge(sem("const_in"), 16)
            pe.wait_ge(sem("params_in"), 16 * 12)
            for c in range(CA):
                pe.transpose(bank(6)[:, 37 * c:37 * c + 37], param_rows[0:37, c * P:(c + 1) * P], ident[0:37, 0:37])
            for c in range(XC):
                pe.transpose(bank(6)[:, 148 + 5 * c:153 + 5 * c], param_rows[0:5, 512 + c * P:512 + (c + 1) * P],
                             ident[0:5, 0:5])
            for c in range(KD):
                ins = pe.transpose(bank(6)[:, 208 + 5 * c:213 + 5 * c],
                                   param_rows[0:5, 2048 + c * P:2048 + (c + 1) * P], ident[0:5, 0:5])
            ins.then_inc(*reaches("paramsT_mm"))
            pe.wait_ge(sem("states_in"), 48)
            for c in range(XC):
                ins = pe.transpose(bank(7)[:, 24 * c:24 * c + 24], state_b[0:24, c * P:(c + 1) * P], ident[0:24, 0:24])
            ins.then_inc(sem("stateT_mm"), 1)
            pe.wait_ge(sem("params_ready"), 3)
            pe.wait_ge(sem("halo_ready"), 1)
            for h in range(2):
                for c in range(CA):
                    ins = pe.transpose(bank(6 + h)[:, 120 * c:120 * c + 120], state_a[0:120, h, c * P:(c + 1) * P],
                                       ident[0:120, 0:120])
                ins.then_inc(sem("stateT_mm"), 1)
            norm(0)
            pe.wait_ge(sem("hT_ready"), 6)
            pe.wait_ge(sem("halo_ready"), 9)

            def arrived(n):
                pe.wait_ge(sem(f"piece{n % 4}"), 16 * (n // 4 + 1))

            for n, signal in ((0, "val_mm"), (1, "gate_mm")):
                arrived(n)
                for c in range(CA):
                    for k in range(KD):
                        ins = mm(bank(4 * n + c)[:, 0:T], piece(n)[:, k, c * P:(c + 1) * P], hT[:, k, :], k == 0, k == KD - 1)
                    ins.then_inc(sem(signal), 1)
            for c in range(XC):
                n = 2 + c // 4
                if c % 4 == 0:
                    arrived(n)
                if c < 4:
                    pe.wait_ge(sem("u_ready"), c + 1)
                elif c < 8:
                    pe.wait_ge(sem("sig_ready"), c - 3)
                else:
                    pe.wait_ge(sem("xbc_ready"), c - 7)
                for k in range(KD):
                    ins = mm(bank(c % 8)[:, 0:T], piece(n)[:, k, (c % 4) * P:(c % 4 + 1) * P], hT[:, k, :], k == 0, k == KD - 1)
                ins.then_inc(sem("xbc_mm"), 1)
            pe.wait_ge(sem("xbc_ready"), 5)
            pe.wait_ge(sem("rows_in"), 16 * 10)
            for i, t0, n in TILES:
                for k in range(KD):
                    ins = mm(bank(4)[0:n, 16 * i:16 * i + 16], hT[:, k, t0:t0 + n], w_dt[:, k, :], k == 0, k == KD - 1)
            ins.then_inc(*reaches("dt_mm"))
            arrived(5)
            arrived(6)
            for g in range(6):
                i, h = g // 2, g % 2
                t0, n = TILES[i][1:]
                pe.wait_ge(sem("xbc_ready"), min(XC, 6 + g))
                for k in range(KD):
                    ins = mm(bank((13 + g) % 8)[0:n, :], hT[:, k, t0:t0 + n], piece(5 + h)[:, k, :], k == 0, k == KD - 1)
                ins.then_inc(sem("z_mm"), 1)
            pe.wait_ge(sem("z_ready"), 6)
            pe.wait_ge(sem("xbc_ready"), XC)
            pe.wait_ge(sem("dt_raw_ready"), 3)
            pe.wait_ge(sem("last_ready"), 2)
            for c in range(CA):
                cc = slice(c * P, (c + 1) * P)
                pe.transpose(bank(3)[0:64, cc], u_last[:, c, :], ident)
                pe.transpose(bank(4)[0:30, cc], u_p[:, c, 256:286], ident)
            for c in range(XC):
                cc = slice((c % 4) * P, (c % 4 + 1) * P)
                pe.transpose(bank(5 + c // 4)[0:3, cc], xbc_p[:, c, 256:259], ident)
                ins = pe.transpose(bank(c // 4)[0:24, cc], xbc_last[:, c, :], ident)
            ins.then_inc(*reaches("tails_mm"))
            pe.wait_ge(sem("ua_ready"), CA)
            pe.wait_ge(sem("tails_ready"), 8)
            for c in range(CA):
                ins = mm(bank(3)[:, 0:T], ones, ua[:, c, :], c == 0, c == CA - 1)
            ins.then_inc(*reaches("mean_mm"))
            pe.wait_ge(*reached("squares_ready"))
            for c in range(CA):
                ins = mm(bank(4)[:, 0:T], ones, squares[:, c, :], c == 0, c == CA - 1)
            ins.then_inc(*reaches("var_mm"))
            pe.wait_ge(sem("xbcT_ready"), XC)
            for g in range(9):
                i, k = g // 3, g % 3
                t0, n = TILES[i][1:]
                if g >= 6:
                    pe.wait_ge(sem("x_tok_ready"), g - 5)
                for c in range(4 if k < 2 else 2):
                    ins = pe.transpose(bank([5, 6, 7, 0, 1, 2][g % 6])[0:n, c * P:(c + 1) * P],
                                       xbcT[:, 4 * k + c, t0:t0 + n], ident)
                ins.then_inc(sem("xT_mm"), 1)
            pe.wait_ge(sem("x_tok_ready"), 9)
            pe.wait_ge(*reached("dA_ready"))
            pe.wait_ge(*reached("ua_normed"))
            for i, t0, n in TILES:
                tri = K["tri_p"] if i < 2 else K["tri_s"][0:64, :]
                last = ones if i < 2 else K["last_s"][0:64, :]
                mask = K["mask_p"] if i < 2 else K["mask_s"][0:64, :]
                if i:
                    pe.wait_ge(sem("mixT_ready"), 2 * i)
                mm(bank(0)[0:n, 0:16], tri, dA[0:n, i, :], True, True)
                mm(bank(0)[0:n, 16:32], last, dA[0:n, i, :], True, True)
                mm(bank(0)[0:16, 32:32 + n], dA[0:n, i, :], tri, True, True).then_inc(sem("cum_mm"), 1)
                for g in range(NG):
                    ins = mm(bank(1, 2, n)[0:n, g, :], xbcT[:, 8 + g, t0:t0 + n], xbcT[:, 10 + g, t0:t0 + n], True, True)
                ins.then_inc(sem("cb_mm"), 1)
                pe.wait_ge(sem("cumT_ready"), i + 1)
                if i == 1:
                    pe.wait_ge(sem("p_state_ready"), 2)
                if i == 2:
                    pe.wait_ge(sem("p_ssm_ready"), 2)
                for q in range(4):
                    v = bank(2 + q, 4, n)[0:n]
                    for h in range(4):
                        pe.matmul(v[:, h, :], head_row[0:16, 4 * q + h, 0:n], cumT[0:16, 0:n], start=(h == 0),
                                  stop=False, skip_group_check=True)
                    ins = pe.matmul(v, ident[0:n, 0:n], mask.unsqueeze(1).to_broadcast([n, 4, n]), start=False,
                                    stop=True, skip_group_check=True)
                    ins.then_inc(sem("arow_mm"), 1)
                pe.wait_ge(sem("wts_ready"), 2 * i + 2)
                pe.wait_ge(sem("xdt_ready"), i + 1)
                if i:
                    pe.wait_ge(sem("y_ready"), i)
                for h in range(NH):
                    ins = mm(bank(6 + h // 8)[0:n, (h % 8) * HP:(h % 8 + 1) * HP], decay[0:n, h, 0:n], xdt[0:n, h, :], True, True)
                ins.then_inc(sem("y_mm"), 1)
                pe.wait_ge(sem("decay_ready"), 4 * i + 4)
                if i == 1:
                    for g in range(NG):
                        ins = mm(bank(2 + g), xbcT[:, 10 + g, t0:t0 + n], p_state[:, 512 * g:512 * g + 512], True, True)
                    ins.then_inc(*reaches("inter_mm"))
                if i < 2:
                    pe.wait_ge(sem("xw_ready"), i + 1)
                    for g in range(NG):
                        ins = mm(bank(4 + g), b_tok[0:n, i, g * NST:(g + 1) * NST],
                                 xw[0:n, 8 * g:8 * g + 8, :], True, True)
                    ins.then_inc(sem("state_mm"), 1)
                if i == 1:
                    pe.wait_ge(sem("p_state_ready"), 4)
                    for g in range(2):
                        for c in range(4):
                            ins = pe.transpose(bank(4 + g, 4, P)[:, c, :], p_state[:, (4 * g + c) * P:(4 * g + c + 1) * P], ident)
                        ins.then_inc(sem("p_ssmT_mm"), 1)
                if i == 2:
                    pe.wait_ge(*reached("dA_rows_ready"))
                    pe.wait_ge(sem("scan_exps_ready"), 3)
                    for c in range(KD):
                        ins = mm(bank(0)[:, 8 * c:8 * c + 8], dA_rows[0:n, c * P:(c + 1) * P], K["batch"][0:n, :], True, True)
                    ins.then_inc(*reaches("dA_sum_mm"))
                    pe.wait_ge(*reached("decs_ready"))
                    for b in range(NB):
                        pe.wait_ge(sem(f"h_old{b % 2}"), 16 * (b // 2 + 1))
                        for g in range(2):
                            if b:
                                pe.wait_ge(sem("h_oldT_ready"), 2 * b - 1 + g)
                            else:
                                pe.wait_ge(sem("p_ssm_ready"), 2)
                            for c in range(4):
                                ins = pe.transpose(bank(4 + g, 4, P)[:, c, :], h_old[b % 2][:, 4 * g + c, :], ident)
                            ins.then_inc(sem("h_oldT_mm"), 1)
                        pe.wait_ge(*reached("c_pad_ready"))
                        for g in range(NG):
                            pe.wait_ge(sem("h_oldT_ready"), 2 * b + g + 1)
                            pe.matmul(bank(2 + g)[0:n, :], c_pad[:, g, b, :], h_oldT[:, 512 * g:512 * g + 512],
                                      start=(b == 0), stop=(b == NB - 1), skip_group_check=True
                                      ).then_inc(sem("inter_acc"), 1)
                        pe.wait_ge(sem("b_one_ready"), b + 1)
                        pe.wait_ge(sem("xw_ready"), 3)
                        if b:
                            pe.wait_ge(sem("h_new_ready"), KD * b)
                        for c in range(KD):
                            ins = mm(bank(c // 4, 4, P)[:, c % 4, :], xw[0:n, 2 * c:2 * c + 2, :],
                                     b_one[0:n, b % 2, (c // 4) * NST:(c // 4 + 1) * NST], True, True)
                        ins.then_inc(sem("h_add_mm"), 1)
                pe.wait_ge(sem("yn_ready"), i + 1)
                pe.wait_ge(sem("wts_ready"), 2 * i + 2)
                if i == 2:
                    pe.wait_ge(sem("h_new_ready"), KD * NB)
                for g in range(2):
                    for c in range(4):
                        ins = pe.transpose(bank(g, 4, n)[:, c, :], y[0:n, 8 * g + 2 * c:8 * g + 2 * c + 2, :], ident[0:n, 0:n])
                    ins.then_inc(sem("yT_mm"), 1)
            pe.wait_ge(sem("mixT_ready"), 6)
            pe.wait_ge(sem("ya_ready"), CA)
            for h in range(2):
                for q in range(2):
                    n_ = 7 + 2 * h + q
                    arrived(n_)
                    for i, t0, n in TILES:
                        for k in range(8 if q == 0 else 4):
                            ins = mm(bank(3 * h + i)[0:n, :], mixT[:, 8 * q + k, t0:t0 + n], piece(n_)[:, k, :],
                                     q == 0 and k == 0, q == 1 and k == 3)
                        if q or i == 2:
                            ins.then_inc(sem("mix_out_mm"), 1)
            norm(1)
            pe.wait_ge(sem("hT_ready"), 12)
            for m in range(2 * NSTEP + 1):
                if m < 2 * NSTEP:
                    j, q = m // 2, m % 2
                    g, u, dn = slot(j % NSLOT)
                    if q == 0:
                        pe.wait_ge(sem(f"weights{j % NSLOT}"), 48 * (j // NSLOT + 1))
                    for w, b_, signal in ((g, 6, "ff_gate_mm"), (u, 7, "ff_up_mm")):
                        if m:
                            pe.wait_ge(sem("ff_silu" if b_ == 6 else "ff_ready"), m)
                        for k in range(KD):
                            ins = mm(bank(b_)[:, 0:T], w[:, k, q * P:(q + 1) * P], hT[:, k, :], k == 0, k == KD - 1)
                        ins.then_inc(sem(signal), 1)
                if m:
                    c = m - 1
                    dn = slot((c // 2) % NSLOT)[2]
                    pe.wait_ge(sem("ff_ready"), m)
                    for i, t0, n in TILES:
                        for h in range(2):
                            ins = mm(bank(2 * i + h)[0:n, :], ff[:, c % 4, t0:t0 + n], dn[:, c % 2, 512 * h:512 * h + 512],
                                     c == 0, c == 2 * NSTEP - 1)
                    if c % 2:
                        ins.then_inc(sem("ff_used"), 1)
            norm(2)
            pe.wait_ge(sem("hT_ready"), 18)
            pe.wait_ge(sem("state_d_in"), 16)
            for c in range(CA):
                ins = pe.transpose(bank(7)[:, 16 * c:16 * c + 16], state_d[0:16, c * P:(c + 1) * P], ident[0:16, 0:16])
            ins.then_inc(*reaches("stateT1_mm"))
            for (p, c0, nc_), b0, step in zip(pieces1[:3], (0, 3, 4), (1, 0, 1)):
                pe.wait_ge(sem(f"piece{p}"), 16 * (3, 3, 3, 2, 0, 0)[p] + 16)
                for i, t0, n in TILES:
                    dst = bank(b0 + i * step)[0:n, 0:512] if step else bank(3)[0:n, 68 * i:68 * i + 68]
                    for k in range(KD):
                        ins = mm(dst, hT[:, k, t0:t0 + n], piece1(p)[:, k, 0:nc_], k == 0, k == KD - 1)
                    if step or i == 2:
                        ins.then_inc(sem("tok_mm"), 1)
            for (p, c0, nc_), b0, signal in zip(pieces1[3:], (0, 4, 0), ("din_mm", "cg_mm", "bg_mm")):
                pe.wait_ge(sem(f"piece{p}"), 16 * (3, 3, 3, 2, 0, 0)[p] + 16)
                for c in range(CA):
                    if signal == "din_mm":
                        pe.wait_ge(sem("tok_ready"), (1, 2, 3, 5)[c])
                    elif signal == "cg_mm":
                        pe.wait_ge(sem("rotT_ready" if c < 3 else "halo1_ready"), 9 if c < 3 else 1)
                    else:
                        pe.wait_ge(sem("din_ready"), c + 1)
                    for k in range(KD):
                        ins = mm(bank(b0 + c)[:, 0:T], piece1(p)[:, k, c * P:(c + 1) * P], hT[:, k, :], k == 0, k == KD - 1)
                    ins.then_inc(sem(signal), 1)
                if signal == "din_mm":
                    pe.wait_ge(sem("tok_ready"), 8)
                    pe.wait_ge(sem("rot_ready"), 3)
                    for g in range(9):
                        i, k = g // 3, g % 3
                        n = TILES[i][2]
                        if g >= 3:
                            pe.wait_ge(sem("rotT_ready"), g - 2)
                        for r in range(4 if k < 2 else 2):
                            src = (q_tok[0:n, i, r, :] if k == 0 else qi_tok[0:n, i, r, :] if k == 1 else
                                   tok[0:n, i, 512:640] if r == 0 else ki_tok[0:n, i, :])
                            ins = pe.transpose(bank(4 + k)[:, r * n:(r + 1) * n], src, ident[0:n, 0:n])
                        ins.then_inc(sem("rotT_mm"), 1)
            pe.wait_ge(sem("cd_ready"), 2 * CA)
            for c in range(CA):
                ins = pe.transpose(bank(7)[0:2, c * P:(c + 1) * P], cd_p[:, c, SEQ:SEQ + 2], ident)
            ins.then_inc(sem("tails1_mm"), 1)
            pe.wait_ge(*reached("cd_last_ready"))
            for c in range(CA):
                ins = pe.transpose(bank(4)[0:16, c * P:(c + 1) * P], cd_last[:, c, :], ident)
            ins.then_inc(sem("tails1_mm"), 1)
            pe.wait_ge(*reached("conv_d_ready"))
            for i in range(2):
                for h in range(4):
                    ins = mm(bank(2 * i + h // 2)[:, 256 * (h % 2):256 * (h % 2) + 256], qiT[0:64, h, P * i:P * i + P],
                             kkT[0:64, 1, 0:SEQ], True, True)
                ins.then_inc(sem("idx_p_mm"), 1)
            pe.wait_ge(*reached("q_packed"))
            pe.wait_ge(sem("relu_p_ready"), 2)
            pe.wait_ge(sem("tails1_ready"), 2)
            for b in range(NB):
                pe.wait_ge(sem(f"kidx{b % 2}"), 16 * NPG * (b // 2 + 1))
                for g in range(2):
                    if b:
                        pe.wait_ge(sem("kidxT_ready"), 2 * b - 1 + g)
                    for c in range(4):
                        j = 8 * g + 2 * c
                        ins = pe.transpose(bank(5 + g, 4, P)[:, c, :],
                                           kidx[b % 2][:, j:j + 2, :].rearrange("p a b -> p (a b)"), ident)
                    ins.then_inc(sem("kidxT_mm"), 1)
                pe.wait_ge(sem("kidxT_ready"), 2 * b + 2)
                if b == 4:
                    pe.wait_ge(sem("relu_s_ready"), 1)
                r0 = 32 * (b % 4)
                for j in range(NPG):
                    h0 = 64 * (j % 2)
                    mm(bank(2 * (j % 2) + j // 8)[r0:r0 + 32, P * (j // 2 % 4):P * (j // 2 % 4) + P], qi_b[h0:h0 + 64, b, :],
                       kidxT[b % 2][h0:h0 + 64, j // 2, :], True, True)
                mm(bank(4)[r0:r0 + 32, 0:NT], qi_b[0:64, b, :], kkT[0:64, 1, SEQ + NT * b:SEQ + NT * b + NT], True, True
                   ).then_inc(sem("dots_mm"), 1)
            pe.wait_ge(sem("wsT_ready"), 2)
            for g in range(2):
                ins = pe.transpose(bank(7)[:, NS * g:NS * g + NS], rep[0:NS, g, :], ident[0:NS, 0:NS])
            ins.then_inc(*reaches("wsT_mm"))
            pe.wait_ge(*reached("ws_ready"))
            pe.wait_ge(sem("relu_s_ready"), 2)
            for c in range(5):
                w = 512 if c < 4 else NT
                for g in range(2):
                    ins = mm(bank(c)[0:NS, 0:w], ws[:, g, :], relu_s[g][:, 512 * c:512 * c + w], g == 0, g == 1)
            ins.then_inc(*reaches("isum_mm"))
            pe.wait_ge(*reached("work_s_ready"))
            for i in range(2):
                if i:
                    pe.wait_ge(sem("s_p_taken"), 1)
                for h in range(8):
                    g, r = h // 4, h % 4
                    ins = mm(bank(h // 2)[:, 256 * (h % 2):256 * (h % 2) + 256], qT[64 * g:64 * g + 64, r, P * i:P * i + P],
                             kkT[64 * g:64 * g + 64, 0, 0:SEQ], True, True)
                ins.then_inc(sem("s_p_mm"), 1)
                pe.wait_ge(sem("probs_p_ready"), i + 1)
                for q in range(4):
                    if 4 * i + q >= 2:
                        pe.wait_ge(sem("pt_prompt_ready"), 4 * i + q - 1)
                    for h in range(2 * q, 2 * q + 2):
                        for kc in range(2):
                            ins = pe.transpose(bank(4 + q % 2, 2, 2, P)[:, h % 2, kc, :], probs_p[:, h, kc * P:(kc + 1) * P], ident)
                    ins.then_inc(sem("pt_prompt_mm"), 1)
                pe.wait_ge(sem("pt_prompt_ready"), 4 * i + 4)
                if i:
                    pe.wait_ge(sem("att_ready"), 1)
                for h in range(8):
                    g, r = h // 4, h % 4
                    for kc in range(2):
                        ins = mm(bank(7)[64 * g:64 * g + 64, r * P:(r + 1) * P], v_tok[:, kc, 64 * g:64 * g + 64],
                                 probs_pT[:, h, kc, :], kc == 0, kc == 1)
                ins.then_inc(sem("pv_p_mm"), 1)
            pe.wait_ge(*reached("rep_ready"))
            for b in range(NB):
                q = b // 2
                pe.wait_ge(sem(f"kidx{b % 2}"), 16 * NPG * (NB // 2 + b // 2 + 1))
                for g in range(4):
                    n_ = 4 * b + g
                    if n_ >= 2:
                        pe.wait_ge(sem("kT_ready"), n_ - 1)
                    if b % 2 == 0 and b:
                        pe.wait_ge(sem("pt_ready"), 5 * q)
                    for c in range(4):
                        ins = pe.transpose(bank(5 + g % 2, 4, P)[:, c, :], k_pages[b % 2][:, 4 * g + c, :], ident)
                    ins.then_inc(sem("kT_mm"), 1)
                if b % 2 == 0 and b:
                    pe.wait_ge(sem("exp_ready"), q)
                r0 = 64 * (b % 2)
                for c in range(4):
                    pe.wait_ge(sem("kT_ready"), 4 * b + c + 1)
                    pe.matmul(bank(c)[r0:r0 + 64, :], q_blk[:, b, :], k_T[:, 512 * c:512 * c + 512], start=True, stop=False,
                              skip_group_check=True)
                pe.matmul(bank(4)[r0:r0 + 64, 0:NT], q_blk[:, b, :], kkT[:, 0, SEQ + NT * b:SEQ + NT * b + NT], start=True,
                          stop=False, skip_group_check=True).then_inc(sem("s_mm"), 1)
                if b % 2:
                    pe.wait_ge(*reached("bias_s_ready"))
                    for c in range(5):
                        w = 512 if c < 4 else NT
                        ins = pe.matmul(bank(c)[:, 0:w], rep[0:NS, q, :], work_s[0:NS, 512 * c:512 * c + w], start=False,
                                        stop=True, skip_group_check=True)
                    ins.then_inc(sem("masked_mm"), 1)
                    pe.wait_ge(sem("probs_ready"), q + 1)
                    for g in range(5):
                        if g >= 2:
                            pe.wait_ge(sem("pt_ready"), 5 * q + g - 1)
                        for c in range(4 if g < 4 else 1):
                            w = P if g < 4 else NT
                            k0 = (4 * g + c) * P
                            ins = pe.transpose(bank(5 + g % 2)[0:w, c * P:(c + 1) * P], probs[:, k0:k0 + w], ident)
                        ins.then_inc(sem("pt_mm"), 1)
                    pe.wait_ge(sem("pt_ready"), 5 * q + 5)
                    if q:
                        pe.wait_ge(sem("att_s_ready"), 4 * q)
                    else:
                        pe.wait_ge(sem("att_ready"), 2)
                    pe.wait_ge(sem("v_new_in"), 16 * NB)
                    for bb in (b - 1, b):
                        r0 = 64 * (bb % 2)
                        pe.wait_ge(sem(f"v_in{bb % 2}"), 16 * NPG * (bb // 2 + 1))
                        for j in range(NPG):
                            mm(bank(7)[:, r0:r0 + 64], v_pages[bb % 2][:, j, :], probsT[:, j, r0:r0 + 64], j == 0, False)
                        mm(bank(7)[:, r0:r0 + 64], v_new[0:NT, bb, :], probsT[0:NT, 16, r0:r0 + 64], False, True
                           ).then_inc(sem("pv_mm"), 1)
            pe.wait_ge(sem("att_s_ready"), 16)
            for h, p in ((0, 5), (1, 4)):
                pe.wait_ge(sem(f"out{h}"), 48)
                for i, t0, n in TILES:
                    for k in range(KD):
                        ins = mm(bank(3 * h + i)[0:n, :], mix1T[:, k, t0:t0 + n], piece1(p)[:, k, :], k == 0, k == KD - 1)
                    ins.then_inc(sem("out1_mm"), 1)
            norm(3, xn3)
            pe.wait_ge(sem("hT_ready"), 24)
            for i, t0, n in TILES:
                for k in range(KD):
                    ins = mm(bank(6)[0:n, NE * i:NE * i + NE], hT[:, k, t0:t0 + n], w_router[:, k, :], k == 0, k == KD - 1)
            ins.then_inc(*reaches("logits_mm"))
            pe.wait_ge(*reached("routed_ready"))
            for i, t0, n in TILES:
                for j in range(i + 1):
                    nj = TILES[j][2]
                    ins = mm(bank(7)[0:n, NE * i:NE * i + NE], (ones if j < i else K["tri_p"])[0:nj, 0:n],
                             routed[0:nj, j, :], j == 0, j == i)
            for j in range(3):
                nj = TILES[j][2]
                ins = mm(bank(7)[:, 3 * NE:4 * NE], ones[0:nj, :], routed[0:nj, j, :], j == 0, j == 2)
            ins.then_inc(*reaches("rank_mm"))
            def gather(n, e, banks_):
                pe.wait_ge(sem("sel_ready"), 3 * n + 3)
                for g in range(2):
                    for c in range(4):
                        for i, t0, rows_ in TILES:
                            ins = mm(bank(banks_ + g, 4, P)[:, c, :], xn3[0:rows_, i, (4 * g + c) * P:(4 * g + c + 1) * P],
                                     sel[0:rows_, i, e, :], i == 0, i == 2)
                    ins.then_inc(sem("moe_h_mm"), 1)

            def turn_sel(n, e, b_):
                pe.wait_ge(sem("gated_ready"), 3 * n + 3)
                for i, t0, rows_ in TILES:
                    ins = pe.transpose(bank(b_)[:, t0:t0 + rows_], sel[0:rows_, i, e, :], ident[0:rows_, 0:rows_])
                ins.then_inc(sem("selT_mm"), 1)

            def back(experts):
                for i, t0, rows_ in TILES:
                    for h in range(2):
                        for q, (e, at_) in enumerate(experts):
                            ins = mm(bank(2 + 2 * i + h)[0:rows_, :], selT[:, e, t0:t0 + rows_],
                                     moe_y[:, at_, 512 * h:512 * h + 512], q == 0, q == len(experts) - 1)
                        ins.then_inc(sem("back_mm"), 1)

            for e in range(NE):
                if e >= 2:
                    pe.wait_ge(sem("moe_h_ready"), 2 * e - 2)
                gather(e, e, 2 * (e % 2))
            for e in range(NE):
                if e >= 2:
                    pe.wait_ge(sem("selT_ready"), e - 1)
                turn_sel(e, e, 4 + e % 2)
            pe.wait_ge(sem("moe_h_ready"), 2 * NE)
            pe.wait_ge(sem("selT_ready"), NE)

            def expert(n, h_in):
                for m in range(2 * NSTEP + 1):
                    if m < 2 * NSTEP:
                        j, q = m // 2, m % 2
                        g, u, dn = slot(j % NSLOT)
                        loads = 3 if j % NSLOT < 3 else 2
                        if q == 0:
                            pe.wait_ge(sem(f"weights{j % NSLOT}"), n * (48 * loads) + 48 * (loads + j // NSLOT + 1))
                        if m >= 2:
                            pe.wait_ge(sem("ff_ready"), n * 2 * NSTEP + 2 * NSTEP + m - 1)
                        for w, b_, signal in ((g, 2 + 2 * q, "ff_gate_mm"), (u, 3 + 2 * q, "ff_up_mm")):
                            for k in range(KD):
                                ins = mm(bank(b_)[:, 0:CAP], w[:, k, q * P:(q + 1) * P],
                                         h_in(k), k == 0, k == KD - 1)
                            ins.then_inc(sem(signal), 1)
                    if m:
                        c = m - 1
                        dn = slot((c // 2) % NSLOT)[2]
                        pe.wait_ge(sem("ff_ready"), n * 2 * NSTEP + 2 * NSTEP + m)
                        for h in range(2):
                            ins = mm(bank(h)[0:CAP, :], moe_ff[:, c % 4, :], dn[:, c % 2, 512 * h:512 * h + 512],
                                     c == 0, c == 2 * NSTEP - 1)
                            if c % 2 and h == 1 and c < 2 * NSTEP - 1:
                                ins.then_inc(sem("ff_used"), 1)
                            elif c == 2 * NSTEP - 1:
                                ins.then_inc(sem("moe_down_mm" if h == 1 else "ff_used"), 1)
            with pe.Fori(0, NE) as e:
                expert(e, lambda k: moe_h[:, ds(e, 1), k, :].rearrange("p a b -> p (a b)"))
            pe.wait_ge(sem("moe_y0"), NE)
            pe.wait_ge(sem("moe_y1"), NE)
            back([(e, e) for e in range(NE)])

            def overflow(w):
                n = w + NE
                pe.wait_ge(sem("y_out_ready"), 6 * w + 6)
                gather(n, 0, 2)
                turn_sel(n, 0, 4)
                pe.wait_ge(sem("moe_h_ready"), 2 * n + 2)
                pe.wait_ge(sem("selT_ready"), n + 1)
                expert(n, lambda k: moe_h[:, 0, k, :])
                pe.wait_ge(sem("moe_y0"), n + 1)
                pe.wait_ge(sem("moe_y1"), n + 1)
                back([(0, 1)])

            while_overflow(pe, overflow)

        @block.vector
        def _(dve):
            own = Own(dve, sem("dve_step"))

            def norm(k, gain, xn=xn):
                dve.wait_ge(sem("ss_ready"), 3 * (k + 1))
                dve.tensor_scalar(ms, ss, 1.0 / D, EPS, ALU.mult, ALU.add).then_inc(sem("ms_ready"), 1)
                dve.wait_ge(sem("rstd_ready"), RSTD[k])
                for i, t0, n in TILES:
                    dve.tensor_scalar(xn[0:n, i, :], x[0:n, i, :], rstd[0:n, i:i + 1], None,
                                      ALU.mult).then_inc(sem("xn_ready"), 1)
                for i, t0, n in TILES:
                    for g in range(2):
                        dve.wait_ge(sem("xnT_mm"), 6 * k + 2 * i + g + 1)
                        dve.tensor_tensor(hT[:, 4 * g:4 * g + 4, t0:t0 + n], bank(2 * i + g, 4, n),
                                          gain[:, 4 * g:4 * g + 4].unsqueeze(2).to_broadcast([P, 4, n]),
                                          ALU.mult).then_inc(sem("hT_ready"), 1)

            dve.memset(ss, 1.0).then_inc(sem("cleared"), 1)
            dve.memset(raw_dt.rearrange("p a b -> p (a b)"), 0.0).then_inc(sem("cleared"), 1)
            dve.memset(u_p[:, :, 0:30], 0.0)
            own.link(dve.memset(xbc_p[:, :, 0:3], 0.0))
            dve.wait_ge(sem("params_ready"), 3)
            norm(0, vecD[:, :, 0])
            for c in range(CA):
                dve.wait_ge(sem("sig_ready"), c + 1)
                dve.tensor_tensor(u_p[:, c, 30:], bank(c)[:, 0:SEQ], ua[:, c, 0:SEQ], ALU.mult)
                dve.tensor_tensor(u_s[:, c, :, 30:], bank(c)[:, SEQ:T].rearrange("p (b t) -> p b t", b=NB),
                                  ua[:, c, SEQ:T].rearrange("p (b t) -> p b t", b=NB), ALU.mult).then_inc(sem("u_ready"), 1)
            dve.wait_ge(sem("u_ready"), CA)
            dve.wait_ge(sem("halo_ready"), 9)

            def conv(dst_p, dst_s, src_p, src_s, taps, bias, width, signal):
                for j in range(width):
                    for dst, src in ((dst_p, src_p[:, j:j + SEQ]), (dst_s, src_s[:, :, j:j + NT])):
                        if j:
                            own.wait(1)
                            ins = dve.scalar_tensor_tensor(dst, src, taps[:, j:j + 1], dst, ALU.mult, ALU.add)
                        else:
                            ins = dve.tensor_scalar(dst, src, taps[:, 0:1], 0.0 if bias is None else bias,
                                                    ALU.mult, ALU.add)
                        if j == width - 1 and dst is dst_s:
                            ins.then_inc(sem(signal), 1)
                        else:
                            own.mark(ins)

            def tokens(a, c):
                return a[:, c, 0:SEQ], a[:, c, SEQ:T].rearrange("p (b t) -> p b t", b=NB)

            for c in range(CA):
                own.wait()
                conv(*tokens(ua, c), u_p[:, c, :], u_s[:, c], vecA[:, c, :], vecA[:, c, 31:32], WA, "ua_ready")
            dve.wait_ge(sem("dt_raw_ready"), 3)
            dve.wait_ge(sem("rows_in"), 16 * 10)
            own.link(dve.tensor_tensor(raw_dt, raw_dt, rows["e_dt_bias"].unsqueeze(1).to_broadcast([P, 3, NH]), ALU.add))
            dve.scalar_tensor_tensor(dt_abs, raw_dt, -1.0, raw_dt, ALU.mult, ALU.max).then_inc(*reaches("dt_abs_ready"))
            for c in range(XC):
                dve.wait_ge(sem("xbc_ready"), c + 1)
                conv(*tokens(xbcT, c), xbc_p[:, c, :], xbc_s[:, c], vecB[:, c, :], vecB[:, c, 4:5], WB, "conv_b_ready")
            dve.wait_ge(*reached("dt_log_ready"))
            own.link(dve.scalar_tensor_tensor(dts, raw_dt, 0.0, dt_log, ALU.max, ALU.add))
            dve.tensor_tensor(dA, dts, neg_a.unsqueeze(1).to_broadcast([P, 3, NH]), ALU.mult).then_inc(*reaches("dA_ready"))
            mean, var, r = small
            dve.wait_ge(*reached("mean_mm"))
            own.link(dve.tensor_scalar(mean, bank(3)[:, 0:T], 1.0 / DA, None, ALU.mult))
            dve.tensor_tensor(ua, ua, mean.unsqueeze(1).to_broadcast([P, CA, T]), ALU.subtract).then_inc(*reaches("ua_centred"))
            dve.wait_ge(*reached("var_mm"))
            dve.tensor_scalar(var, bank(4)[:, 0:T], 1.0 / DA, EPS, ALU.mult, ALU.add).then_inc(sem("ms_ready"), 1)
            dve.wait_ge(sem("rstd_ready"), 2)
            dve.tensor_tensor(ua, ua, r.unsqueeze(1).to_broadcast([P, CA, T]), ALU.mult).then_inc(*reaches("ua_normed"))
            dve.wait_ge(sem("x_tok_ready"), 9)
            for i, t0, n in TILES:
                xt = x_tok[0:n, i, :].rearrange("p (h q) -> p h q", h=NH)

                def per_head(a):
                    return a[0:n].unsqueeze(2).to_broadcast([n, NH, HP])

                dve.wait_ge(sem("cum_mm"), i + 1)
                own.mark(dve.tensor_scalar(negcum[0:n], bank(0)[0:n, 0:16], -1.0, None, ALU.mult))
                own.mark(dve.tensor_copy(cumT[0:16, 0:n], bank(0)[0:16, 32:32 + n]))
                own.wait()
                dve.tensor_tensor(w_arg[0:n], bank(0)[0:n, 16:32], negcum[0:n], ALU.add).then_inc(sem("cumT_ready"), 1)
                dve.tensor_tensor(xdt[0:n], xt, per_head(dts[:, i, :]), ALU.mult).then_inc(sem("xdt_ready"), 1)
                dve.wait_ge(sem("xdt_ready"), i + 1)
                dve.wait_ge(sem("scan_exps_ready"), i + 1)
                dve.tensor_tensor(xw[0:n], xdt[0:n], per_head(w_end), ALU.mult).then_inc(sem("xw_ready"), 1)
                if i == 2:
                    own.mark(dve.memset(c_pad.rearrange("p a b c -> p (a b c)"), 0.0))
                    own.wait()
                    for b in range(NB):
                        ins = dve.tensor_copy(c_pad[:, :, b, NT * b:NT * b + NT], xbcT[:, 10:12, t0 + NT * b:t0 + NT * b + NT])
                    ins.then_inc(*reaches("c_pad_ready"))
                    dve.wait_ge(sem("p_ssmT_mm"), 2)
                    dve.tensor_copy(dA_rows[0:n].rearrange("p (h q) -> p h q", h=NH),
                                    per_head(dA[:, i, :])).then_inc(*reaches("dA_rows_ready"))
                dve.wait_ge(sem("cb_mm"), i + 1)
                for g in range(NG):
                    dve.wait_ge(sem("decay_ready"), 4 * i + 2 * g + 2)
                    v = decay[0:n, 8 * g:8 * g + 8, 0:n]
                    dve.tensor_tensor(v, v, bank(1, 2, n)[0:n, g, :].unsqueeze(1).to_broadcast([n, 8, n]),
                                      ALU.mult).then_inc(sem("wts_ready"), 1)
                if i < 2:
                    dve.wait_ge(sem("state_mm"), i + 1)
                    if i == 1:
                        dve.wait_ge(*reached("inter_mm"))
                        v = p_state.rearrange("p (h q) -> p h q", h=NH)
                        own.link(dve.tensor_tensor(v, v, per_head(e_last), ALU.mult))
                    for g in range(2):
                        v = p_state[:, 512 * g:512 * g + 512]
                        if i == 0:
                            dve.tensor_copy(v, bank(4 + g)).then_inc(sem("p_state_ready"), 1)
                        else:
                            dve.tensor_tensor(v, v, bank(4 + g), ALU.add).then_inc(sem("p_state_ready"), 1)
                else:
                    for b in range(NB):
                        if b >= 2:
                            dve.wait_ge(sem("h_add_mm"), b - 1)
                        dve.tensor_scalar(b_one[0:n, b % 2, :], b_tok[0:n, i, :], K["batch"][0:n, b:b + 1], None,
                                          ALU.mult).then_inc(sem("b_one_ready"), 1)
                        if b == 0:
                            dve.wait_ge(*reached("decs_ready"))
                            dve.wait_ge(sem("p_ssm_stored"), 16)
                        if b >= 2:
                            dve.wait_ge(sem(f"h_stored{b % 2}"), 16 * (b // 2))
                        dve.wait_ge(sem(f"h_old{b % 2}"), 16 * (b // 2 + 1))
                        dve.wait_ge(sem("h_add_mm"), b + 1)
                        for c in range(KD):
                            dve.scalar_tensor_tensor(h_new[b % 2][:, c, :], h_old[b % 2][:, c, :], decs[:, c, b:b + 1],
                                                     bank(c // 4, 4, P)[:, c % 4, :], ALU.mult, ALU.add
                                                     ).then_inc(sem("h_new_ready"), 1)
                dve.wait_ge(sem("y_mm"), i + 1)
                if i:
                    dve.wait_ge(*reached("inter_mm"))
                    if i == 2:
                        dve.wait_ge(sem("inter_acc"), 2 * NB)
                    for g in range(2):
                        own.mark(dve.tensor_tensor(y[0:n, 8 * g:8 * g + 8, :], bank(2 + g, 8, HP)[0:n],
                                                   e_cum[0:n, 8 * g:8 * g + 8].unsqueeze(2).to_broadcast([n, 8, HP]), ALU.mult))
                    own.wait()
                    for g in range(2):
                        own.mark(dve.tensor_tensor(y[0:n, 8 * g:8 * g + 8, :], y[0:n, 8 * g:8 * g + 8, :],
                                                   bank(6 + g, 8, HP)[0:n], ALU.add))
                else:
                    for g in range(2):
                        own.mark(dve.tensor_copy(y[0:n, 8 * g:8 * g + 8, :], bank(6 + g, 8, HP)[0:n]))
                own.link(dve.tensor_tensor(xt, xt, per_head(rows["e_d_skip"]), ALU.mult))
                own.link(dve.tensor_tensor(y[0:n], y[0:n], xt, ALU.add))
                dve.wait_ge(sem("xw_ready"), i + 1)
                dve.wait_ge(sem("z_ready"), 6)
                dve.tensor_tensor(y[0:n], y[0:n], z[0:n, i, :].rearrange("p (h q) -> p h q", h=NH), ALU.mult
                                  ).then_inc(sem("y_ready"), 1)
                dve.wait_ge(sem("gs_ready"), 2 * i + 2)
                dve.tensor_scalar(gms, gs, 2.0 / D, EPS, ALU.mult, ALU.add).then_inc(sem("ms_ready"), 1)
                dve.wait_ge(sem("rstd_ready"), 3 + i)
                for g in range(2):
                    ins = dve.tensor_scalar(y[0:n, 8 * g:8 * g + 8, :], y[0:n, 8 * g:8 * g + 8, :], grs[0:n, g:g + 1],
                                            None, ALU.mult)
                ins.then_inc(sem("yn_ready"), 1)
                for g in range(2):
                    dve.wait_ge(sem("yT_mm"), 2 * i + g + 1)
                    dve.tensor_tensor(mixT[:, 4 + 4 * g:8 + 4 * g, t0:t0 + n], bank(g, 4, n),
                                      vecD[:, 4 * g:4 * g + 4, 2:3].to_broadcast([P, 4, n]), ALU.mult
                                      ).then_inc(sem("mixT_ready"), 1)
            for h in range(2):
                for i, t0, n in TILES:
                    dve.wait_ge(sem("mix_out_mm"), 4 * h + 2 + i)
                    v = x[0:n, i, 512 * h:512 * h + 512]
                    dve.tensor_tensor(v, v, bank(3 * h + i)[0:n, :], ALU.add).then_inc(sem("x_ready"), 1)
            norm(1, vecD[:, :, 1])
            for m in range(2 * NSTEP):
                dve.wait_ge(sem("ff_up_mm"), m + 1)
                dve.wait_ge(sem("ff_silu"), m + 1)
                dve.tensor_tensor(ff[:, m % 4, :], silu_t[:, m % 2, :], bank(7)[:, 0:T], ALU.mult).then_inc(sem("ff_ready"), 1)

            def residual(first_bank, order, mm_signal, done):
                for q, (i, h) in enumerate(order):
                    n = TILES[i][2]
                    if mm_signal:
                        dve.wait_ge(sem(mm_signal), q + 1)
                    v = x[0:n, i, 512 * h:512 * h + 512]
                    dve.tensor_tensor(v, v, bank(first_bank + q)[0:n, :], ALU.add).then_inc(sem(done), 1)

            dve.wait_ge(sem("ff_used"), NSTEP)
            residual(0, [(i, h) for i in range(3) for h in range(2)], None, "x_ready")
            norm(2, vecD[:, :, 3])
            dve.memset(tok[:, 2, :], 0.0).then_inc(*reaches("tok_cleared"))
            dve.wait_ge(sem("tok_ready"), 8)
            ki = tok[:, :, 1024:1088]
            own.link(dve.reduce_sum(ki_s, ki, AX))
            own.link(dve.tensor_scalar(ki_s, ki_s, 1.0 / HD, None, ALU.mult))
            dve.tensor_tensor(ki, ki, ki_s.unsqueeze(2).to_broadcast([P, 3, HD]), ALU.subtract).then_inc(*reaches("ki_centred"))
            dve.wait_ge(*reached("ki_squared"))
            own.link(dve.reduce_sum(ki_v, rope_t[0].rearrange("p a b c -> p a (b c)")[:, :, 0:64], AX))
            dve.tensor_scalar(ki_ms, ki_v, 1.0 / HD, EPS, ALU.mult, ALU.add).then_inc(sem("ms_ready"), 1)
            dve.wait_ge(*reached("qk_squared"))
            own.link(dve.reduce_sum(qk_ss, squares1.rearrange("p a (h d) -> p (a h) d", d=HD), AX))
            dve.tensor_scalar(qk_ms, qk_ss, 1.0 / HD, EPS, ALU.mult, ALU.add).then_inc(sem("ms_ready"), 1)
            dve.wait_ge(sem("rstd_ready"), 8)
            own.link(dve.tensor_tensor(ki, ki, ki_rs.unsqueeze(2).to_broadcast([P, 3, HD]), ALU.mult))
            own.link(dve.tensor_tensor(ki, ki, rows["o_kidx_g"].unsqueeze(1).to_broadcast([P, 3, HD]), ALU.mult))
            own.link(dve.tensor_tensor(ki, ki, rows["o_kidx_b"].unsqueeze(1).to_broadcast([P, 3, HD]), ALU.add))
            dve.wait_ge(sem("rstd_ready"), 9)
            for i in range(3):
                v = tok[:, i, 0:640].rearrange("p (h d) -> p h d", d=HD)
                own.mark(dve.tensor_tensor(v, v, qk_rs[:, 10 * i:10 * i + 10].unsqueeze(2).to_broadcast([P, 10, HD]), ALU.mult))
            own.wait()
            for i in range(3):
                v = tok[:, i, 0:640].rearrange("p (h d) -> p h d", d=HD)
                own.mark(dve.tensor_tensor(v[:, 0:8], v[:, 0:8], rows["o_q_norm"].unsqueeze(1).to_broadcast([P, 8, HD]), ALU.mult))
                own.mark(dve.tensor_tensor(v[:, 8:10], v[:, 8:10], rows["o_k_norm"].unsqueeze(1).to_broadcast([P, 2, HD]), ALU.mult))
            own.wait()
            for a, heads in ((0, 10), (768, 5)):
                v = tok[:, :, a:a + HD * heads].rearrange("p a (h d) -> p a h d", d=HD)
                one, two = v[:, :, :, 0:8], v[:, :, :, 8:16]
                c_, s_ = (f.unsqueeze(2).to_broadcast([P, 3, heads, 8]) for f in (cos, sin))
                t = [r_[:, :, 0:heads, :] for r_ in rope_t]
                own.mark(dve.tensor_tensor(t[0], one, c_, ALU.mult))
                own.mark(dve.tensor_tensor(t[1], two, s_, ALU.mult))
                own.mark(dve.tensor_tensor(t[2], one, s_, ALU.mult))
                own.mark(dve.tensor_tensor(t[3], two, c_, ALU.mult))
                own.wait()
                dve.tensor_tensor(one, t[0], t[1], ALU.subtract)
                dve.tensor_tensor(two, t[2], t[3], ALU.add).then_inc(sem("rot_ready"), 1)
                dve.wait_ge(sem("rot_ready"), 1 if a == 0 else 2)
            for i in range(3):
                own.mark(dve.tensor_copy(q_tok[:, i].rearrange("p r (g d) -> p r g d", g=2),
                                         tok[:, i, 0:512].rearrange("p (g r d) -> p r g d", g=2, r=4)))
                own.mark(dve.tensor_copy(qi_tok[:, i].rearrange("p h (u d) -> p h u d", u=2),
                                         tok[:, i, 768:1024].rearrange("p (h d) -> p h d", d=HD).unsqueeze(2).to_broadcast([P, 4, 2, HD])))
            dve.tensor_copy(ki_tok.rearrange("p a (u d) -> p a u d", u=2),
                            ki.unsqueeze(2).to_broadcast([P, 3, 2, HD])).then_inc(sem("rot_ready"), 1)
            dve.wait_ge(sem("rotT_mm"), 9)
            dve.memset(cd_p[:, :, 0:2], 0.0).then_inc(*reaches("din_free"))
            for c in range(CA):
                dve.wait_ge(sem("din_ready"), c + 1)
                dve.wait_ge(sem("cg_mm"), c + 1)
                src, mul = tokens(din_t, c), bank(4 + c)
                dve.tensor_tensor(cd_p[:, c, 2:], src[0], mul[:, 0:SEQ], ALU.mult).then_inc(sem("cd_ready"), 1)
                dve.tensor_tensor(cd_s[:, c, :, 2:], src[1], mul[:, SEQ:T].rearrange("p (b t) -> p b t", b=NB),
                                  ALU.mult).then_inc(sem("cd_ready"), 1)
            dve.wait_ge(sem("cd_ready"), 2 * CA)
            dve.wait_ge(sem("halo1_ready"), 1)
            dve.tensor_copy(cd_last.rearrange("p c (b t) -> p c b t", b=NB), cd_s[:, :, :, NT:NT + 2]).then_inc(*reaches("cd_last_ready"))
            for c in range(CA):
                conv(*tokens(mix1T, 4 + c), cd_p[:, c, :], cd_s[:, c], vecA[:, c, 34:37], None, 3, "conv_d_taps")
            for c in range(CA):
                dve.wait_ge(sem("conv_d_taps"), c + 1)
                dve.wait_ge(sem("bg_mm"), c + 1)
                v = mix1T[:, 4 + c, :]
                ins = dve.tensor_tensor(v, v, bank(c)[:, 0:T], ALU.mult)
            ins.then_inc(*reaches("conv_d_ready"))
            dve.wait_ge(sem("rotT_ready"), 9)
            dve.wait_ge(sem("v_ready"), 2)
            dve.wait_ge(sem("tails1_mm"), 2)
            own.mark(dve.memset(q_blk.rearrange("p a b -> p (a b)"), 0.0))
            own.wait()
            for g in range(2):
                for r in range(4):
                    own.mark(dve.tensor_copy(q_blk[64 * g:64 * g + 64, :, 32 * g + 8 * r:32 * g + 8 * r + 8],
                                             qT[64 * g:64 * g + 64, r, SEQ:T].rearrange("p (b t) -> p b t", b=NB)))
            dve.tensor_copy(qi_b.rearrange("p b (h t) -> p b h t", h=4),
                            qiT[:, :, SEQ:T].rearrange("p h (b t) -> p b h t", b=NB)).then_inc(*reaches("q_packed"))
            for g in range(2):
                dve.tensor_tensor(rep[0:NS, g, :].rearrange("p (b h t) -> p b h t", b=4, h=4),
                                  ident[0:NS, 32 * g:32 * g + 32].rearrange("p (b t) -> p b t", b=4).unsqueeze(2).to_broadcast([NS, 4, 4, 8]),
                                  w_idx[0:NS, 2, :].unsqueeze(1).unsqueeze(3).to_broadcast([NS, 4, 4, 8]), ALU.mult
                                  ).then_inc(sem("wsT_ready"), 1)

            def choose(work, count):
                for _ in range(count // 8):
                    own.link(dve.max(best[0:work.shape[0]], work))
                    own.link(dve.match_replace(work, best[0:work.shape[0]], work, TAKEN))

            for i in range(2):
                dve.wait_ge(sem("relu_p_ready"), i + 1)
                v = sc_p[:, i, :]
                own.link(dve.tensor_scalar(v, relu_p[:, 0, :], w_idx[:, i, 0:1], None, ALU.mult))
                for h in range(1, 4):
                    own.mark(dve.scalar_tensor_tensor(v, relu_p[:, h, :], w_idx[:, i, h:h + 1], v, ALU.mult, ALU.add))
                    own.wait()
                dve.tensor_tensor(v, v, causal[:, i, :], ALU.add).then_inc(sem("sc_p_ready"), 1)
            dve.wait_ge(sem("sc_p_ready"), 2)
            for i in range(2):
                choose(sc_p[:, i, :], TOPP)
            own.link(dve.tensor_scalar(bias_p, sc_p, -2e38, NEG, ALU.is_gt, ALU.mult))
            dve.tensor_tensor(bias_p, bias_p, causal, ALU.min).then_inc(*reaches("sc_p_taken"))
            dve.wait_ge(*reached("sc_p_taken"))
            dve.wait_ge(*reached("isum_mm"))
            dve.wait_ge(sem("halo1_ready"), 1)
            dve.wait_ge(*reached("conv_d_ready"))
            own.link(dve.tensor_copy(work_s[0:NS, :], psum[0:NS, 0:KEYS]))
            own.link(dve.tensor_tensor(work_s[0:NS, PAST:], work_s[0:NS, PAST:], K["new_ok"][0:NS], ALU.mult))
            dve.tensor_tensor(work_s[0:NS, PAST:], work_s[0:NS, PAST:], K["new_neg"][0:NS], ALU.add).then_inc(*reaches("work_s_ready"))
            for i in range(2):
                dve.wait_ge(sem("s_p_mm"), i + 1)
                if i:
                    dve.wait_ge(sem("pt_prompt_mm"), 4)
                own.link(dve.tensor_tensor(probs_p, psum[:, 0:8 * SEQ].rearrange("p (h k) -> p h k", h=8),
                                           bias_p[:, i, :].unsqueeze(1).to_broadcast([P, 8, SEQ]), ALU.add))
                dve.reduce_max(mx, probs_p, AX).then_inc(sem("s_p_taken"), 1)
                dve.wait_ge(sem("s_p_taken"), i + 1)
                dve.tensor_scalar(nmx, mx, -HD ** -0.5, None, ALU.mult).then_inc(sem("nmx_p_ready"), 1)
                dve.wait_ge(sem("exp_p_ready"), i + 1)
                own.link(dve.reciprocal(rsum, sums))
                dve.tensor_tensor(probs_p, probs_p, rsum.unsqueeze(2).to_broadcast([P, 8, SEQ]), ALU.mult
                                  ).then_inc(sem("probs_p_ready"), 1)
            dve.wait_ge(*reached("wsT_mm"))
            dve.tensor_copy(rep[0:NS].rearrange("p q (b g t) -> p (q b) g t", b=2, g=8),
                            ident[0:NS, 0:NS].rearrange("p (b t) -> p b t", b=NB).unsqueeze(2).to_broadcast([NS, NB, 8, NT])
                            ).then_inc(*reaches("rep_ready"))
            dve.wait_ge(*reached("work_s_ready"))
            choose(work_s[0:NS, :], TOPS)
            dve.tensor_scalar(work_s[0:NS, :], work_s[0:NS, :], -2e38, NEG, ALU.is_gt, ALU.mult).then_inc(*reaches("bias_s_ready"))
            for q in range(NB // 2):
                dve.wait_ge(sem("masked_mm"), q + 1)
                own.link(dve.reduce_max(mx[:, 0:1], psum[:, 0:KEYS], AX))
                dve.tensor_scalar(nmx[:, 0:1], mx[:, 0:1], -HD ** -0.5, None, ALU.mult).then_inc(sem("nmx_ready"), 1)
                dve.wait_ge(sem("exp_ready"), q + 1)
                own.link(dve.reciprocal(rsum[:, 0:1], sums[:, 0:1]))
                dve.tensor_scalar(probs, probs, rsum[:, 0:1], None, ALU.mult).then_inc(sem("probs_ready"), 1)
                dve.wait_ge(sem("pv_mm"), 2 * q + 2)
                for b in range(2):
                    for g in range(2):
                        t0 = SEQ + NT * (2 * q + b)
                        dve.tensor_copy(mix1T[64 * g:64 * g + 64, 0:4, t0:t0 + NT],
                                        bank(7)[64 * g:64 * g + 64, 64 * b + 32 * g:64 * b + 32 * g + 32].rearrange("p (r t) -> p r t", r=4)
                                        ).then_inc(sem("att_s_ready"), 1)
            residual(0, [(i, h) for h in range(2) for i in range(3)], "out1_mm", "x_ready")
            norm(3, vecD[:, :, 4], xn3)
            for a in (logits, routed, gate, rank):
                own.mark(dve.memset(a.rearrange("p a b -> p (a b)"), 0.0))
            own.wait()
            dve.wait_ge(*reached("logits_mm"))
            b_r = rows["o_b_router"]
            own.mark(dve.tensor_tensor(logits[:, 0:2], bank(6)[:, 0:16].rearrange("p (a b) -> p a b", a=2),
                                       b_r.unsqueeze(1).to_broadcast([P, 2, NE]), ALU.add))
            own.mark(dve.tensor_tensor(logits[0:NS, 2], bank(6)[0:NS, 16:24], b_r[0:NS], ALU.add))
            own.wait()
            for i in range(3):
                own.mark(dve.max(top[:, i, :], logits[:, i, :]))
            own.wait()
            for i in range(3):
                own.mark(dve.max_index(top_i[:, i, :], top[:, i, :], logits[:, i, :]))
            own.wait()
            own.link(dve.tensor_copy(top_f, top_i))
            for i in range(3):
                for k, a in ((0, first), (1, second)):
                    own.mark(dve.tensor_scalar(a[:, i, :], K["slots"][:, 0:NE], top_f[:, i, k:k + 1], None, ALU.is_equal))
            own.wait()
            own.mark(dve.tensor_tensor(routed[:, 0:2], first[:, 0:2], second[:, 0:2], ALU.add))
            dve.tensor_tensor(routed[0:NS, 2], first[0:NS, 2], second[0:NS, 2], ALU.add).then_inc(*reaches("routed_ready"))
            dve.tensor_tensor(gap, top[:, :, 1], top[:, :, 0], ALU.subtract).then_inc(*reaches("gap_ready"))
            dve.wait_ge(*reached("e_gap_ready"))
            own.link(dve.tensor_scalar(g_one, e_gap, 1.0, None, ALU.add))
            own.link(dve.reciprocal(g_one, g_one))
            own.link(dve.tensor_tensor(g_two, g_one, e_gap, ALU.mult))
            own.mark(dve.tensor_tensor(first, first, g_one.unsqueeze(2).to_broadcast([P, 3, NE]), ALU.mult))
            own.mark(dve.tensor_tensor(second, second, g_two.unsqueeze(2).to_broadcast([P, 3, NE]), ALU.mult))
            own.wait()
            own.link(dve.tensor_tensor(gate, first, second, ALU.add))
            dve.wait_ge(*reached("rank_mm"))
            own.mark(dve.tensor_scalar(rank[:, 0:2], bank(7)[:, 0:16].rearrange("p (a b) -> p a b", a=2), -1.0, None, ALU.add))
            own.mark(dve.tensor_scalar(rank[0:NS, 2], bank(7)[0:NS, 16:24], -1.0, None, ALU.add))
            own.wait()

            own.link(dve.tensor_copy(counts, bank(7)[:, 3 * NE:4 * NE]))
            own.mark(dve.tensor_scalar(more[0], counts, float(CAP), None, ALU.is_gt))
            own.mark(dve.tensor_scalar(more[1], counts, 2.0 * CAP, None, ALU.is_gt))
            own.mark(dve.memset(upto[0][:, 0:8], 0.0))
            own.mark(dve.memset(upto[1][:, 0:8], 0.0))
            own.wait()
            own.link(dve.tensor_tensor(more[0], more[0], more[1], ALU.add))
            own.link(dve.tensor_copy(upto[0][:, 8:16], more[0]))
            for k, shift in enumerate((1, 2, 4)):
                own.link(dve.tensor_tensor(upto[(k + 1) % 2][:, 8:16], upto[k % 2][:, 8:16],
                                           upto[k % 2][:, 8 - shift:16 - shift], ALU.add))
            total = upto[1][:, 8:16]
            for w in range(NOVER):
                own.mark(dve.tensor_scalar(before, total, float(w), 0.0, ALU.is_le, ALU.add, accum_out=over_e[:, w:w + 1]))
                own.wait()
                own.mark(dve.tensor_tensor(before, before, more[0], ALU.mult))
                own.wait()
                own.link(dve.reduce_sum(over_at[:, w:w + 1], before, AX))
                own.link(dve.tensor_scalar(over_at[:, w:w + 1], over_at[:, w:w + 1], -float(CAP), float(CAP * (w + 1)),
                                           ALU.mult, ALU.add))
            own.link(dve.tensor_copy(over_e[:, NOVER:NOVER + 1], total[:, 7:8]))
            dve.tensor_copy(over_i, over_e).then_inc(*reaches("over_ready"))

            def slots(rank_of, weight, e, done):
                for i, t0, n in TILES:
                    dve.tensor_scalar(sel[0:n, i, e, :], K["slots"][0:n, 0:CAP], rank_of(i)[0:n], weight(i)[0:n],
                                      ALU.is_equal, ALU.mult).then_inc(sem(done), 1)

            def column(a, e):
                return lambda i: a[:, i, e:e + 1] if isinstance(e, int) else a[:, i, ds(e, 1)]

            def slot_features(n, e, banks_):
                for g in range(2):
                    dve.wait_ge(sem("moe_h_mm"), 2 * n + g + 1)
                    dve.tensor_tensor(moe_h[:, e, 4 * g:4 * g + 4, :], bank(banks_ + g, 4, P)[:, :, 0:CAP],
                                      vecD[:, 4 * g:4 * g + 4, 4:5].to_broadcast([P, 4, CAP]), ALU.mult
                                      ).then_inc(sem("moe_h_ready"), 1)

            def expert(n, y_out):
                for m in range(2 * NSTEP):
                    dve.wait_ge(sem("ff_up_mm"), n * 2 * NSTEP + 2 * NSTEP + m + 1)
                    dve.wait_ge(sem("ff_silu"), n * 2 * NSTEP + 2 * NSTEP + m + 1)
                    dve.tensor_tensor(moe_ff[:, m % 4, :], moe_silu[:, m % 2, :], bank(3 + 2 * (m % 2))[:, 0:CAP],
                                      ALU.mult).then_inc(sem("ff_ready"), 1)
                dve.wait_ge(sem("moe_down_mm"), n + 1)
                dve.tensor_copy(y_out, bank(0).unsqueeze(1)).then_inc(sem("moe_y0"), 1)

            for e in range(NE):
                slots(column(rank, e), column(routed, e), e, "sel_ready")
            for e in range(NE):
                slot_features(e, e, 2 * (e % 2))
            for e in range(NE):
                slots(column(rank, e), column(gate, e), e, "gated_ready")
            with dve.Fori(0, NE) as e:
                expert(e, moe_y[:, ds(e, 1), 0:512])
            order = [(i, h) for i in range(3) for h in range(2)]
            residual(2, order, "back_mm", "y_out_ready")

            def overflow(w):
                n = w + NE
                e = dve.value_load(over_i[0:1, ds(w, 1)], min_val=0, max_val=NE - 1)
                dve.tensor_tensor(over_rank, rank[:, :, ds(e, 1)], over_at[:, ds(w, 1)].unsqueeze(1).to_broadcast([P, 3, 1]),
                                  ALU.subtract).then_inc(sem("over_step"), 1)
                dve.wait_ge(sem("over_step"), w + 1)
                slots(lambda i: over_rank[:, i, :], column(routed, e), 0, "sel_ready")
                slot_features(n, 0, 2)
                slots(lambda i: over_rank[:, i, :], column(gate, e), 0, "gated_ready")
                expert(n, moe_y[:, 1:2, 0:512])
                for q, (i, h) in enumerate(order):
                    rows_ = TILES[i][2]
                    dve.wait_ge(sem("back_mm"), 6 * w + 7 + q)
                    v = x[0:rows_, i, 512 * h:512 * h + 512]
                    ins = dve.tensor_tensor(v, v, bank(2 + q)[0:rows_, :], ALU.add)
                    ins.then_inc(sem("y_out_ready"), 1)

            while_overflow(dve, overflow)


INS = ['x_prompt', 'x_sample', 'state_conv_a', 'state_ssm', 'state_conv_b', 'cache_k', 'cache_v', 'cache_kidx',
       'state_conv_d', 'page_table', 'e_norm_mix', 'e_w_in', 'e_conv_a_w', 'e_conv_a_b', 'e_ln_a_g', 'e_ln_a_b',
       'e_conv_b_w', 'e_conv_b_b', 'e_dt_bias', 'e_a_log', 'e_d_skip', 'e_ssm_norm', 'e_w_out', 'e_norm_ffn',
       'e_w_gate', 'e_w_up', 'e_w_down', 'o_norm_mix', 'o_w_in', 'o_q_norm', 'o_k_norm', 'o_kidx_g', 'o_kidx_b',
       'o_conv_d_w', 'o_w_out', 'o_norm_ffn', 'o_w_router', 'o_b_router', 'o_we_gate', 'o_we_up', 'o_we_down']
OUTS = [("y_prompt", (1, SEQ, D)), ("y_sample", (NB, NT, D)), ("p_conv_a", (1, 1, WA - 1, DA)),
        ("p_ssm", (1, 1, NH, HP, NST)), ("p_conv_b", (1, 1, WB - 1, XC * P)), ("p_k", (1, 1, SEQ, 2, HD)),
        ("p_v", (1, 1, SEQ, 2, HD)), ("p_kidx", (1, 1, SEQ, HD)), ("p_conv_d", (1, 1, 2, DA)),
        ("s_conv_a", (1, NB, WA - 1, DA)), ("s_ssm", (1, NB, NH, HP, NST)), ("s_conv_b", (1, NB, WB - 1, XC * P)),
        ("s_k", (1, NB, NT, 2, HD)), ("s_v", (1, NB, NT, 2, HD)), ("s_kidx", (1, NB, NT, HD)),
        ("s_conv_d", (1, NB, 2, DA))]


def kernel(**inputs):
    import numpy as np
    from concourse import bacc
    from concourse.bass_utils import run_bass_kernel_spmd

    nc = bacc.Bacc("TRN2", target_bir_lowering=False, num_devices=1)
    arrays = {"constants": constants()}
    for name in INS:
        arrays[name] = np.ascontiguousarray(inputs[name])
    inp = {n: nc.dram_tensor(n, a.shape, mybir.dt.from_np(a.dtype), kind="ExternalInput").ap()
           for n, a in arrays.items()}
    out = {n: nc.dram_tensor(n, s, F32, kind="ExternalOutput").ap() for n, s in OUTS}
    step_program(nc, inp, out)
    r = run_bass_kernel_spmd(nc, [arrays], core_ids=[0])
    return tuple(r.results[0][n] for n, _ in OUTS)
```

```python
from contextlib import ExitStack

import concourse.bass as bass
from concourse import mybir
from concourse.alu_op_type import AluOpType as ALU

F32 = mybir.dt.float32
F32R = mybir.dt.float32r
I32 = mybir.dt.int32
U32 = mybir.dt.uint32
ACT = mybir.ActivationFunctionType
AX = mybir.AxisListType.X
ds = bass.ds

P = 128
WORDS = 53184
KEPT = 34436
D = 1024
KD = D // P
SEQ = 256
NB = 8
NT = 8
NS = NB * NT
T = SEQ + NS
TILES = [(0, 0, P), (1, P, P), (2, 2 * P, NS)]
DA = 512
CA = DA // P
WA = 31
XC = 12
WB = 4
NH = 16
HP = 64
NG = 2
NST = 128
DFF = 2816
FS = 256
NSTEP = DFF // FS
NE = 8
PAST = 2048
PAGE = 128
N_POOL = 160
NPG = PAST // PAGE
KEYS = PAST + NT
TOPP = 64
TOPS = 256
EPS = 1e-6
NEG = -1e30
TAKEN = -3e38
CAP = 128
NBLOCK = -(-T // CAP)
NOVER = (2 * T - 1) // CAP
HD = 64
E_IN = 2 * DA + D + XC * P + NH

CONST = {}
_at = 0
for _n, _w in (("ident", 128), ("ones", 128), ("tri_p", 128), ("tri_s", 64), ("last_s", 64), ("mask_p", 128),
               ("mask_s", 64), ("causal", 512), ("new_ok", 8), ("new_neg", 8), ("cos", 24), ("sin", 24),
               ("batch", 8), ("slots", 128), ("half", 3), ("head_row", 16 * 128)):
    CONST[_n] = (_at, _w)
    _at += _w
NCONST = _at


def constants():
    import numpy as np
    c = np.zeros((P, NCONST), np.float32)

    def put(name, a):
        o, w = CONST[name]
        a = np.asarray(a, np.float32).reshape(a.shape[0], -1)
        c[:a.shape[0], o:o + a.shape[1]] = a

    i = np.arange(P)
    j = np.arange(NS)
    put("ident", np.eye(P))
    put("ones", np.ones((P, P)))
    put("tri_p", i[:, None] <= i[None, :])
    same = (j[:, None] // NT) == (j[None, :] // NT)
    put("tri_s", same & (j[:, None] <= j[None, :]))
    put("last_s", same)
    put("mask_p", np.where(i[:, None] <= i[None, :], 0, NEG))
    put("mask_s", np.where(same & (j[:, None] <= j[None, :]), 0, NEG))
    key = np.arange(SEQ)
    put("causal", np.stack([np.where(key[None] <= (i + t * P)[:, None], 0, NEG) for t in range(2)], 1))
    ok = (np.arange(NT)[None] <= (j % NT)[:, None])
    put("new_ok", ok)
    put("new_neg", np.where(ok, 0, NEG))
    half = 8
    inv = np.float32(500000.0) ** (-np.arange(half, dtype=np.float32) / np.float32(half))
    pos = np.zeros((P, 3), np.float32)
    pos[:, 0], pos[:, 1] = i, i + P
    pos[:NS, 2] = PAST + j % NT
    ang = (pos[:, :, None] * inv[None, None].astype(np.float32)).astype(np.float32)
    put("cos", np.cos(ang))
    put("sin", np.sin(ang))
    put("batch", (j[:, None] // NT) == np.arange(NB)[None])
    put("slots", np.broadcast_to(i[None], (P, P)))
    put("half", np.full((P, 3), -0.5))
    put("head_row", np.repeat(np.eye(NH, dtype=np.float32)[:, :, None], P, 2))
    return c


RING = 0
SLOT = 4096
STEP = 8 * FS * 2 + 2 * D
NSLOT = 4
NSLOT0 = 3
TAIL = RING + 4 * SLOT
FIXED = RING + NSLOT * STEP


class Own:

    def __init__(self, eng, semaphore):
        self.eng, self.semaphore, self.n = eng, semaphore, 0

    def mark(self, ins):
        ins.then_inc(self.semaphore, 1)
        self.n += 1

    def wait(self, behind=0):
        if self.n > behind:
            self.eng.wait_ge(self.semaphore, self.n - behind)

    def link(self, ins):
        self.mark(ins)
        self.wait()


def step_program(nc, inp, out):
    with ExitStack() as ctx:
        arena = ctx.enter_context(nc.sbuf_tensor("arena", [P, KEPT], F32))
        with nc.sbuf_tensor("parts", [P, WORDS - KEPT], F32R) as parts:
            pass
        zone = ctx.enter_context(nc.sbuf_tensor("zone", [P, WORDS - KEPT], F32))
        psum = ctx.enter_context(nc.psum_tensor("psum", [P, 8 * 512], F32))
        sems = {}

        def sem(name):
            if name not in sems:
                sems[name] = ctx.enter_context(nc.semaphore(name))
            return sems[name]

        where = [FIXED]

        def at(off, *dims):
            n = 1
            for d in dims:
                n *= d
            if off >= KEPT:
                v = zone[:, off - KEPT:off - KEPT + n]
            else:
                assert off + n <= KEPT
                v = arena[:, off:off + n]
            if len(dims) == 2:
                v = v.rearrange("p (a b) -> p a b", a=dims[0])
            elif len(dims) == 3:
                v = v.rearrange("p (a b c) -> p a b c", a=dims[0], b=dims[1])
            elif len(dims) == 4:
                v = v.rearrange("p (a b c d) -> p a b c d", a=dims[0], b=dims[1], c=dims[2])
            return v

        def new(*dims):
            n = 1
            for d in dims:
                n *= d
            v = at(where[0], *dims)
            where[0] += n
            assert where[0] <= WORDS, where[0]
            return v

        def bank(i, *dims):
            v = psum[:, 512 * i:512 * i + 512]
            if dims:
                n = 1
                for d in dims:
                    n *= d
                v = psum[:, 512 * i:512 * i + n]
                if len(dims) == 2:
                    v = v.rearrange("p (a b) -> p a b", a=dims[0])
                elif len(dims) == 3:
                    v = v.rearrange("p (a b c) -> p a b c", a=dims[0], b=dims[1])
            return v

        const = new(NCONST)
        K = {n: const[:, o:o + w] for n, (o, w) in CONST.items()}
        ident = K["ident"]
        ones = K["ones"]
        causal = K["causal"].rearrange("p (a b) -> p a b", a=2)
        cos = K["cos"].rearrange("p (a b) -> p a b", a=3)
        sin = K["sin"].rearrange("p (a b) -> p a b", a=3)
        head_row = K["head_row"].rearrange("p (a b) -> p a b", a=NH)
        HEAD_ROW = FIXED + CONST["head_row"][0]
        x = new(3, D)
        HT = where[0]
        hT = new(KD, T)
        vecA = new(CA, 37)
        vecB = new(XC, 5)
        vecD = new(KD, 5)
        rows = {}
        for n, w in (("e_dt_bias", 16), ("e_a_log", 16), ("e_d_skip", 16), ("o_q_norm", 64), ("o_k_norm", 64),
                     ("o_kidx_g", 64), ("o_kidx_b", 64), ("o_b_router", 8)):
            rows[n] = new(w)
        w_router = new(KD, NE)
        pages = new(P)
        ss = new(3)
        ms = new(3)
        rstd = new(3)
        FREE = where[0]
        assert FREE == KEPT, FREE

        u_p = new(CA, WA - 1 + SEQ)
        u_s = new(CA, NB, WA - 1 + NT)
        ua = new(CA, T)
        mixT = new(CA + KD, T)
        XBC = where[0]
        xbc_p = new(XC, WB - 1 + SEQ)
        xbc_s = new(XC, NB, WB - 1 + NT)
        Z = where[0]
        z = new(3, D)
        XT = where[0]
        x_tok = new(3, D)
        xn = at(Z, 3, D)
        param_rows = at(XT, 3 * D)
        xbcT = at(TAIL, XC, T)
        b_tok = at(TAIL + XC * T, 3, NG * NST)
        TMP = TAIL + XC * T + 3 * NG * NST
        xdt = at(TMP, NH, HP)
        xw = at(TMP + D, NH, HP)
        y = at(TMP + 2 * D, NH, HP)
        b_one = at(TMP + 3 * D, 2, NG * NST)
        assert TMP + 3 * D + 512 <= FIXED
        decay = at(FREE, NH, P)
        state_a = at(TMP, 2, DA)
        state_b = at(TMP + D, XC * P)
        squares = at(TMP, CA, T)
        small = [at(TMP + 1280 + 320 * i, T) for i in range(3)]
        h_old = [at(XBC + D * i, KD, P) for i in range(2)]
        h_new = [at(XBC + 2 * D + D * i, KD, P) for i in range(2)]
        h_oldT = at(TAIL, D)
        p_state = at(TAIL, D)
        dA_rows = at(TAIL + D, D)
        c_pad = at(FREE + 4 * 286 + 4 * 8 * 38, NG, NB, NS)
        raw_dt = new(3, NH)
        dts, dA, dt_abs, dt_log = new(3, NH), new(3, NH), new(3, NH), new(3, NH)
        negcum, w_end, e_cum, e_last, neg_a, w_arg = [new(NH) for _ in range(6)]
        decs = new(KD, NB)
        w_dt = new(KD, NH)
        u_last = at(TMP + 2 * D, CA, NS)
        xbc_last = at(TMP + 2 * D + CA * NS, XC, NB * 3)
        tail_us, tail_up, tail_xp = at(XT, 512), at(XT + 512, 512), at(XT + 1024, XC * P)
        tail_xs = mixT[:, CA:CA + 5, :].rearrange("p a b -> p (a b)")[:, 0:XC * P]
        cumT = at(TMP + 3 * D, P)
        gs, gms, grs = new(2), new(2), new(2)

        silu_t = at(HT, 2, T)
        ff = at(HT + 2 * T, T)
        where_part = [0]

        def new_parts(*dims):
            n = 1
            for d in dims:
                n *= d
            both = []
            for _ in range(2):
                v = parts[:, where_part[0]:where_part[0] + n]
                where_part[0] += n
                both.append(v.rearrange("p (a b) -> p a b", a=dims[0]) if len(dims) == 2 else
                            v.rearrange("p (a b c) -> p a b c", a=dims[0], b=dims[1]) if len(dims) == 3 else v)
            return both

        x_parts = new_parts(KD, T)
        gu_parts = [new_parts(2, KD, P) for _ in range(2)]
        down_parts = [new_parts(D) for _ in range(2)]
        ff_parts = [new_parts(T) for _ in range(2)]
        CHUNKS = 2 * NSTEP
        SPLITS = [("gu", 0), ("gu", 1), ("down", 0)]
        for m in range(CHUNKS):
            SPLITS += [("gu", m + 2)] * (m + 2 < CHUNKS) + [("down", m + 1)] * (m + 1 < CHUNKS)

        def downs(n, m):
            return n * CHUNKS + CHUNKS + m

        def moe_split(n, m):
            return n * CHUNKS + len(SPLITS) + m + 1

        def arrivals(n, j):
            loads = 3 if j % NSLOT < 3 else 2
            before_ = (4, 4, 3, 0)[j % NSLOT]
            return n * (48 * loads) + 48 * (before_ + j // NSLOT + 1)

        def split_at(kind, m):
            return SPLITS.index((kind, m)) + 1

        def slot(s):
            o = RING + s * STEP
            return at(o, KD, FS), at(o + KD * FS, KD, FS), at(o + 2 * KD * FS, 2, D)

        def to_split(kind, m):
            g, u, dn = slot(m // 2 % NSLOT0)
            q = m % 2
            if kind == "down":
                return [(dn[:, q, :], down_parts[q][0], down_parts[q][1])]
            return [(w[:, :, q * P:(q + 1) * P], gu_parts[q][0][:, i], gu_parts[q][1][:, i]) for i, w in enumerate((g, u))]

        where[0] = FREE
        qT = new(4, T)
        kkT = new(2, T)
        qiT = new(4, T)
        mix1T = new(KD, T)
        v_new = new(NB, P)
        q_blk = new(NB, 64)
        WORK = where[0]
        work_s = new(KEYS)
        bias_p = new(2, SEQ)
        rep = new(4, P)
        qi_b = new(NB, 32)
        ws = new(2, NS)
        best = new(8)
        mx, nmx, sums, rsum = new(8), new(8), new(8), new(8)
        qk_ss, qk_ms, qk_rs = new(30), new(30), new(30)
        ki_s, ki_v, ki_ms, ki_rs = new(3), new(3), new(3), new(3)
        rope_t = [at(WORK + 240 * i, 3, 10, 8) for i in range(4)]
        v_tok = new(3, P)
        w_idx = new(3, 4)
        ZB = where[0]
        tok = new(3, 1092)
        q_tok = new(3, 4, P)
        qi_tok = new(3, 4, P)
        ki_tok = new(3, P)
        cd_p = at(WORK - NB * 64 - NB * P, CA, 2 + SEQ)
        cd_last = at(WORK - NB * 64 - NB * P + CA * (2 + SEQ), CA, 16)
        cd_s = at(4 * SLOT + KD * 68, CA, NB, 2 + NT)
        state_d = at(4 * SLOT + KD * 68 + CA * NB * (2 + NT), DA)
        tail_dp, tail_ds = at(ZB + KEYS + 2 * PAST, DA), at(ZB + KEYS + 2 * PAST + DA, DA)
        assert ZB + KEYS + 2 * PAST + 2 * DA <= WORDS
        squares1 = at(ZB + 3 * 1092, 3, 640)
        where[0] = ZB
        relu_s = [new(KEYS) for _ in range(2)]
        relu_p = at(ZB, 4, SEQ)
        sc_p = at(ZB + 4 * SEQ, 2, SEQ)
        KIDX = NPG * HD
        kidx = [at(RING + NSLOT0 * STEP + KIDX * b if b < 6 else HEAD_ROW + KIDX * (b - 6), NPG, HD) for b in range(NB)]
        kidxT = [at(ZB + 2 * KEYS + KIDX * i, NPG // 2, P) for i in range(2)]
        B3 = ZB
        probs = at(B3, KEYS)
        K_AT = [RING + PAST * i for i in (0, 1, 4, 5, 8, 9)] + [HEAD_ROW, B3 + KEYS]
        V_AT = [RING + PAST * i for i in (2, 3, 6, 7, 10, 11)] + [B3 + KEYS + PAST, RING]
        assert B3 + KEYS + 2 * PAST <= WORDS
        k_pages = [at(o, NPG, P) for o in K_AT]
        k_T = [at(o, PAST) for o in K_AT]
        v_pages = [at(o, NPG, P) for o in V_AT]
        probsT = at(HT, 17, P)
        probs_p = at(B3, 8, SEQ)
        probs_pT = at(HT, 8, 2, P)

        sel = at(FREE, 3, NE, CAP)
        moe_silu = at(FREE + 3 * NE * CAP, 2, CAP)
        moe_ff = at(FREE + 3 * NE * CAP + 2 * CAP, 4, CAP)
        MH = FREE + 3 * NE * CAP + 6 * CAP
        moe_h = at(MH, NE, KD, P)[:, :, :, 0:CAP]
        moe_y = at(MH, NE, D)
        xn3 = at(MH + NE * D, 3, D)
        selT = at(HT, NE, T)
        where[0] = MH + NE * D + 3 * D
        logits, routed, gate, rank = new(3, NE), new(3, NE), new(3, NE), new(3, NE)
        top, first, second = new(3, 8), new(3, NE), new(3, NE)
        top_i = new(3, 8).bitcast(U32)
        top_f = new(3, 8)
        counts, more, before = new(NE), [new(NE) for _ in range(NBLOCK - 1)], new(NE)
        upto = [new(16), new(16)]
        over_e, over_at, over_rank = new(NOVER + 1), new(NOVER), new(3, 1)
        over_i = new(NOVER + 1).bitcast(I32)
        gap, e_gap, g_one, g_two = new(3), new(3), new(3), new(3)
        assert where[0] <= WORDS - 2 * D - 4 * P
        where_part[0] = WORDS - KEPT - 2 * D - 4 * P
        moe_down_parts = new_parts(D)
        moe_ff_parts = [new_parts(P) for _ in range(2)]
        pieces1 = [(5, 512, 512), (0, 1024, 68), (1, 0, 512), (2, 1092, 512), (3, 2116, 512), (4, 1604, 512)]

        PIECES0 = [3, 3, 3, 2, 0, 0]
        PIECE1_AT = {5: 3 * SLOT, 0: 4 * SLOT, 1: 0, 2: SLOT, 3: 2 * SLOT, 4: 3 * SLOT}

        def piece1(p):
            return at(RING + PIECE1_AT[p], KD, 68 if p == 0 else 512)

        def out_piece(h):
            return at(RING + (2 + h) * SLOT, KD, 512)

        RSTD = [1, 5, 6, 9]

        ONCE = {
            "vector": ["dt_abs_ready", "dA_ready", "ua_centred", "var_ready", "ua_normed", "c_pad_ready", "dA_rows_ready",
                       "x_lo_ready", "tok_cleared", "ki_centred", "din_free", "q_packed", "sc_p_taken", "work_s_ready",
                       "rep_ready", "cd_last_ready", "conv_d_ready", "q_blk_ready", "bias_s_ready", "routed_ready", "gap_ready", "over_ready"
                       ],
            "scalar": ["dt_log_ready", "neg_a_ready", "squares_ready", "std_ready", "decs_ready", "x_hi_ready", "qk_squared", "ki_squared", "ws_ready",
                       "e_gap_ready"],
            "tensor": ["paramsT_mm", "dt_mm", "tails_mm", "mean_mm", "var_mm", "inter_mm", "dA_sum_mm", "stateT1_mm",
                       "wsT_mm", "isum_mm", "logits_mm", "rank_mm"],
        }
        done = {engine: 0 for engine in ONCE}

        def reached(name):
            for engine, names in ONCE.items():
                if name in names:
                    return sem(engine + "_reached"), names.index(name) + 1

        def reaches(name):
            for engine, names in ONCE.items():
                if name in names:
                    assert names[done[engine]] == name, name
                    done[engine] += 1
                    return sem(engine + "_reached"), 1

        def while_overflow(eng, body):
            eng.wait_ge(*reached("over_ready"))
            n = eng.value_load(over_i[0:1, NOVER:NOVER + 1], min_val=0, max_val=NOVER)
            with eng.Fori(0, NOVER) as w:
                with eng.If(w < n):
                    body(w)

        block = ctx.enter_context(nc.Block())

        pieces0 = [("e_w_in", 0, 8, 512 * i, 512) for i in range(2)] + \
                  [("e_w_in", 0, 8, 2048 + 512 * i, 512) for i in range(3)] + \
                  [("e_w_in", 0, 8, 1024 + 512 * i, 512) for i in range(2)] + \
                  [("e_w_out", k, n, 512 * h, 512) for h in range(2) for k, n in ((0, 8), (8, 4))]

        used0 = [("val_mm", 4), ("gate_mm", 4), ("xbc_mm", 4), ("xbc_mm", 8), ("xbc_mm", 12), ("z_mm", 6), ("z_mm", 6),
                 ("mix_out_mm", 1), ("mix_out_mm", 4), ("mix_out_mm", 5), ("mix_out_mm", 8)]

        def piece(n):
            return at(RING + (n % 4) * SLOT, 8, 512)

        @block.sync
        def _(sp):
            sp.dma_start(pages.bitcast(I32)[0:1, :], inp["page_table"].rearrange("b j -> (b j)").unsqueeze(0)
                         ).then_inc(sem("const_in"), 16)
            for i, (t, t0, n) in enumerate(TILES):
                src = inp["x_prompt"][0, t0:t0 + n, :] if t < 2 else inp["x_sample"].rearrange("b t d -> (b t) d")
                sp.dma_start(x[0:n, t, :], src).then_inc(sem("x_in"), 16)
            sp.dma_start(const, inp["constants"]).then_inc(sem("const_in"), 16)
            for n, (name, k0, nk, c0, nc_) in enumerate(pieces0):
                if n == 2:
                    sp.wait_ge(sem("params_in"), 16 * 12)
                    sp.wait_ge(sem("states_in"), 48)
                if n >= 4:
                    sp.wait_ge(sem(used0[n - 4][0]), used0[n - 4][1])
                sp.dma_start(piece(n)[:, 0:nk, 0:nc_],
                             inp[name][0, k0 * P:(k0 + nk) * P, c0:c0 + nc_].rearrange("(k p) n -> p k n", p=P)
                             ).then_inc(sem(f"piece{n % 4}"), 16)

            def ff_step(names, e, j):
                s_ = j % (NSLOT0 if e is None else NSLOT)
                g, u, dn = slot(s_)
                if e is not None:
                    j = (j - 3) % NSTEP
                for dst, name, rows_ in ((g, names[0], False), (u, names[1], False), (dn, names[2], True)):
                    w = inp[name][0] if e is None else inp[name][0, e]
                    if e is not None and not isinstance(e, int):
                        w = inp[name][0, ds(e, 1)]
                        src = (w[:, j * FS:(j + 1) * FS, :].rearrange("e (k p) n -> p (e k) n", p=P) if rows_ else
                               w[:, :, j * FS:(j + 1) * FS].rearrange("e (k p) n -> p (e k) n", p=P))
                    else:
                        src = (w[j * FS:(j + 1) * FS, :].rearrange("(k p) n -> p k n", p=P) if rows_ else
                               w[:, j * FS:(j + 1) * FS].rearrange("(k p) n -> p k n", p=P))
                    sp.dma_start(dst, src).then_inc(sem(f"weights{s_}"), 16)

            def load_pages(b, buffers, source, pair=None):
                with sp.Fori(0, NPG // 4) as j4:
                    ids = [sp.value_load(pages.bitcast(I32)[0:1, ds(j4 * 4 + (u + b * NPG), 1)], min_val=0,
                                         max_val=N_POOL - 1) for u in range(4)]
                    for u, page in enumerate(ids):
                        for buffer, name in zip(buffers, source):
                            src = inp[name][0, ds(page, 1)]
                            src = src.rearrange("a p d -> p a d" if name == "cache_kidx" else "a p g d -> p a (g d)")
                            sp.dma_start(buffer[b][:, ds(j4 * 4 + u, 1), :], src).then_inc(sem(f"pages_in{b // 2 if pair is None else pair}"), 16)

            sp.wait_ge(sem("const_in"), 32)
            for j in range(NSTEP):
                if j < NSLOT0:
                    sp.wait_ge(sem("mix_out_mm"), 5 if j == 0 else 8)
                else:
                    sp.wait_ge(sem("ff_used"), j - NSLOT0 + 1)
                ff_step(("e_w_gate", "e_w_up", "e_w_down"), None, j)
                if j >= NSTEP - NB:
                    load_pages(j - (NSTEP - NB), (kidx,), ("cache_kidx",))
            for (p, c0, nc_), (signal, last) in zip(pieces1, (("ff_used", 9), ("ff_used", 9), ("ff_used", 10), ("ff_used", 11),
                                                              ("ff_used", 11), ("tok_mm", 3))):
                sp.wait_ge(sem(signal), last)
                sp.dma_start(piece1(p)[:, :, 0:nc_], inp["o_w_in"][0, :, c0:c0 + nc_].rearrange("(k p) n -> p k n", p=P)
                             ).then_inc(sem(f"piece{p}"), 16)
            for b in range(NB - 1):
                if b == 0:
                    sp.wait_ge(sem("din_mm"), CA)
                elif b == 2:
                    sp.wait_ge(sem("bg_mm"), CA)
                elif b == 4:
                    sp.wait_ge(*reached("isum_mm"))
                    sp.wait_ge(*reached("conv_d_ready"))
                load_pages(b, (k_pages, v_pages), ("cache_k", "cache_v"))
            load_pages(NB - 1, (k_pages,), ("cache_k",))
            sp.wait_ge(sem("pv_mm"), 2)
            load_pages(NB - 1, (v_pages,), ("cache_v",), 0)
            sp.wait_ge(sem("pv_mm"), 4)
            for h in range(2):
                w = inp["o_w_out"][0, :, 512 * h:512 * h + 512]
                dst = out_piece(h)
                for g in range(2):
                    sp.dma_start(dst[64 * g:64 * g + 64, 0:4, :],
                                 w[256 * g:256 * g + 256, :].rearrange("(r d) n -> d r n", d=HD)).then_inc(sem(f"out{h}"), 16)
                sp.dma_start(dst[:, 4:8, :], w[512:, :].rearrange("(k p) n -> p k n", p=P)).then_inc(sem(f"out{h}"), 16)
            moe_w = ("o_we_gate", "o_we_up", "o_we_down")
            for j, signal, last in ((3, "pv_mm", 6), (0, "pv_mm", NB), (1, "out1_mm", 3), (2, "out1_mm", 6)):
                sp.wait_ge(sem(signal), last)
                ff_step(moe_w, 0, j)
            with sp.Fori(0, NE - 1) as e:
                for j in range(4, NSTEP):
                    sp.wait_ge(sem("ff_used"), e * NSTEP + NSTEP + j - 3)
                    ff_step(moe_w, e, j)
                for j, last in ((3, 8), (0, 9), (1, 10), (2, 11)):
                    sp.wait_ge(sem("ff_used"), e * NSTEP + NSTEP + last)
                    ff_step(moe_w, e + 1, j)
            for j in range(4, NSTEP):
                sp.wait_ge(sem("ff_used"), NE * NSTEP + j - 3)
                ff_step(moe_w, NE - 1, j)

            def overflow(w):
                e = sp.value_load(over_i[0:1, ds(w, 1)], min_val=0, max_val=NE - 1)
                sp.wait_ge(sem("ff_down_mm"), downs(w + NE, 0))
                for j in range(NSTEP):
                    if j >= NSLOT:
                        sp.wait_ge(sem("ff_used"), w * NSTEP + NE * NSTEP + NSTEP + j - 3)
                    ff_step(moe_w, e, j)

            while_overflow(sp, overflow)

        @block.gpsimd
        def _(pool):
            def load(dst, src, signal):
                pool.dma_start(dst, src).then_inc(sem(signal), 16)

            pr = param_rows
            load(pr[0:31, 0:512], inp["e_conv_a_w"][0], "params_in")
            load(pr[31:32, 0:512], inp["e_conv_a_b"], "params_in")
            load(pr[32:33, 0:512], inp["e_ln_a_g"], "params_in")
            load(pr[33:34, 0:512], inp["e_ln_a_b"], "params_in")
            load(pr[34:37, 0:512], inp["o_conv_d_w"][0], "params_in")
            load(pr[0:4, 512:2048], inp["e_conv_b_w"][0], "params_in")
            load(pr[4:5, 512:2048], inp["e_conv_b_b"], "params_in")
            for i, n in enumerate(("e_norm_mix", "e_norm_ffn", "e_ssm_norm", "o_norm_mix", "o_norm_ffn")):
                load(pr[i:i + 1, 2048:3072], inp[n], "params_in")
            sa = inp["state_conv_a"][0].rearrange("(h b) t c -> h (b t) c", h=2)
            for h in range(2):
                load(state_a[0:120, h, :], sa[h], "states_in")
            load(state_b[0:24, :], inp["state_conv_b"][0].rearrange("b t c -> (b t) c"), "states_in")
            def rsqrt(dst, src, n, count):
                pool.wait_ge(sem("ms_ready"), count)
                pool.tensor_tensor(dst, src, K["half"][:, 0:1].to_broadcast([P, n]) if n > 3 else K["half"][:, 0:n],
                                   ALU.pow).then_inc(sem("rstd_ready"), 1)

            pool.wait_ge(sem("const_in"), 32)
            rsqrt(rstd, ms, 3, 1)
            for n in rows:
                load(rows[n], inp[n][0].partition_broadcast(P), "rows_in")
            load(w_dt, inp["e_w_in"][0, :, E_IN - NH:E_IN].rearrange("(k p) n -> p k n", p=P), "rows_in")
            load(w_router, inp["o_w_router"][0].rearrange("(k p) n -> p k n", p=P), "rows_in")
            load(out["s_conv_a"][0, :, 0:WA - 1 - NT, :], inp["state_conv_a"][0, :, NT:WA - 1, :], "tails_stored")

            pool.wait_ge(sem("tails_ready"), 8)
            for b in range(NB):
                load(out["s_conv_a"][0, b, WA - 1 - NT:WA - 1, :], tail_us[b * NT:b * NT + NT, :], "tails_stored")
            load(out["p_conv_a"][0, 0], tail_up[0:30, :], "tails_stored")
            load(out["p_conv_b"][0, 0], tail_xp[0:3, :], "tails_stored")
            load(out["s_conv_b"][0].rearrange("b t c -> (b t) c"), tail_xs[0:24, :], "tails_stored")
            ssm_in = inp["state_ssm"][0].rearrange("b (c h) p n -> b (h p) c n", h=2)
            ssm_out = out["s_ssm"][0].rearrange("b (c h) p n -> b (h p) c n", h=2)
            pool.wait_ge(sem("conv_b_ready"), XC)
            for b in range(2):
                load(h_old[b], ssm_in[b], f"h_old{b}")
            for i in range(3):
                rsqrt(grs, gms, 2, 2 + i)
                if i == 1:
                    pool.wait_ge(sem("p_ssm_ready"), 2)
                    load(out["p_ssm"][0, 0].rearrange("(c h) p n -> (h p) c n", h=2), h_new[0], "p_ssm_stored")
                    for b in range(NB):
                        pool.wait_ge(sem("h_new_ready"), KD * (b + 1))
                        load(ssm_out[b], h_new[b % 2], f"h_stored{b % 2}")
                        if b + 2 < NB:
                            pool.wait_ge(sem("h_oldT_mm"), 2 * b + 2)
                            load(h_old[b % 2], ssm_in[b + 2], f"h_old{b % 2}")
            rsqrt(rstd, ms, 3, RSTD[1])
            pool.wait_ge(sem("ff_used"), NSTEP)
            load(state_d[0:16, :], inp["state_conv_d"][0].rearrange("b t c -> (b t) c"), "states_in")
            rsqrt(rstd, ms, 3, 6)
            rsqrt(ki_rs, ki_ms, 3, 7)
            rsqrt(qk_rs, qk_ms, 30, 8)
            pool.wait_ge(sem("rot_ready"), 2)
            for i, t0, n in TILES:
                for a, b, name in ((512, 640, "k"), (640, 768, "v"), (1024, 1088, "kidx")):
                    dst = (out["p_" + name][0, 0, t0:t0 + n] if i < 2 else
                           out["s_" + name][0].rearrange("b t ... -> (b t) ...") if name == "kidx" else
                           out["s_" + name][0].rearrange("b t g d -> (b t) g d"))
                    if name != "kidx":
                        dst = dst.rearrange("t g d -> t (g d)")
                    load(dst, tok[0:n, i, a:b], "kv_stored")
            pool.wait_ge(*reached("conv_d_ready"))
            pool.wait_ge(sem("tails1_mm"), 2)
            for b in range(NB):
                load(v_new[0:NT, b, :], v_tok[b * NT:b * NT + NT, 2, :], "v_new_in")
            pool.wait_ge(sem("tails1_ready"), 2)
            load(out["p_conv_d"][0, 0], tail_dp[0:2, :], "tails1_stored")
            load(out["s_conv_d"][0].rearrange("b t c -> (b t) c"), tail_ds[0:16, :], "tails1_stored")
            rsqrt(rstd, ms, 3, 9)
            pool.wait_ge(sem("y_out_ready"), 6)
            while_overflow(pool, lambda w: pool.wait_ge(sem("y_out_ready"), 6 * w + 12))
            load(out["y_prompt"][0].rearrange("(a p) d -> p a d", p=P), x[:, 0:2, :], "y_stored")
            load(out["y_sample"].rearrange("b t d -> (b t) d"), x[0:64, 2, :], "y_stored")
            pool.wait_ge(sem("y_stored"), 32)
            pool.wait_ge(sem("h_stored0"), 64)
            pool.wait_ge(sem("h_stored1"), 64)
            pool.wait_ge(sem("tails_stored"), 16 * 12)
            pool.wait_ge(sem("kv_stored"), 16 * 9)
            pool.wait_ge(sem("tails1_stored"), 32)

        @block.scalar
        def _(act):
            own = Own(act, sem("act_step"))

            def norm(k, xn=xn):
                for i, t0, n in TILES:
                    act.activation(xn[0:n, i, :], x[0:n, i, :], ACT.Square,
                                   accum_out=ss[0:n, i:i + 1]).then_inc(sem("ss_ready"), 1)

            def copy(dst, src, signal):
                act.activation(dst, src, ACT.Copy).then_inc(sem(signal), 1)

            act.wait_ge(sem("x_in"), 48)
            act.wait_ge(sem("cleared"), 2)
            norm(0)
            act.wait_ge(*reached("paramsT_mm"))
            copy(vecA.rearrange("p a b -> p (a b)"), bank(6)[:, 0:148], "params_ready")
            copy(vecB.rearrange("p a b -> p (a b)"), bank(6)[:, 148:208], "params_ready")
            copy(vecD.rearrange("p a b -> p (a b)"), bank(6)[:, 208:248], "params_ready")
            act.wait_ge(sem("stateT_mm"), 1)
            copy(xbc_s[:, :, :, 0:3], bank(7)[:, 0:288].rearrange("p (c b t) -> p c b t", c=XC, b=NB), "halo_ready")
            for h in range(2):
                act.wait_ge(sem("stateT_mm"), 2 + h)
                for c in range(CA):
                    copy(u_s[:, c, 4 * h:4 * h + 4, 0:30],
                         bank(6 + h)[:, 120 * c:120 * c + 120].rearrange("p (b t) -> p b t", b=4), "halo_ready")
            for c in range(CA):
                act.wait_ge(sem("gate_mm"), c + 1)
                act.activation(ua[:, c, :], bank(4 + c)[:, 0:T], ACT.Sigmoid).then_inc(sem("sig_ready"), 1)
            for c in range(XC):
                act.wait_ge(sem("xbc_mm"), c + 1)
                act.activation(xbc_p[:, c, 3:], bank(c % 8)[:, 0:SEQ], ACT.Copy)
                copy(xbc_s[:, c, :, 3:], bank(c % 8)[:, SEQ:T].rearrange("p (b t) -> p b t", b=NB), "xbc_ready")
            act.wait_ge(*reached("dt_mm"))
            for i, t0, n in TILES:
                copy(raw_dt[0:n, i, :], bank(4)[0:n, 16 * i:16 * i + 16], "dt_raw_ready")
            act.wait_ge(sem("u_ready"), CA)
            act.wait_ge(sem("xbc_ready"), XC)
            copy(u_last.rearrange("p c (b t) -> p c b t", b=NB), u_s[:, :, :, 30:38], "last_ready")
            copy(xbc_last.rearrange("p c (b t) -> p c b t", b=NB), xbc_s[:, :, :, 8:11], "last_ready")
            for g in range(6):
                i, h = g // 2, g % 2
                n = TILES[i][2]
                act.wait_ge(sem("z_mm"), g + 1)
                act.activation(z[0:n, i, 512 * h:512 * h + 512], bank((13 + g) % 8)[0:n, :],
                               ACT.Silu).then_inc(sem("z_ready"), 1)
            act.wait_ge(*reached("tails_mm"))
            copy(tail_us[0:64, :], bank(3)[0:64, :], "tails_ready")
            copy(tail_up[0:30, :], bank(4)[0:30, :], "tails_ready")
            for j in range(3):
                copy(tail_xp[0:3, 512 * j:512 * j + 512], bank(5 + j)[0:3, :], "tails_ready")
                copy(tail_xs[0:24, 512 * j:512 * j + 512], bank(j)[0:24, :], "tails_ready")
            act.wait_ge(*reached("dt_abs_ready"))
            own.link(act.activation(dt_log, dt_abs, ACT.Exp, scale=-1.0))
            act.activation(dt_log, dt_log, ACT.Ln, bias=1.0).then_inc(*reaches("dt_log_ready"))
            act.wait_ge(sem("rows_in"), 16 * 10)
            own.link(act.activation(neg_a, rows["e_a_log"], ACT.Exp))
            act.activation(neg_a, neg_a, ACT.Copy, scale=-1.0).then_inc(*reaches("neg_a_ready"))
            for c in range(XC):
                act.wait_ge(sem("conv_b_ready"), c + 1)
                act.activation(xbcT[:, c, :], xbcT[:, c, :], ACT.Silu).then_inc(sem("xbcT_ready"), 1)
            act.wait_ge(*reached("ua_centred"))
            act.activation(squares, ua, ACT.Square).then_inc(*reaches("squares_ready"))
            act.wait_ge(*reached("var_ready"))
            act.activation(small[2], small[1], ACT.Sqrt).then_inc(*reaches("std_ready"))
            act.wait_ge(*reached("ua_normed"))
            for c in range(CA):
                act.activation(mixT[:, c, :], ua[:, c, :], ACT.Silu, scale=vecA[:, c, 32:33],
                               bias=vecA[:, c, 33:34]).then_inc(sem("ya_ready"), 1)
            act.wait_ge(sem("tails_stored"), 16 * 12)
            for g in range(9):
                i, k = g // 3, g % 3
                n = TILES[i][2]
                act.wait_ge(sem("xT_mm"), g + 1)
                src = bank([5, 6, 7, 0, 1, 2][g % 6])
                if k < 2:
                    copy(x_tok[0:n, i, 512 * k:512 * k + 512], src[0:n, :], "x_tok_ready")
                else:
                    copy(b_tok[0:n, i, :], src[0:n, 0:256], "x_tok_ready")
            for i, t0, n in TILES:
                act.wait_ge(sem("cumT_ready"), i + 1)
                own.mark(act.activation(e_cum[0:n], bank(0)[0:n, 0:16], ACT.Exp))
                own.mark(act.activation(w_end[0:n], w_arg[0:n], ACT.Exp))
                act.activation(e_last[0:n], bank(0)[0:n, 16:32], ACT.Exp).then_inc(sem("scan_exps_ready"), 1)
                for q in range(4):
                    act.wait_ge(sem("arow_mm"), 4 * i + q + 1)
                    for h in range(4 * q, 4 * q + 4):
                        ins = act.activation(decay[0:n, h, 0:n], bank(2 + q)[0:n, (h % 4) * n:(h % 4) * n + n],
                                             ACT.Exp, bias=negcum[0:n, h:h + 1])
                    ins.then_inc(sem("decay_ready"), 1)
                if i == 1:
                    for g in range(2):
                        act.wait_ge(sem("p_ssmT_mm"), g + 1)
                        copy(h_new[0][:, 4 * g:4 * g + 4, :], bank(4 + g, 4, P), "p_ssm_ready")
                if i == 2:
                    act.wait_ge(*reached("dA_sum_mm"))
                    act.activation(decs, bank(0)[:, 0:64].rearrange("p (c b) -> p c b", c=KD),
                                   ACT.Exp).then_inc(*reaches("decs_ready"))
                    for b in range(NB):
                        if b == 0:
                            act.wait_ge(sem("p_ssmT_mm"), 2)
                        for g in range(2):
                            act.wait_ge(sem("h_oldT_mm"), 2 * b + g + 1)
                            if b:
                                act.wait_ge(sem("inter_acc"), 2 * b - 1 + g)
                            copy(h_oldT[:, 512 * g:512 * g + 512], bank(4 + g), "h_oldT_ready")
                act.wait_ge(sem("y_ready"), i + 1)
                for g in range(2):
                    act.activation(xdt[0:n, 8 * g:8 * g + 8, :], y[0:n, 8 * g:8 * g + 8, :], ACT.Square,
                                   accum_out=gs[0:n, g:g + 1]).then_inc(sem("gs_ready"), 1)
            act.wait_ge(sem("x_ready"), 6)
            norm(1)

            def silu(dst, src, gate_mm, done, value):
                act.wait_ge(sem(gate_mm), value)
                act.activation(dst, src, ACT.Silu).then_inc(sem(done), 1)

            act.wait_ge(sem("hT_ready"), 12)
            for b in range(2):
                act.wait_ge(sem(f"h_stored{b}"), 64)
            act.activation(x_parts[0], hT, ACT.Copy).then_inc(*reaches("x_hi_ready"))

            def split_hi(kind, m):
                if kind == "gu":
                    if m % 2 == 0:
                        act.wait_ge(sem(f"weights{m // 2 % NSLOT0}"), 48 * (m // 2 // NSLOT0 + 1))
                    if m >= 2:
                        act.wait_ge(sem("ff_up_mm"), m - 1)
                elif m >= 2:
                    act.wait_ge(sem("ff_down_mm"), m - 1)
                for src, upper, _ in to_split(kind, m):
                    ins = act.activation(upper, src, ACT.Copy)
                ins.then_inc(sem("split_hi"), 1)

            for kind, m in SPLITS[:3]:
                split_hi(kind, m)
            for m in range(CHUNKS):
                if m >= 2:
                    act.wait_ge(sem("ff_ready"), m - 1)
                silu(silu_t[:, m % 2, :], bank(6)[:, 0:T], "ff_gate_mm", "ff_silu", m + 1)
                if m + 2 < CHUNKS:
                    split_hi("gu", m + 2)
                if m + 1 < CHUNKS:
                    split_hi("down", m + 1)
            act.wait_ge(sem("x_ready"), 12)
            norm(2)
            act.wait_ge(*reached("tok_cleared"))
            for g in range(7):
                act.wait_ge(sem("tok_mm"), min(g + 1, 4) if g < 4 else g + 1)
                if g < 3:
                    n = TILES[g][2]
                    copy(tok[0:n, g, 512:1024], bank(g)[0:n, :], "tok_ready")
                elif g == 3:
                    copy(tok[:, 0:2, 1024:1092], bank(3, 2, 68), "tok_ready")
                    copy(tok[0:NS, 2, 1024:1092], bank(3)[0:NS, 136:204], "tok_ready")
                else:
                    n = TILES[g - 4][2]
                    copy(tok[0:n, g - 4, 0:512], bank(g)[0:n, :], "tok_ready")
            act.wait_ge(sem("tok_ready"), 8)
            act.activation(squares1, tok[:, :, 0:640], ACT.Square).then_inc(*reaches("qk_squared"))
            act.wait_ge(*reached("ki_centred"))
            act.activation(rope_t[0].rearrange("p a b c -> p a (b c)")[:, :, 0:64], tok[:, :, 1024:1088],
                           ACT.Square).then_inc(*reaches("ki_squared"))
            copy(v_tok, tok[:, :, 640:768], "v_ready")
            act.activation(w_idx, tok[:, :, 1088:1092], ACT.Copy,
                           scale=4 ** -0.5 * HD ** -0.5).then_inc(sem("v_ready"), 1)
            for g in range(9):
                i, k = g // 3, g % 3
                t0, n = TILES[i][1:]
                act.wait_ge(sem("rotT_mm"), g + 1)
                dst = (qT, qiT, kkT)[k]
                m = 4 if k < 2 else 2
                copy(dst[:, :, t0:t0 + n], bank(4 + k, m, n), "rotT_ready")
            act.wait_ge(*reached("stateT1_mm"))
            copy(cd_s[:, :, :, 0:2], bank(7)[:, 0:64].rearrange("p (c b t) -> p c b t", c=CA, b=NB), "halo1_ready")
            act.wait_ge(*reached("din_free"))
            for c in range(CA):
                act.wait_ge(sem("din_mm"), c + 1)
                act.activation(cd_p[:, c, 2:], bank(c)[:, 0:SEQ], ACT.Copy)
                copy(cd_s[:, c, :, 2:], bank(c)[:, SEQ:T].rearrange("p (b t) -> p b t", b=NB), "din_ready")
            for i in range(2):
                act.wait_ge(sem("idx_p_mm"), i + 1)
                if i == 0:
                    act.wait_ge(sem("kv_stored"), 16 * 9)
                else:
                    act.wait_ge(sem("sc_p_ready"), 1)
                act.activation(relu_p.rearrange("p a b -> p (a b)"), psum[:, 1024 * i:1024 * i + 1024],
                               ACT.Relu).then_inc(sem("relu_p_ready"), 1)
            for b in range(NB):
                for g in range(2):
                    act.wait_ge(sem("kidxT_mm"), 2 * b + g + 1)
                    if b >= 2:
                        act.wait_ge(sem("dots_mm"), b - 1)
                    copy(kidxT[b % 2][:, 4 * g:4 * g + 4, :], bank(5 + g, 4, P), "kidxT_ready")
                if b % 4 == 3:
                    act.wait_ge(sem("dots_mm"), b + 1)
                    if b == 3:
                        act.wait_ge(*reached("sc_p_taken"))
                    for odd in range(2):
                        act.activation(relu_s[b // 4][:, 0:PAST].rearrange("p (a o k) -> p a o k", o=2, k=P)[:, :, odd, :],
                                       psum[:, 1024 * odd:1024 * odd + 1024].rearrange("p (a k) -> p a k", k=P), ACT.Relu)
                    act.activation(relu_s[b // 4][:, PAST:], bank(4)[:, 0:NT], ACT.Relu).then_inc(sem("relu_s_ready"), 1)
            act.wait_ge(*reached("wsT_mm"))
            act.activation(ws, bank(7, 2, NS), ACT.Copy).then_inc(*reaches("ws_ready"))
            act.wait_ge(sem("tails1_mm"), 2)
            copy(tail_dp[0:2, :], bank(7)[0:2, :], "tails1_ready")
            copy(tail_ds[0:16, :], bank(4)[0:16, :], "tails1_ready")
            for i in range(2):
                act.wait_ge(sem("nmx_p_ready"), i + 1)
                for h in range(8):
                    ins = act.activation(probs_p[:, h, :], probs_p[:, h, :], ACT.Exp, bias=nmx[:, h:h + 1],
                                         scale=HD ** -0.5, accum_out=sums[:, h:h + 1])
                ins.then_inc(sem("exp_p_ready"), 1)
                act.wait_ge(sem("rsum_p_ready"), i + 1)
                for h in range(8):
                    ins = act.activation(probs_p[:, h, :], probs_p[:, h, :], ACT.Copy, scale=rsum[:, h:h + 1])
                ins.then_inc(sem("probs_p_ready"), 1)
                for g in range(4):
                    act.wait_ge(sem("pt_prompt_mm"), 4 * i + g + 1)
                    copy(probs_pT[:, 2 * g:2 * g + 2], bank(4 + g % 2, 2, 2, P), "pt_prompt_ready")
                act.wait_ge(sem("pv_p_mm"), i + 1)
                copy(mix1T[:, 0:4, P * i:P * i + P], bank(7, 4, P), "att_ready")
            def turn_keys(rows_):
                for b in rows_:
                    for g in range(4):
                        act.wait_ge(sem("kT_mm"), 4 * b + g + 1)
                        copy(k_T[b][:, 512 * g:512 * g + 512], bank(5 + g % 2), "kT_ready")

            turn_keys(range(6))
            act.wait_ge(sem("tails1_stored"), 32)
            for q in range(NB // 2):
                act.wait_ge(sem("nmx_ready"), q + 1)
                if q:
                    act.wait_ge(sem("pt_mm"), 5 * q)
                act.activation(probs, psum[:, 0:KEYS], ACT.Exp, bias=nmx[:, 0:1], scale=HD ** -0.5,
                               accum_out=sums[:, 0:1]).then_inc(sem("exp_ready"), 1)
                if q:
                    act.wait_ge(sem("pv_mm"), 2 * q)
                for g in range(5):
                    act.wait_ge(sem("pt_mm"), 5 * q + g + 1)
                    if g < 4:
                        copy(probsT[:, 4 * g:4 * g + 4, :], bank(5 + g % 2, 4, P), "pt_ready")
                    else:
                        copy(probsT[0:NT, 16, :], bank(5)[0:NT, 0:P], "pt_ready")
                if q == 1:
                    turn_keys((6, 7))
            act.wait_ge(sem("x_ready"), 18)
            norm(3, xn3)
            act.wait_ge(*reached("gap_ready"))
            act.activation(e_gap, gap, ACT.Exp).then_inc(*reaches("e_gap_ready"))
            for e in range(NE):
                act.wait_ge(sem("selT_mm"), e + 1)
                copy(selT[0:CAP, e, :], bank(4 + e % 2)[0:CAP, 0:T], "selT_ready")

            def expert(n, y_out):
                for m in range(2 * NSTEP):
                    act.wait_ge(sem("ff_ready"), n * 2 * NSTEP + 2 * NSTEP + m - 1)
                    silu(moe_silu[:, m % 2, :], bank(2 + 2 * (m % 2))[:, 0:CAP], "ff_gate_mm", "ff_silu",
                         n * 2 * NSTEP + 2 * NSTEP + m + 1)
                    if m % 2 == 0:
                        act.wait_ge(sem(f"weights{m // 2 % NSLOT}"), arrivals(n, m // 2))
                    act.wait_ge(sem("ff_down_mm"), downs(n, m))
                    act.activation(moe_down_parts[0], slot(m // 2 % NSLOT)[2][:, m % 2, :], ACT.Copy
                                   ).then_inc(sem("split_hi"), 1)
                act.wait_ge(sem("ff_down_mm"), downs(n, CHUNKS))
                act.activation(y_out, bank(1)[0:CAP].unsqueeze(1), ACT.Copy).then_inc(sem("moe_y1"), 1)

            with act.Fori(0, NE) as e:
                expert(e, moe_y[0:CAP, ds(e, 1), 512:1024])

            def overflow(w):
                n = w + NE
                act.wait_ge(sem("selT_mm"), n + 1)
                copy(selT[0:CAP, 0, :], bank(4)[0:CAP, 0:T], "selT_ready")
                expert(n, moe_y[0:CAP, 1:2, 512:1024])

            while_overflow(act, overflow)

        @block.tensor
        def _(pe):
            def mm(dst, w, m, start, stop):
                return pe.matmul(dst, w, m, start=start, stop=stop)

            def norm(k, xn=xn):
                for i, t0, n in TILES:
                    pe.wait_ge(sem("xn_ready"), 3 * k + i + 1)
                    for g in range(2):
                        for c in range(4):
                            ins = pe.transpose(bank(2 * i + g, 4, n)[:, c, :],
                                               xn[0:n, i, (4 * g + c) * P:(4 * g + c + 1) * P], ident[0:n, 0:n])
                        ins.then_inc(sem("xnT_mm"), 1)

            pe.wait_ge(sem("const_in"), 32)
            pe.wait_ge(sem("params_in"), 16 * 12)
            for c in range(CA):
                pe.transpose(bank(6)[:, 37 * c:37 * c + 37], param_rows[0:37, c * P:(c + 1) * P], ident[0:37, 0:37])
            for c in range(XC):
                pe.transpose(bank(6)[:, 148 + 5 * c:153 + 5 * c], param_rows[0:5, 512 + c * P:512 + (c + 1) * P],
                             ident[0:5, 0:5])
            for c in range(KD):
                ins = pe.transpose(bank(6)[:, 208 + 5 * c:213 + 5 * c],
                                   param_rows[0:5, 2048 + c * P:2048 + (c + 1) * P], ident[0:5, 0:5])
            ins.then_inc(*reaches("paramsT_mm"))
            pe.wait_ge(sem("states_in"), 48)
            for c in range(XC):
                ins = pe.transpose(bank(7)[:, 24 * c:24 * c + 24], state_b[0:24, c * P:(c + 1) * P], ident[0:24, 0:24])
            ins.then_inc(sem("stateT_mm"), 1)
            pe.wait_ge(sem("params_ready"), 3)
            pe.wait_ge(sem("halo_ready"), 1)
            for h in range(2):
                for c in range(CA):
                    ins = pe.transpose(bank(6 + h)[:, 120 * c:120 * c + 120], state_a[0:120, h, c * P:(c + 1) * P],
                                       ident[0:120, 0:120])
                ins.then_inc(sem("stateT_mm"), 1)
            norm(0)
            pe.wait_ge(sem("hT_ready"), 6)
            pe.wait_ge(sem("halo_ready"), 9)

            def arrived(n):
                pe.wait_ge(sem(f"piece{n % 4}"), 16 * (n // 4 + 1))

            for n, signal in ((0, "val_mm"), (1, "gate_mm")):
                arrived(n)
                for c in range(CA):
                    for k in range(KD):
                        ins = mm(bank(4 * n + c)[:, 0:T], piece(n)[:, k, c * P:(c + 1) * P], hT[:, k, :], k == 0, k == KD - 1)
                    ins.then_inc(sem(signal), 1)
            for c in range(XC):
                n = 2 + c // 4
                if c % 4 == 0:
                    arrived(n)
                if c < 4:
                    pe.wait_ge(sem("u_ready"), c + 1)
                elif c < 8:
                    pe.wait_ge(sem("sig_ready"), c - 3)
                else:
                    pe.wait_ge(sem("xbc_ready"), c - 7)
                for k in range(KD):
                    ins = mm(bank(c % 8)[:, 0:T], piece(n)[:, k, (c % 4) * P:(c % 4 + 1) * P], hT[:, k, :], k == 0, k == KD - 1)
                ins.then_inc(sem("xbc_mm"), 1)
            pe.wait_ge(sem("xbc_ready"), 5)
            pe.wait_ge(sem("rows_in"), 16 * 10)
            for i, t0, n in TILES:
                for k in range(KD):
                    ins = mm(bank(4)[0:n, 16 * i:16 * i + 16], hT[:, k, t0:t0 + n], w_dt[:, k, :], k == 0, k == KD - 1)
            ins.then_inc(*reaches("dt_mm"))
            arrived(5)
            arrived(6)
            for g in range(6):
                i, h = g // 2, g % 2
                t0, n = TILES[i][1:]
                pe.wait_ge(sem("xbc_ready"), min(XC, 6 + g))
                for k in range(KD):
                    ins = mm(bank((13 + g) % 8)[0:n, :], hT[:, k, t0:t0 + n], piece(5 + h)[:, k, :], k == 0, k == KD - 1)
                ins.then_inc(sem("z_mm"), 1)
            pe.wait_ge(sem("z_ready"), 6)
            pe.wait_ge(sem("xbc_ready"), XC)
            pe.wait_ge(sem("dt_raw_ready"), 3)
            pe.wait_ge(sem("last_ready"), 2)
            for c in range(CA):
                cc = slice(c * P, (c + 1) * P)
                pe.transpose(bank(3)[0:64, cc], u_last[:, c, :], ident)
                pe.transpose(bank(4)[0:30, cc], u_p[:, c, 256:286], ident)
            for c in range(XC):
                cc = slice((c % 4) * P, (c % 4 + 1) * P)
                pe.transpose(bank(5 + c // 4)[0:3, cc], xbc_p[:, c, 256:259], ident)
                ins = pe.transpose(bank(c // 4)[0:24, cc], xbc_last[:, c, :], ident)
            ins.then_inc(*reaches("tails_mm"))
            pe.wait_ge(sem("ua_ready"), CA)
            pe.wait_ge(sem("tails_ready"), 8)
            for c in range(CA):
                ins = mm(bank(3)[:, 0:T], ones, ua[:, c, :], c == 0, c == CA - 1)
            ins.then_inc(*reaches("mean_mm"))
            pe.wait_ge(*reached("squares_ready"))
            for c in range(CA):
                ins = mm(bank(4)[:, 0:T], ones, squares[:, c, :], c == 0, c == CA - 1)
            ins.then_inc(*reaches("var_mm"))
            pe.wait_ge(sem("xbcT_ready"), XC)
            for g in range(9):
                i, k = g // 3, g % 3
                t0, n = TILES[i][1:]
                if g >= 6:
                    pe.wait_ge(sem("x_tok_ready"), g - 5)
                for c in range(4 if k < 2 else 2):
                    ins = pe.transpose(bank([5, 6, 7, 0, 1, 2][g % 6])[0:n, c * P:(c + 1) * P],
                                       xbcT[:, 4 * k + c, t0:t0 + n], ident)
                ins.then_inc(sem("xT_mm"), 1)
            pe.wait_ge(sem("x_tok_ready"), 9)
            pe.wait_ge(*reached("dA_ready"))
            pe.wait_ge(*reached("ua_normed"))
            for i, t0, n in TILES:
                tri = K["tri_p"] if i < 2 else K["tri_s"][0:64, :]
                last = ones if i < 2 else K["last_s"][0:64, :]
                mask = K["mask_p"] if i < 2 else K["mask_s"][0:64, :]
                if i:
                    pe.wait_ge(sem("mixT_ready"), 2 * i)
                mm(bank(0)[0:n, 0:16], tri, dA[0:n, i, :], True, True)
                mm(bank(0)[0:n, 16:32], last, dA[0:n, i, :], True, True)
                mm(bank(0)[0:16, 32:32 + n], dA[0:n, i, :], tri, True, True).then_inc(sem("cum_mm"), 1)
                for g in range(NG):
                    ins = mm(bank(1, 2, n)[0:n, g, :], xbcT[:, 8 + g, t0:t0 + n], xbcT[:, 10 + g, t0:t0 + n], True, True)
                ins.then_inc(sem("cb_mm"), 1)
                pe.wait_ge(sem("cumT_ready"), i + 1)
                if i == 1:
                    pe.wait_ge(sem("p_state_ready"), 2)
                if i == 2:
                    pe.wait_ge(sem("p_ssm_ready"), 2)
                for q in range(4):
                    v = bank(2 + q, 4, n)[0:n]
                    for h in range(4):
                        pe.matmul(v[:, h, :], head_row[0:16, 4 * q + h, 0:n], cumT[0:16, 0:n], start=(h == 0),
                                  stop=False, skip_group_check=True)
                    ins = pe.matmul(v, ident[0:n, 0:n], mask.unsqueeze(1).to_broadcast([n, 4, n]), start=False,
                                    stop=True, skip_group_check=True)
                    ins.then_inc(sem("arow_mm"), 1)
                pe.wait_ge(sem("wts_ready"), 2 * i + 2)
                pe.wait_ge(sem("xdt_ready"), i + 1)
                if i:
                    pe.wait_ge(sem("y_ready"), i)
                for h in range(NH):
                    ins = mm(bank(6 + h // 8)[0:n, (h % 8) * HP:(h % 8 + 1) * HP], decay[0:n, h, 0:n], xdt[0:n, h, :], True, True)
                ins.then_inc(sem("y_mm"), 1)
                pe.wait_ge(sem("decay_ready"), 4 * i + 4)
                if i == 1:
                    for g in range(NG):
                        ins = mm(bank(2 + g), xbcT[:, 10 + g, t0:t0 + n], p_state[:, 512 * g:512 * g + 512], True, True)
                    ins.then_inc(*reaches("inter_mm"))
                if i < 2:
                    pe.wait_ge(sem("xw_ready"), i + 1)
                    for g in range(NG):
                        ins = mm(bank(4 + g), b_tok[0:n, i, g * NST:(g + 1) * NST],
                                 xw[0:n, 8 * g:8 * g + 8, :], True, True)
                    ins.then_inc(sem("state_mm"), 1)
                if i == 1:
                    pe.wait_ge(sem("p_state_ready"), 4)
                    for g in range(2):
                        for c in range(4):
                            ins = pe.transpose(bank(4 + g, 4, P)[:, c, :], p_state[:, (4 * g + c) * P:(4 * g + c + 1) * P], ident)
                        ins.then_inc(sem("p_ssmT_mm"), 1)
                if i == 2:
                    pe.wait_ge(*reached("dA_rows_ready"))
                    pe.wait_ge(sem("scan_exps_ready"), 3)
                    for c in range(KD):
                        ins = mm(bank(0)[:, 8 * c:8 * c + 8], dA_rows[0:n, c * P:(c + 1) * P], K["batch"][0:n, :], True, True)
                    ins.then_inc(*reaches("dA_sum_mm"))
                    pe.wait_ge(*reached("decs_ready"))
                    for b in range(NB):
                        pe.wait_ge(sem(f"h_old{b % 2}"), 16 * (b // 2 + 1))
                        for g in range(2):
                            if b:
                                pe.wait_ge(sem("h_oldT_ready"), 2 * b - 1 + g)
                            else:
                                pe.wait_ge(sem("p_ssm_ready"), 2)
                            for c in range(4):
                                ins = pe.transpose(bank(4 + g, 4, P)[:, c, :], h_old[b % 2][:, 4 * g + c, :], ident)
                            ins.then_inc(sem("h_oldT_mm"), 1)
                        pe.wait_ge(*reached("c_pad_ready"))
                        for g in range(NG):
                            pe.wait_ge(sem("h_oldT_ready"), 2 * b + g + 1)
                            pe.matmul(bank(2 + g)[0:n, :], c_pad[:, g, b, :], h_oldT[:, 512 * g:512 * g + 512],
                                      start=(b == 0), stop=(b == NB - 1), skip_group_check=True
                                      ).then_inc(sem("inter_acc"), 1)
                        pe.wait_ge(sem("b_one_ready"), b + 1)
                        pe.wait_ge(sem("xw_ready"), 3)
                        if b:
                            pe.wait_ge(sem("h_new_ready"), KD * b)
                        for c in range(KD):
                            ins = mm(bank(c // 4, 4, P)[:, c % 4, :], xw[0:n, 2 * c:2 * c + 2, :],
                                     b_one[0:n, b % 2, (c // 4) * NST:(c // 4 + 1) * NST], True, True)
                        ins.then_inc(sem("h_add_mm"), 1)
                pe.wait_ge(sem("yn_ready"), i + 1)
                pe.wait_ge(sem("wts_ready"), 2 * i + 2)
                if i == 2:
                    pe.wait_ge(sem("h_new_ready"), KD * NB)
                for g in range(2):
                    for c in range(4):
                        ins = pe.transpose(bank(g, 4, n)[:, c, :], y[0:n, 8 * g + 2 * c:8 * g + 2 * c + 2, :], ident[0:n, 0:n])
                    ins.then_inc(sem("yT_mm"), 1)
            pe.wait_ge(sem("mixT_ready"), 6)
            pe.wait_ge(sem("ya_ready"), CA)
            for h in range(2):
                for q in range(2):
                    n_ = 7 + 2 * h + q
                    arrived(n_)
                    for i, t0, n in TILES:
                        for k in range(8 if q == 0 else 4):
                            ins = mm(bank(3 * h + i)[0:n, :], mixT[:, 8 * q + k, t0:t0 + n], piece(n_)[:, k, :],
                                     q == 0 and k == 0, q == 1 and k == 3)
                        if q or i == 2:
                            ins.then_inc(sem("mix_out_mm"), 1)
            norm(1)
            pe.wait_ge(*reached("x_lo_ready"))

            def three(dst, w, a, start, stop):
                mm(dst, w[0], a[0], start, False)
                mm(dst, w[0], a[1], False, False)
                return mm(dst, w[1], a[0], False, stop)

            for m in range(CHUNKS + 1):
                if m < CHUNKS:
                    pe.wait_ge(sem("split_lo"), split_at("gu", m))
                    for i, b_, signal in ((0, 6, "ff_gate_mm"), (1, 7, "ff_up_mm")):
                        if m:
                            pe.wait_ge(sem("ff_silu" if b_ == 6 else "ff_ready"), m)
                        for k in range(KD):
                            ins = three(bank(b_)[:, 0:T], [v[:, i, k, :] for v in gu_parts[m % 2]],
                                        [v[:, k, :] for v in x_parts], k == 0, k == KD - 1)
                        ins.then_inc(sem(signal), 1)
                if m:
                    c = m - 1
                    pe.wait_ge(sem("ff_ready"), m)
                    pe.wait_ge(sem("split_lo"), split_at("down", c))
                    for i, t0, n in TILES:
                        for h in range(2):
                            ins = three(bank(2 * i + h)[0:n, :], [v[:, t0:t0 + n] for v in ff_parts[c % 2]],
                                        [v[:, 512 * h:512 * h + 512] for v in down_parts[c % 2]], c == 0, c == CHUNKS - 1)
                    ins.then_inc(sem("ff_down_mm"), 1)
            norm(2)
            pe.wait_ge(sem("hT_ready"), 18)
            pe.wait_ge(sem("states_in"), 64)
            for c in range(CA):
                ins = pe.transpose(bank(7)[:, 16 * c:16 * c + 16], state_d[0:16, c * P:(c + 1) * P], ident[0:16, 0:16])
            ins.then_inc(*reaches("stateT1_mm"))
            for (p, c0, nc_), b0, step in zip(pieces1[:3], (0, 3, 4), (1, 0, 1)):
                pe.wait_ge(sem(f"piece{p}"), 16 * PIECES0[p] + 16)
                for i, t0, n in TILES:
                    dst = bank(b0 + i * step)[0:n, 0:512] if step else bank(3)[0:n, 68 * i:68 * i + 68]
                    for k in range(KD):
                        ins = mm(dst, hT[:, k, t0:t0 + n], piece1(p)[:, k, 0:nc_], k == 0, k == KD - 1)
                    if step or i == 2:
                        ins.then_inc(sem("tok_mm"), 1)
            def channels(p, b0, signal, free):
                pe.wait_ge(sem(f"piece{p}"), 16 * PIECES0[p] + 16)
                for c in range(CA):
                    if free:
                        pe.wait_ge(*free(c))
                    for k in range(KD):
                        ins = mm(bank(b0 + c)[:, 0:T], piece1(p)[:, k, c * P:(c + 1) * P], hT[:, k, :], k == 0, k == KD - 1)
                    ins.then_inc(sem(signal), 1)

            channels(2, 0, "din_mm", lambda c: (sem("tok_ready"), (1, 2, 3, 5)[c]))
            pe.wait_ge(sem("tok_ready"), 8)
            pe.wait_ge(sem("rot_ready"), 3)
            for g in range(9):
                i, k = g // 3, g % 3
                n = TILES[i][2]
                if g >= 3:
                    pe.wait_ge(sem("rotT_ready"), g - 2)
                for r in range(4 if k < 2 else 2):
                    src = (q_tok[0:n, i, r, :] if k == 0 else qi_tok[0:n, i, r, :] if k == 1 else
                           tok[0:n, i, 512:640] if r == 0 else ki_tok[0:n, i, :])
                    ins = pe.transpose(bank(4 + k)[:, r * n:(r + 1) * n], src, ident[0:n, 0:n])
                ins.then_inc(sem("rotT_mm"), 1)
            pe.wait_ge(sem("rotT_ready"), 9)
            pe.wait_ge(sem("din_ready"), CA)
            for i in range(2):
                for h in range(4):
                    ins = mm(bank(2 * i + h // 2)[:, 256 * (h % 2):256 * (h % 2) + 256], qiT[0:64, h, P * i:P * i + P],
                             kkT[0:64, 1, 0:SEQ], True, True)
                ins.then_inc(sem("idx_p_mm"), 1)
            pe.wait_ge(*reached("q_packed"))
            pe.wait_ge(sem("relu_p_ready"), 2)
            for b in range(NB):
                pe.wait_ge(sem(f"pages_in{b // 2}"), 2 * 16 * NPG)
                for g in range(2):
                    if b:
                        pe.wait_ge(sem("kidxT_ready"), 2 * b - 1 + g)
                    for c in range(4):
                        j = 8 * g + 2 * c
                        ins = pe.transpose(bank(5 + g, 4, P)[:, c, :],
                                           kidx[b][:, j:j + 2, :].rearrange("p a b -> p (a b)"), ident)
                    ins.then_inc(sem("kidxT_mm"), 1)
                pe.wait_ge(sem("kidxT_ready"), 2 * b + 2)
                if b == 4:
                    pe.wait_ge(sem("relu_s_ready"), 1)
                r0 = 32 * (b % 4)
                for j in range(NPG):
                    h0 = 64 * (j % 2)
                    mm(bank(2 * (j % 2) + j // 8)[r0:r0 + 32, P * (j // 2 % 4):P * (j // 2 % 4) + P], qi_b[h0:h0 + 64, b, :],
                       kidxT[b % 2][h0:h0 + 64, j // 2, :], True, True)
                mm(bank(4)[r0:r0 + 32, 0:NT], qi_b[0:64, b, :], kkT[0:64, 1, SEQ + NT * b:SEQ + NT * b + NT], True, True
                   ).then_inc(sem("dots_mm"), 1)
            pe.wait_ge(sem("wsT_ready"), 2)
            for g in range(2):
                ins = pe.transpose(bank(7)[:, NS * g:NS * g + NS], rep[0:NS, g, :], ident[0:NS, 0:NS])
            ins.then_inc(*reaches("wsT_mm"))
            pe.wait_ge(*reached("ws_ready"))
            pe.wait_ge(sem("relu_s_ready"), 2)
            for c in range(5):
                w = 512 if c < 4 else NT
                for g in range(2):
                    ins = mm(bank(c)[0:NS, 0:w], ws[:, g, :], relu_s[g][:, 512 * c:512 * c + w], g == 0, g == 1)
            ins.then_inc(*reaches("isum_mm"))
            pe.wait_ge(*reached("work_s_ready"))
            channels(3, 4, "cg_mm", None)
            channels(4, 0, "bg_mm", None)
            pe.wait_ge(sem("cd_ready"), 2 * CA)
            for c in range(CA):
                ins = pe.transpose(bank(7)[0:2, c * P:(c + 1) * P], cd_p[:, c, SEQ:SEQ + 2], ident)
            ins.then_inc(sem("tails1_mm"), 1)
            pe.wait_ge(*reached("cd_last_ready"))
            for c in range(CA):
                ins = pe.transpose(bank(4)[0:16, c * P:(c + 1) * P], cd_last[:, c, :], ident)
            ins.then_inc(sem("tails1_mm"), 1)
            pe.wait_ge(sem("tails1_ready"), 2)
            pe.wait_ge(*reached("conv_d_ready"))
            for i in range(2):
                if i:
                    pe.wait_ge(sem("s_p_taken"), 1)
                for h in range(8):
                    g, r = h // 4, h % 4
                    ins = mm(bank(h // 2)[:, 256 * (h % 2):256 * (h % 2) + 256], qT[64 * g:64 * g + 64, r, P * i:P * i + P],
                             kkT[64 * g:64 * g + 64, 0, 0:SEQ], True, True)
                ins.then_inc(sem("s_p_mm"), 1)
                pe.wait_ge(sem("probs_p_ready"), i + 1)
                for q in range(4):
                    if 4 * i + q >= 2:
                        pe.wait_ge(sem("pt_prompt_ready"), 4 * i + q - 1)
                    for h in range(2 * q, 2 * q + 2):
                        for kc in range(2):
                            ins = pe.transpose(bank(4 + q % 2, 2, 2, P)[:, h % 2, kc, :], probs_p[:, h, kc * P:(kc + 1) * P], ident)
                    ins.then_inc(sem("pt_prompt_mm"), 1)
                pe.wait_ge(sem("pt_prompt_ready"), 4 * i + 4)
                if i:
                    pe.wait_ge(sem("att_ready"), 1)
                for h in range(8):
                    g, r = h // 4, h % 4
                    for kc in range(2):
                        ins = mm(bank(7)[64 * g:64 * g + 64, r * P:(r + 1) * P], v_tok[:, kc, 64 * g:64 * g + 64],
                                 probs_pT[:, h, kc, :], kc == 0, kc == 1)
                ins.then_inc(sem("pv_p_mm"), 1)
            def turn_keys(rows_):
                for b in rows_:
                    pe.wait_ge(sem(f"pages_in{b // 2}"), (2 + (4 if b < 6 else 3)) * 16 * NPG)
                    for g in range(4):
                        if 4 * b + g >= 2:
                            pe.wait_ge(sem("kT_ready"), 4 * b + g - 1)
                        for c in range(4):
                            ins = pe.transpose(bank(5 + g % 2, 4, P)[:, c, :], k_pages[b][:, 4 * g + c, :], ident)
                        ins.then_inc(sem("kT_mm"), 1)

            def scores(q):
                pe.wait_ge(sem("kT_ready"), 8 * q + 8)
                if q:
                    pe.wait_ge(sem("exp_ready"), q)
                for b in (2 * q, 2 * q + 1):
                    r0 = 64 * (b % 2)
                    for c in range(4):
                        pe.matmul(bank(c)[r0:r0 + 64, :], q_blk[:, b, :], k_T[b][:, 512 * c:512 * c + 512], start=True,
                                  stop=False, skip_group_check=True)
                    pe.matmul(bank(4)[r0:r0 + 64, 0:NT], q_blk[:, b, :], kkT[:, 0, SEQ + NT * b:SEQ + NT * b + NT],
                              start=True, stop=False, skip_group_check=True)

            def mask(q):
                for c in range(5):
                    w = 512 if c < 4 else NT
                    ins = pe.matmul(bank(c)[:, 0:w], rep[0:NS, q, :], work_s[0:NS, 512 * c:512 * c + w], start=False,
                                    stop=True, skip_group_check=True)
                ins.then_inc(sem("masked_mm"), 1)

            turn_keys(range(4))
            pe.wait_ge(*reached("q_blk_ready"))
            scores(0)
            turn_keys((4, 5))
            pe.wait_ge(*reached("rep_ready"))
            pe.wait_ge(*reached("bias_s_ready"))
            mask(0)
            pe.wait_ge(sem("kT_ready"), 24)
            for q in range(NB // 2):
                if q < NB // 2 - 1:
                    scores(q + 1)
                    mask(q + 1)
                pe.wait_ge(sem("probs_ready"), q + 1)
                for g in range(5):
                    if g >= 2:
                        pe.wait_ge(sem("pt_ready"), 5 * q + g - 1)
                    for c in range(4 if g < 4 else 1):
                        w = P if g < 4 else NT
                        k0 = (4 * g + c) * P
                        ins = pe.transpose(bank(5 + g % 2)[0:w, c * P:(c + 1) * P], probs[:, k0:k0 + w], ident)
                    ins.then_inc(sem("pt_mm"), 1)
                pe.wait_ge(sem("pt_ready"), 5 * q + 5)
                if q:
                    pe.wait_ge(sem("att_s_ready"), 4 * q)
                else:
                    pe.wait_ge(sem("att_ready"), 2)
                    pe.wait_ge(sem("v_new_in"), 16 * NB)
                if q == 3:
                    pe.wait_ge(sem("pages_in0"), (2 + 4 + 1) * 16 * NPG)
                for b in (2 * q, 2 * q + 1):
                    r0 = 64 * (b % 2)
                    for j in range(NPG):
                        mm(bank(7)[:, r0:r0 + 64], v_pages[b][:, j, :], probsT[:, j, r0:r0 + 64], j == 0, False)
                    mm(bank(7)[:, r0:r0 + 64], v_new[0:NT, b, :], probsT[0:NT, 16, r0:r0 + 64], False, True
                       ).then_inc(sem("pv_mm"), 1)
                if q == 1:
                    turn_keys((6, 7))
            pe.wait_ge(sem("att_s_ready"), 16)
            for h in range(2):
                pe.wait_ge(sem(f"out{h}"), 48)
                for i, t0, n in TILES:
                    for k in range(KD):
                        ins = mm(bank(3 * h + i)[0:n, :], mix1T[:, k, t0:t0 + n], out_piece(h)[:, k, :], k == 0, k == KD - 1)
                    ins.then_inc(sem("out1_mm"), 1)
            norm(3, xn3)
            pe.wait_ge(sem("hT_ready"), 24)
            for i, t0, n in TILES:
                for k in range(KD):
                    ins = mm(bank(6)[0:n, NE * i:NE * i + NE], hT[:, k, t0:t0 + n], w_router[:, k, :], k == 0, k == KD - 1)
            ins.then_inc(*reaches("logits_mm"))
            pe.wait_ge(*reached("routed_ready"))
            for i, t0, n in TILES:
                for j in range(i + 1):
                    nj = TILES[j][2]
                    ins = mm(bank(7)[0:n, NE * i:NE * i + NE], (ones if j < i else K["tri_p"])[0:nj, 0:n],
                             routed[0:nj, j, :], j == 0, j == i)
            for j in range(3):
                nj = TILES[j][2]
                ins = mm(bank(7)[:, 3 * NE:4 * NE], ones[0:nj, :], routed[0:nj, j, :], j == 0, j == 2)
            ins.then_inc(*reaches("rank_mm"))
            def gather(n, e, banks_):
                pe.wait_ge(sem("sel_ready"), 3 * n + 3)
                for g in range(2):
                    for c in range(4):
                        for i, t0, rows_ in TILES:
                            ins = mm(bank(banks_ + g, 4, P)[:, c, 0:CAP], xn3[0:rows_, i, (4 * g + c) * P:(4 * g + c + 1) * P],
                                     sel[0:rows_, i, e, :], i == 0, i == 2)
                    ins.then_inc(sem("moe_h_mm"), 1)

            def turn_sel(n, e, b_):
                pe.wait_ge(sem("gated_ready"), 3 * n + 3)
                for i, t0, rows_ in TILES:
                    ins = pe.transpose(bank(b_)[0:CAP, t0:t0 + rows_], sel[0:rows_, i, e, :], ident[0:rows_, 0:rows_])
                ins.then_inc(sem("selT_mm"), 1)

            def back(experts):
                for i, t0, rows_ in TILES:
                    for h in range(2):
                        for q, (e, at_) in enumerate(experts):
                            ins = mm(bank(2 + 2 * i + h)[0:rows_, :], selT[0:CAP, e, t0:t0 + rows_],
                                     moe_y[0:CAP, at_, 512 * h:512 * h + 512], q == 0, q == len(experts) - 1)
                        ins.then_inc(sem("back_mm"), 1)

            for e in range(NE):
                if e >= 2:
                    pe.wait_ge(sem("moe_h_ready"), 2 * e - 2)
                gather(e, e, 2 * (e % 2))
            for e in range(NE):
                if e >= 2:
                    pe.wait_ge(sem("selT_ready"), e - 1)
                turn_sel(e, e, 4 + e % 2)
            pe.wait_ge(sem("moe_h_ready"), 2 * NE)
            pe.wait_ge(sem("selT_ready"), NE)

            def expert(n, h_in):
                for m in range(2 * NSTEP + 1):
                    if m < 2 * NSTEP:
                        j, q = m // 2, m % 2
                        g, u, dn = slot(j % NSLOT)
                        if q == 0:
                            pe.wait_ge(sem(f"weights{j % NSLOT}"), arrivals(n, j))
                        if m >= 2:
                            pe.wait_ge(sem("ff_ready"), n * 2 * NSTEP + 2 * NSTEP + m - 1)
                        for w, b_, signal in ((g, 2 + 2 * q, "ff_gate_mm"), (u, 3 + 2 * q, "ff_up_mm")):
                            for k in range(KD):
                                ins = mm(bank(b_)[:, 0:CAP], w[:, k, q * P:(q + 1) * P],
                                         h_in(k), k == 0, k == KD - 1)
                            ins.then_inc(sem(signal), 1)
                    if m:
                        c = m - 1
                        pe.wait_ge(sem("ff_ready"), n * 2 * NSTEP + 2 * NSTEP + m)
                        pe.wait_ge(sem("split_lo"), moe_split(n, c))
                        for h in range(2):
                            ins = three(bank(h)[0:CAP, :], [v[:, 0:CAP] for v in moe_ff_parts[c % 2]],
                                        [v[:, 512 * h:512 * h + 512] for v in moe_down_parts], c == 0, c == CHUNKS - 1)
                            if h == 1:
                                ins.then_inc(sem("ff_down_mm"), 1)
                            elif c % 2:
                                ins.then_inc(sem("ff_used"), 1)
            with pe.Fori(0, NE) as e:
                expert(e, lambda k: moe_h[:, ds(e, 1), k, :].rearrange("p a b -> p (a b)"))
            pe.wait_ge(sem("moe_y0"), NE)
            pe.wait_ge(sem("moe_y1"), NE)
            back([(e, e) for e in range(NE)])

            def overflow(w):
                n = w + NE
                pe.wait_ge(sem("y_out_ready"), 6 * w + 6)
                gather(n, 0, 2)
                turn_sel(n, 0, 4)
                pe.wait_ge(sem("moe_h_ready"), 2 * n + 2)
                pe.wait_ge(sem("selT_ready"), n + 1)
                expert(n, lambda k: moe_h[:, 0, k, :])
                pe.wait_ge(sem("moe_y0"), n + 1)
                pe.wait_ge(sem("moe_y1"), n + 1)
                back([(0, 1)])

            while_overflow(pe, overflow)

        @block.vector
        def _(dve):
            own = Own(dve, sem("dve_step"))

            def norm(k, gain, xn=xn):
                dve.wait_ge(sem("ss_ready"), 3 * (k + 1))
                dve.tensor_scalar(ms, ss, 1.0 / D, EPS, ALU.mult, ALU.add).then_inc(sem("ms_ready"), 1)
                dve.wait_ge(sem("rstd_ready"), RSTD[k])
                for i, t0, n in TILES:
                    dve.tensor_scalar(xn[0:n, i, :], x[0:n, i, :], rstd[0:n, i:i + 1], None,
                                      ALU.mult).then_inc(sem("xn_ready"), 1)
                if k == 0:
                    dve.wait_ge(sem("params_ready"), 3)
                for i, t0, n in TILES:
                    for g in range(2):
                        dve.wait_ge(sem("xnT_mm"), 6 * k + 2 * i + g + 1)
                        dve.tensor_tensor(hT[:, 4 * g:4 * g + 4, t0:t0 + n], bank(2 * i + g, 4, n),
                                          gain[:, 4 * g:4 * g + 4].unsqueeze(2).to_broadcast([P, 4, n]),
                                          ALU.mult).then_inc(sem("hT_ready"), 1)

            dve.memset(ss, 1.0).then_inc(sem("cleared"), 1)
            dve.memset(raw_dt.rearrange("p a b -> p (a b)"), 0.0).then_inc(sem("cleared"), 1)
            dve.memset(u_p[:, :, 0:30], 0.0)
            own.link(dve.memset(xbc_p[:, :, 0:3], 0.0))
            norm(0, vecD[:, :, 0])
            for c in range(CA):
                dve.wait_ge(sem("sig_ready"), c + 1)
                dve.tensor_tensor(u_p[:, c, 30:], bank(c)[:, 0:SEQ], ua[:, c, 0:SEQ], ALU.mult)
                dve.tensor_tensor(u_s[:, c, :, 30:], bank(c)[:, SEQ:T].rearrange("p (b t) -> p b t", b=NB),
                                  ua[:, c, SEQ:T].rearrange("p (b t) -> p b t", b=NB), ALU.mult).then_inc(sem("u_ready"), 1)
            dve.wait_ge(sem("u_ready"), CA)
            dve.wait_ge(sem("halo_ready"), 9)

            def conv(dst_p, dst_s, src_p, src_s, taps, bias, width, signal):
                for j in range(width):
                    for dst, src in ((dst_p, src_p[:, j:j + SEQ]), (dst_s, src_s[:, :, j:j + NT])):
                        if j:
                            own.wait(1)
                            ins = dve.scalar_tensor_tensor(dst, src, taps[:, j:j + 1], dst, ALU.mult, ALU.add)
                        else:
                            ins = dve.tensor_scalar(dst, src, taps[:, 0:1], 0.0 if bias is None else bias,
                                                    ALU.mult, ALU.add)
                        if j == width - 1 and dst is dst_s:
                            ins.then_inc(sem(signal), 1)
                        else:
                            own.mark(ins)

            def tokens(a, c):
                return a[:, c, 0:SEQ], a[:, c, SEQ:T].rearrange("p (b t) -> p b t", b=NB)

            for c in range(CA):
                own.wait()
                conv(*tokens(ua, c), u_p[:, c, :], u_s[:, c], vecA[:, c, :], vecA[:, c, 31:32], WA, "ua_ready")
            dve.wait_ge(sem("dt_raw_ready"), 3)
            dve.wait_ge(sem("rows_in"), 16 * 10)
            own.link(dve.tensor_tensor(raw_dt, raw_dt, rows["e_dt_bias"].unsqueeze(1).to_broadcast([P, 3, NH]), ALU.add))
            dve.scalar_tensor_tensor(dt_abs, raw_dt, -1.0, raw_dt, ALU.mult, ALU.max).then_inc(*reaches("dt_abs_ready"))
            for c in range(XC):
                dve.wait_ge(sem("xbc_ready"), c + 1)
                conv(*tokens(xbcT, c), xbc_p[:, c, :], xbc_s[:, c], vecB[:, c, :], vecB[:, c, 4:5], WB, "conv_b_ready")
            dve.wait_ge(*reached("dt_log_ready"))
            own.link(dve.scalar_tensor_tensor(dts, raw_dt, 0.0, dt_log, ALU.max, ALU.add))
            dve.wait_ge(*reached("neg_a_ready"))
            dve.tensor_tensor(dA, dts, neg_a.unsqueeze(1).to_broadcast([P, 3, NH]), ALU.mult).then_inc(*reaches("dA_ready"))
            mean, var, r = small
            dve.wait_ge(*reached("mean_mm"))
            own.link(dve.tensor_scalar(mean, bank(3)[:, 0:T], 1.0 / DA, None, ALU.mult))
            dve.tensor_tensor(ua, ua, mean.unsqueeze(1).to_broadcast([P, CA, T]), ALU.subtract).then_inc(*reaches("ua_centred"))
            dve.wait_ge(*reached("var_mm"))
            dve.tensor_scalar(var, bank(4)[:, 0:T], 1.0 / DA, EPS, ALU.mult, ALU.add).then_inc(*reaches("var_ready"))
            dve.wait_ge(*reached("std_ready"))
            own.link(dve.reciprocal(r, r))
            dve.tensor_tensor(ua, ua, r.unsqueeze(1).to_broadcast([P, CA, T]), ALU.mult).then_inc(*reaches("ua_normed"))
            dve.wait_ge(sem("x_tok_ready"), 9)
            for i, t0, n in TILES:
                xt = x_tok[0:n, i, :].rearrange("p (h q) -> p h q", h=NH)

                def per_head(a):
                    return a[0:n].unsqueeze(2).to_broadcast([n, NH, HP])

                dve.wait_ge(sem("cum_mm"), i + 1)
                own.mark(dve.tensor_scalar(negcum[0:n], bank(0)[0:n, 0:16], -1.0, None, ALU.mult))
                own.mark(dve.tensor_copy(cumT[0:16, 0:n], bank(0)[0:16, 32:32 + n]))
                own.wait()
                dve.tensor_tensor(w_arg[0:n], bank(0)[0:n, 16:32], negcum[0:n], ALU.add).then_inc(sem("cumT_ready"), 1)
                dve.tensor_tensor(xdt[0:n], xt, per_head(dts[:, i, :]), ALU.mult).then_inc(sem("xdt_ready"), 1)
                dve.wait_ge(sem("xdt_ready"), i + 1)
                dve.wait_ge(sem("scan_exps_ready"), i + 1)
                dve.tensor_tensor(xw[0:n], xdt[0:n], per_head(w_end), ALU.mult).then_inc(sem("xw_ready"), 1)
                if i == 2:
                    own.mark(dve.memset(c_pad.rearrange("p a b c -> p (a b c)"), 0.0))
                    own.wait()
                    for b in range(NB):
                        ins = dve.tensor_copy(c_pad[:, :, b, NT * b:NT * b + NT], xbcT[:, 10:12, t0 + NT * b:t0 + NT * b + NT])
                    ins.then_inc(*reaches("c_pad_ready"))
                    dve.wait_ge(sem("p_ssmT_mm"), 2)
                    dve.tensor_copy(dA_rows[0:n].rearrange("p (h q) -> p h q", h=NH),
                                    per_head(dA[:, i, :])).then_inc(*reaches("dA_rows_ready"))
                dve.wait_ge(sem("cb_mm"), i + 1)
                for g in range(NG):
                    dve.wait_ge(sem("decay_ready"), 4 * i + 2 * g + 2)
                    v = decay[0:n, 8 * g:8 * g + 8, 0:n]
                    dve.tensor_tensor(v, v, bank(1, 2, n)[0:n, g, :].unsqueeze(1).to_broadcast([n, 8, n]),
                                      ALU.mult).then_inc(sem("wts_ready"), 1)
                if i < 2:
                    dve.wait_ge(sem("state_mm"), i + 1)
                    if i == 1:
                        dve.wait_ge(*reached("inter_mm"))
                        v = p_state.rearrange("p (h q) -> p h q", h=NH)
                        own.link(dve.tensor_tensor(v, v, per_head(e_last), ALU.mult))
                    for g in range(2):
                        v = p_state[:, 512 * g:512 * g + 512]
                        if i == 0:
                            dve.tensor_copy(v, bank(4 + g)).then_inc(sem("p_state_ready"), 1)
                        else:
                            dve.tensor_tensor(v, v, bank(4 + g), ALU.add).then_inc(sem("p_state_ready"), 1)
                else:
                    for b in range(NB):
                        if b >= 2:
                            dve.wait_ge(sem("h_add_mm"), b - 1)
                        dve.tensor_scalar(b_one[0:n, b % 2, :], b_tok[0:n, i, :], K["batch"][0:n, b:b + 1], None,
                                          ALU.mult).then_inc(sem("b_one_ready"), 1)
                        if b == 0:
                            dve.wait_ge(*reached("decs_ready"))
                            dve.wait_ge(sem("p_ssm_stored"), 16)
                        if b >= 2:
                            dve.wait_ge(sem(f"h_stored{b % 2}"), 16 * (b // 2))
                        dve.wait_ge(sem(f"h_old{b % 2}"), 16 * (b // 2 + 1))
                        dve.wait_ge(sem("h_add_mm"), b + 1)
                        for c in range(KD):
                            dve.scalar_tensor_tensor(h_new[b % 2][:, c, :], h_old[b % 2][:, c, :], decs[:, c, b:b + 1],
                                                     bank(c // 4, 4, P)[:, c % 4, :], ALU.mult, ALU.add
                                                     ).then_inc(sem("h_new_ready"), 1)
                dve.wait_ge(sem("y_mm"), i + 1)
                if i:
                    dve.wait_ge(*reached("inter_mm"))
                    if i == 2:
                        dve.wait_ge(sem("inter_acc"), 2 * NB)
                    for g in range(2):
                        own.mark(dve.tensor_tensor(y[0:n, 8 * g:8 * g + 8, :], bank(2 + g, 8, HP)[0:n],
                                                   e_cum[0:n, 8 * g:8 * g + 8].unsqueeze(2).to_broadcast([n, 8, HP]), ALU.mult))
                    own.wait()
                    for g in range(2):
                        own.mark(dve.tensor_tensor(y[0:n, 8 * g:8 * g + 8, :], y[0:n, 8 * g:8 * g + 8, :],
                                                   bank(6 + g, 8, HP)[0:n], ALU.add))
                else:
                    for g in range(2):
                        own.mark(dve.tensor_copy(y[0:n, 8 * g:8 * g + 8, :], bank(6 + g, 8, HP)[0:n]))
                own.link(dve.tensor_tensor(xt, xt, per_head(rows["e_d_skip"]), ALU.mult))
                own.link(dve.tensor_tensor(y[0:n], y[0:n], xt, ALU.add))
                dve.wait_ge(sem("xw_ready"), i + 1)
                dve.wait_ge(sem("z_ready"), 6)
                dve.tensor_tensor(y[0:n], y[0:n], z[0:n, i, :].rearrange("p (h q) -> p h q", h=NH), ALU.mult
                                  ).then_inc(sem("y_ready"), 1)
                dve.wait_ge(sem("gs_ready"), 2 * i + 2)
                dve.tensor_scalar(gms, gs, 2.0 / D, EPS, ALU.mult, ALU.add).then_inc(sem("ms_ready"), 1)
                dve.wait_ge(sem("rstd_ready"), 2 + i)
                for g in range(2):
                    ins = dve.tensor_scalar(y[0:n, 8 * g:8 * g + 8, :], y[0:n, 8 * g:8 * g + 8, :], grs[0:n, g:g + 1],
                                            None, ALU.mult)
                ins.then_inc(sem("yn_ready"), 1)
                for g in range(2):
                    dve.wait_ge(sem("yT_mm"), 2 * i + g + 1)
                    dve.tensor_tensor(mixT[:, 4 + 4 * g:8 + 4 * g, t0:t0 + n], bank(g, 4, n),
                                      vecD[:, 4 * g:4 * g + 4, 2:3].to_broadcast([P, 4, n]), ALU.mult
                                      ).then_inc(sem("mixT_ready"), 1)
            for h in range(2):
                for i, t0, n in TILES:
                    dve.wait_ge(sem("mix_out_mm"), 4 * h + 2 + i)
                    v = x[0:n, i, 512 * h:512 * h + 512]
                    dve.tensor_tensor(v, v, bank(3 * h + i)[0:n, :], ALU.add).then_inc(sem("x_ready"), 1)
            norm(1, vecD[:, :, 1])
            dve.wait_ge(*reached("x_hi_ready"))
            dve.wait_ge(sem("hT_ready"), 12)
            dve.tensor_tensor(x_parts[1], hT, x_parts[0].bitcast(F32), ALU.subtract).then_inc(*reaches("x_lo_ready"))

            def split_lo(kind, m):
                dve.wait_ge(sem("split_hi"), split_at(kind, m))
                parts_ = to_split(kind, m)
                for n, (src, upper, rest) in enumerate(parts_):
                    ins = dve.tensor_tensor(rest, src, upper.bitcast(F32), ALU.subtract)
                ins.then_inc(sem("split_lo"), 1)
                if kind == "down" and m % 2:
                    dve.wait_ge(sem("split_lo"), split_at(kind, m))
                    dve.sem_inc(sem("ff_used"), 1)

            for kind, m in SPLITS[:3]:
                split_lo(kind, m)
            for m in range(CHUNKS):
                dve.wait_ge(sem("ff_up_mm"), m + 1)
                dve.wait_ge(sem("ff_silu"), m + 1)
                if m >= 2:
                    dve.wait_ge(sem("ff_down_mm"), m - 1)
                own.link(dve.tensor_tensor(ff, silu_t[:, m % 2, :], bank(7)[:, 0:T], ALU.mult))
                own.link(dve.tensor_copy(ff_parts[m % 2][0], ff))
                dve.tensor_tensor(ff_parts[m % 2][1], ff, ff_parts[m % 2][0].bitcast(F32), ALU.subtract
                                  ).then_inc(sem("ff_ready"), 1)
                if m + 2 < CHUNKS:
                    split_lo("gu", m + 2)
                if m + 1 < CHUNKS:
                    split_lo("down", m + 1)

            def residual(first_bank, order, mm_signal, done):
                for q, (i, h) in enumerate(order):
                    n = TILES[i][2]
                    if mm_signal:
                        dve.wait_ge(sem(mm_signal), q + 1)
                    v = x[0:n, i, 512 * h:512 * h + 512]
                    dve.tensor_tensor(v, v, bank(first_bank + q)[0:n, :], ALU.add).then_inc(sem(done), 1)

            dve.wait_ge(sem("ff_down_mm"), CHUNKS)
            residual(0, [(i, h) for i in range(3) for h in range(2)], None, "x_ready")
            norm(2, vecD[:, :, 3])
            dve.memset(tok[:, 2, :], 0.0).then_inc(*reaches("tok_cleared"))
            dve.wait_ge(sem("tok_ready"), 8)
            ki = tok[:, :, 1024:1088]
            own.link(dve.reduce_sum(ki_s, ki, AX))
            own.link(dve.tensor_scalar(ki_s, ki_s, 1.0 / HD, None, ALU.mult))
            dve.tensor_tensor(ki, ki, ki_s.unsqueeze(2).to_broadcast([P, 3, HD]), ALU.subtract).then_inc(*reaches("ki_centred"))
            dve.wait_ge(*reached("ki_squared"))
            own.link(dve.reduce_sum(ki_v, rope_t[0].rearrange("p a b c -> p a (b c)")[:, :, 0:64], AX))
            dve.tensor_scalar(ki_ms, ki_v, 1.0 / HD, EPS, ALU.mult, ALU.add).then_inc(sem("ms_ready"), 1)
            dve.wait_ge(*reached("qk_squared"))
            own.link(dve.reduce_sum(qk_ss, squares1.rearrange("p a (h d) -> p (a h) d", d=HD), AX))
            dve.tensor_scalar(qk_ms, qk_ss, 1.0 / HD, EPS, ALU.mult, ALU.add).then_inc(sem("ms_ready"), 1)
            dve.wait_ge(sem("rstd_ready"), 7)
            own.link(dve.tensor_tensor(ki, ki, ki_rs.unsqueeze(2).to_broadcast([P, 3, HD]), ALU.mult))
            own.link(dve.tensor_tensor(ki, ki, rows["o_kidx_g"].unsqueeze(1).to_broadcast([P, 3, HD]), ALU.mult))
            own.link(dve.tensor_tensor(ki, ki, rows["o_kidx_b"].unsqueeze(1).to_broadcast([P, 3, HD]), ALU.add))
            dve.wait_ge(sem("rstd_ready"), 8)
            for i in range(3):
                v = tok[:, i, 0:640].rearrange("p (h d) -> p h d", d=HD)
                own.mark(dve.tensor_tensor(v, v, qk_rs[:, 10 * i:10 * i + 10].unsqueeze(2).to_broadcast([P, 10, HD]), ALU.mult))
            own.wait()
            for i in range(3):
                v = tok[:, i, 0:640].rearrange("p (h d) -> p h d", d=HD)
                own.mark(dve.tensor_tensor(v[:, 0:8], v[:, 0:8], rows["o_q_norm"].unsqueeze(1).to_broadcast([P, 8, HD]), ALU.mult))
                own.mark(dve.tensor_tensor(v[:, 8:10], v[:, 8:10], rows["o_k_norm"].unsqueeze(1).to_broadcast([P, 2, HD]), ALU.mult))
            own.wait()
            for a, heads in ((0, 10), (768, 5)):
                v = tok[:, :, a:a + HD * heads].rearrange("p a (h d) -> p a h d", d=HD)
                one, two = v[:, :, :, 0:8], v[:, :, :, 8:16]
                c_, s_ = (f.unsqueeze(2).to_broadcast([P, 3, heads, 8]) for f in (cos, sin))
                t = [r_[:, :, 0:heads, :] for r_ in rope_t]
                own.mark(dve.tensor_tensor(t[0], one, c_, ALU.mult))
                own.mark(dve.tensor_tensor(t[1], two, s_, ALU.mult))
                own.mark(dve.tensor_tensor(t[2], one, s_, ALU.mult))
                own.mark(dve.tensor_tensor(t[3], two, c_, ALU.mult))
                own.wait()
                dve.tensor_tensor(one, t[0], t[1], ALU.subtract)
                dve.tensor_tensor(two, t[2], t[3], ALU.add).then_inc(sem("rot_ready"), 1)
                dve.wait_ge(sem("rot_ready"), 1 if a == 0 else 2)
            for i in range(3):
                own.mark(dve.tensor_copy(q_tok[:, i].rearrange("p r (g d) -> p r g d", g=2),
                                         tok[:, i, 0:512].rearrange("p (g r d) -> p r g d", g=2, r=4)))
                own.mark(dve.tensor_copy(qi_tok[:, i].rearrange("p h (u d) -> p h u d", u=2),
                                         tok[:, i, 768:1024].rearrange("p (h d) -> p h d", d=HD).unsqueeze(2).to_broadcast([P, 4, 2, HD])))
            dve.tensor_copy(ki_tok.rearrange("p a (u d) -> p a u d", u=2),
                            ki.unsqueeze(2).to_broadcast([P, 3, 2, HD])).then_inc(sem("rot_ready"), 1)
            dve.wait_ge(sem("rotT_mm"), 9)
            dve.memset(cd_p[:, :, 0:2], 0.0).then_inc(*reaches("din_free"))
            dve.wait_ge(sem("rotT_ready"), 9)
            dve.wait_ge(sem("v_ready"), 2)
            dve.tensor_copy(qi_b.rearrange("p b (h t) -> p b h t", h=4),
                            qiT[:, :, SEQ:T].rearrange("p h (b t) -> p b h t", b=NB)).then_inc(*reaches("q_packed"))
            for g in range(2):
                dve.tensor_tensor(rep[0:NS, g, :].rearrange("p (b h t) -> p b h t", b=4, h=4),
                                  ident[0:NS, 32 * g:32 * g + 32].rearrange("p (b t) -> p b t", b=4).unsqueeze(2).to_broadcast([NS, 4, 4, 8]),
                                  w_idx[0:NS, 2, :].unsqueeze(1).unsqueeze(3).to_broadcast([NS, 4, 4, 8]), ALU.mult
                                  ).then_inc(sem("wsT_ready"), 1)

            def choose(work, count, between=None):
                for n in range(count // 8):
                    own.link(dve.max(best[0:work.shape[0]], work))
                    own.link(dve.match_replace(work, best[0:work.shape[0]], work, TAKEN))
                    if between and n in between:
                        between[n]()

            for i in range(2):
                dve.wait_ge(sem("relu_p_ready"), i + 1)
                v = sc_p[:, i, :]
                own.link(dve.tensor_scalar(v, relu_p[:, 0, :], w_idx[:, i, 0:1], None, ALU.mult))
                for h in range(1, 4):
                    own.mark(dve.scalar_tensor_tensor(v, relu_p[:, h, :], w_idx[:, i, h:h + 1], v, ALU.mult, ALU.add))
                    own.wait()
                dve.tensor_tensor(v, v, causal[:, i, :], ALU.add).then_inc(sem("sc_p_ready"), 1)
            dve.wait_ge(sem("sc_p_ready"), 2)
            for i in range(2):
                choose(sc_p[:, i, :], TOPP)
            own.link(dve.tensor_scalar(bias_p, sc_p, -2e38, NEG, ALU.is_gt, ALU.mult))
            dve.tensor_tensor(bias_p, bias_p, causal, ALU.min).then_inc(*reaches("sc_p_taken"))
            dve.wait_ge(*reached("sc_p_taken"))
            dve.wait_ge(*reached("isum_mm"))
            own.link(dve.tensor_copy(work_s[0:NS, :], psum[0:NS, 0:KEYS]))
            own.link(dve.tensor_tensor(work_s[0:NS, PAST:], work_s[0:NS, PAST:], K["new_ok"][0:NS], ALU.mult))
            dve.tensor_tensor(work_s[0:NS, PAST:], work_s[0:NS, PAST:], K["new_neg"][0:NS], ALU.add).then_inc(*reaches("work_s_ready"))
            dve.wait_ge(*reached("wsT_mm"))
            dve.tensor_copy(rep[0:NS].rearrange("p q (b g t) -> p (q b) g t", b=2, g=8),
                            ident[0:NS, 0:NS].rearrange("p (b t) -> p b t", b=NB).unsqueeze(2).to_broadcast([NS, NB, 8, NT])
                            ).then_inc(*reaches("rep_ready"))

            def short_conv():
                for c in range(CA):
                    dve.wait_ge(sem("din_ready"), c + 1)
                    dve.wait_ge(sem("cg_mm"), c + 1)
                    v, w, mul = cd_p[:, c, 2:], cd_s[:, c, :, 2:], bank(4 + c)
                    dve.tensor_tensor(v, v, mul[:, 0:SEQ], ALU.mult).then_inc(sem("cd_ready"), 1)
                    dve.tensor_tensor(w, w, mul[:, SEQ:T].rearrange("p (b t) -> p b t", b=NB),
                                      ALU.mult).then_inc(sem("cd_ready"), 1)
                dve.wait_ge(sem("cd_ready"), 2 * CA)
                dve.wait_ge(sem("halo1_ready"), 1)
                dve.tensor_copy(cd_last.rearrange("p c (b t) -> p c b t", b=NB), cd_s[:, :, :, NT:NT + 2]
                                ).then_inc(*reaches("cd_last_ready"))
                for c in range(CA):
                    conv(*tokens(mix1T, 4 + c), cd_p[:, c, :], cd_s[:, c], vecA[:, c, 34:37], None, 3, "conv_d_taps")

            def conv_gate():
                for c in range(CA):
                    dve.wait_ge(sem("conv_d_taps"), c + 1)
                    dve.wait_ge(sem("bg_mm"), c + 1)
                    v = mix1T[:, 4 + c, :]
                    ins = dve.tensor_tensor(v, v, bank(c)[:, 0:T], ALU.mult)
                ins.then_inc(*reaches("conv_d_ready"))
                dve.wait_ge(sem("tails1_mm"), 2)
                own.mark(dve.memset(q_blk.rearrange("p a b -> p (a b)"), 0.0))
                own.wait()
                for g in range(2):
                    for r in range(4):
                        ins = dve.tensor_copy(q_blk[64 * g:64 * g + 64, :, 32 * g + 8 * r:32 * g + 8 * r + 8],
                                              qT[64 * g:64 * g + 64, r, SEQ:T].rearrange("p (b t) -> p b t", b=NB))
                ins.then_inc(*reaches("q_blk_ready"))

            def prompt_max(i):
                dve.wait_ge(sem("s_p_mm"), i + 1)
                if i:
                    dve.wait_ge(sem("pt_prompt_mm"), 4)
                own.link(dve.tensor_tensor(probs_p, psum[:, 0:8 * SEQ].rearrange("p (h k) -> p h k", h=8),
                                           bias_p[:, i, :].unsqueeze(1).to_broadcast([P, 8, SEQ]), ALU.add))
                dve.reduce_max(mx, probs_p, AX).then_inc(sem("s_p_taken"), 1)
                dve.wait_ge(sem("s_p_taken"), i + 1)
                dve.tensor_scalar(nmx, mx, -HD ** -0.5, None, ALU.mult).then_inc(sem("nmx_p_ready"), 1)

            def prompt_probs(i):
                dve.wait_ge(sem("exp_p_ready"), i + 1)
                dve.reciprocal(rsum, sums).then_inc(sem("rsum_p_ready"), 1)

            dve.wait_ge(*reached("work_s_ready"))
            choose(work_s[0:NS, :], TOPS, {4: short_conv, 6: conv_gate, 7: lambda: prompt_max(0), 8: lambda: prompt_probs(0),
                                           11: lambda: prompt_max(1), 12: lambda: prompt_probs(1)})
            dve.tensor_scalar(work_s[0:NS, :], work_s[0:NS, :], -2e38, NEG, ALU.is_gt, ALU.mult).then_inc(*reaches("bias_s_ready"))

            def row_max(q):
                dve.wait_ge(sem("masked_mm"), q + 1)
                own.link(dve.reduce_max(mx[:, 0:1], psum[:, 0:KEYS], AX))
                dve.tensor_scalar(nmx[:, 0:1], mx[:, 0:1], -HD ** -0.5, None, ALU.mult).then_inc(sem("nmx_ready"), 1)

            row_max(0)
            for q in range(NB // 2):
                dve.wait_ge(sem("exp_ready"), q + 1)
                own.link(dve.reciprocal(rsum[:, 0:1], sums[:, 0:1]))
                dve.tensor_scalar(probs, probs, rsum[:, 0:1], None, ALU.mult).then_inc(sem("probs_ready"), 1)
                if q < NB // 2 - 1:
                    row_max(q + 1)
                dve.wait_ge(sem("pv_mm"), 2 * q + 2)
                for b in range(2):
                    for g in range(2):
                        t0 = SEQ + NT * (2 * q + b)
                        dve.tensor_copy(mix1T[64 * g:64 * g + 64, 0:4, t0:t0 + NT],
                                        bank(7)[64 * g:64 * g + 64, 64 * b + 32 * g:64 * b + 32 * g + 32].rearrange("p (r t) -> p r t", r=4)
                                        ).then_inc(sem("att_s_ready"), 1)
            residual(0, [(i, h) for h in range(2) for i in range(3)], "out1_mm", "x_ready")
            norm(3, vecD[:, :, 4], xn3)
            for a in (logits, routed, gate, rank):
                own.mark(dve.memset(a.rearrange("p a b -> p (a b)"), 0.0))
            own.wait()
            dve.wait_ge(*reached("logits_mm"))
            b_r = rows["o_b_router"]
            own.mark(dve.tensor_tensor(logits[:, 0:2], bank(6)[:, 0:16].rearrange("p (a b) -> p a b", a=2),
                                       b_r.unsqueeze(1).to_broadcast([P, 2, NE]), ALU.add))
            own.mark(dve.tensor_tensor(logits[0:NS, 2], bank(6)[0:NS, 16:24], b_r[0:NS], ALU.add))
            own.wait()
            for i in range(3):
                own.mark(dve.max(top[:, i, :], logits[:, i, :]))
            own.wait()
            for i in range(3):
                own.mark(dve.max_index(top_i[:, i, :], top[:, i, :], logits[:, i, :]))
            own.wait()
            own.link(dve.tensor_copy(top_f, top_i))
            for i in range(3):
                for k, a in ((0, first), (1, second)):
                    own.mark(dve.tensor_scalar(a[:, i, :], K["slots"][:, 0:NE], top_f[:, i, k:k + 1], None, ALU.is_equal))
            own.wait()
            own.mark(dve.tensor_tensor(routed[:, 0:2], first[:, 0:2], second[:, 0:2], ALU.add))
            dve.tensor_tensor(routed[0:NS, 2], first[0:NS, 2], second[0:NS, 2], ALU.add).then_inc(*reaches("routed_ready"))
            dve.tensor_tensor(gap, top[:, :, 1], top[:, :, 0], ALU.subtract).then_inc(*reaches("gap_ready"))
            dve.wait_ge(*reached("e_gap_ready"))
            own.link(dve.tensor_scalar(g_one, e_gap, 1.0, None, ALU.add))
            own.link(dve.reciprocal(g_one, g_one))
            own.link(dve.tensor_tensor(g_two, g_one, e_gap, ALU.mult))
            own.mark(dve.tensor_tensor(first, first, g_one.unsqueeze(2).to_broadcast([P, 3, NE]), ALU.mult))
            own.mark(dve.tensor_tensor(second, second, g_two.unsqueeze(2).to_broadcast([P, 3, NE]), ALU.mult))
            own.wait()
            own.link(dve.tensor_tensor(gate, first, second, ALU.add))
            dve.wait_ge(*reached("rank_mm"))
            own.mark(dve.tensor_scalar(rank[:, 0:2], bank(7)[:, 0:16].rearrange("p (a b) -> p a b", a=2), -1.0, None, ALU.add))
            own.mark(dve.tensor_scalar(rank[0:NS, 2], bank(7)[0:NS, 16:24], -1.0, None, ALU.add))
            own.wait()

            own.link(dve.tensor_copy(counts, bank(7)[:, 3 * NE:4 * NE]))
            own.mark(dve.tensor_scalar(more[0], counts, float(CAP), None, ALU.is_gt))
            for k in range(2, NBLOCK):
                own.mark(dve.tensor_scalar(more[k - 1], counts, float(k * CAP), None, ALU.is_gt))
            own.mark(dve.memset(upto[0][:, 0:8], 0.0))
            own.mark(dve.memset(upto[1][:, 0:8], 0.0))
            own.wait()
            for k in range(2, NBLOCK):
                own.link(dve.tensor_tensor(more[0], more[0], more[k - 1], ALU.add))
            own.link(dve.tensor_copy(upto[0][:, 8:16], more[0]))
            for k, shift in enumerate((1, 2, 4)):
                own.link(dve.tensor_tensor(upto[(k + 1) % 2][:, 8:16], upto[k % 2][:, 8:16],
                                           upto[k % 2][:, 8 - shift:16 - shift], ALU.add))
            total = upto[1][:, 8:16]
            for w in range(NOVER):
                own.mark(dve.tensor_scalar(before, total, float(w), 0.0, ALU.is_le, ALU.add, accum_out=over_e[:, w:w + 1]))
                own.wait()
                own.mark(dve.tensor_tensor(before, before, more[0], ALU.mult))
                own.wait()
                own.link(dve.reduce_sum(over_at[:, w:w + 1], before, AX))
                own.link(dve.tensor_scalar(over_at[:, w:w + 1], over_at[:, w:w + 1], -float(CAP), float(CAP * (w + 1)),
                                           ALU.mult, ALU.add))
            own.link(dve.tensor_copy(over_e[:, NOVER:NOVER + 1], total[:, 7:8]))
            dve.tensor_copy(over_i, over_e).then_inc(*reaches("over_ready"))

            def slots(rank_of, weight, e, done):
                for i, t0, n in TILES:
                    dve.tensor_scalar(sel[0:n, i, e, :], K["slots"][0:n, 0:CAP], rank_of(i)[0:n], weight(i)[0:n],
                                      ALU.is_equal, ALU.mult).then_inc(sem(done), 1)

            def column(a, e):
                return lambda i: a[:, i, e:e + 1] if isinstance(e, int) else a[:, i, ds(e, 1)]

            def slot_features(n, e, banks_):
                for g in range(2):
                    dve.wait_ge(sem("moe_h_mm"), 2 * n + g + 1)
                    dve.tensor_tensor(moe_h[:, e, 4 * g:4 * g + 4, :], bank(banks_ + g, 4, P)[:, :, 0:CAP],
                                      vecD[:, 4 * g:4 * g + 4, 4:5].to_broadcast([P, 4, CAP]), ALU.mult
                                      ).then_inc(sem("moe_h_ready"), 1)

            def expert(n, y_out):
                for m in range(2 * NSTEP):
                    dve.wait_ge(sem("ff_up_mm"), n * 2 * NSTEP + 2 * NSTEP + m + 1)
                    dve.wait_ge(sem("ff_silu"), n * 2 * NSTEP + 2 * NSTEP + m + 1)
                    dve.tensor_tensor(moe_ff[:, m % 4, :], moe_silu[:, m % 2, :], bank(3 + 2 * (m % 2))[:, 0:CAP],
                                      ALU.mult).then_inc(sem("moe_ff_step"), 1)
                    dve.wait_ge(sem("ff_down_mm"), downs(n, m - 1))
                    dve.wait_ge(sem("moe_ff_step"), n * 2 * CHUNKS + 2 * m + 1)
                    dve.tensor_copy(moe_ff_parts[m % 2][0][:, 0:CAP], moe_ff[:, m % 4, :]).then_inc(sem("moe_ff_step"), 1)
                    dve.wait_ge(sem("moe_ff_step"), n * 2 * CHUNKS + 2 * m + 2)
                    dve.tensor_tensor(moe_ff_parts[m % 2][1][:, 0:CAP], moe_ff[:, m % 4, :],
                                      moe_ff_parts[m % 2][0][:, 0:CAP].bitcast(F32), ALU.subtract).then_inc(sem("ff_ready"), 1)
                    dve.wait_ge(sem("split_hi"), moe_split(n, m))
                    dve.tensor_tensor(moe_down_parts[1], slot(m // 2 % NSLOT)[2][:, m % 2, :], moe_down_parts[0].bitcast(F32),
                                      ALU.subtract).then_inc(sem("split_lo"), 1)
                dve.wait_ge(sem("ff_down_mm"), downs(n, CHUNKS))
                dve.tensor_copy(y_out, bank(0)[0:CAP].unsqueeze(1)).then_inc(sem("moe_y0"), 1)

            for e in range(NE):
                slots(column(rank, e), column(routed, e), e, "sel_ready")
            for e in range(NE):
                slot_features(e, e, 2 * (e % 2))
            for e in range(NE):
                slots(column(rank, e), column(gate, e), e, "gated_ready")
            with dve.Fori(0, NE) as e:
                expert(e, moe_y[0:CAP, ds(e, 1), 0:512])
            order = [(i, h) for i in range(3) for h in range(2)]
            residual(2, order, "back_mm", "y_out_ready")

            def overflow(w):
                n = w + NE
                e = dve.value_load(over_i[0:1, ds(w, 1)], min_val=0, max_val=NE - 1)
                dve.tensor_tensor(over_rank, rank[:, :, ds(e, 1)], over_at[:, ds(w, 1)].unsqueeze(1).to_broadcast([P, 3, 1]),
                                  ALU.subtract).then_inc(sem("over_step"), 1)
                dve.wait_ge(sem("over_step"), w + 1)
                slots(lambda i: over_rank[:, i, :], column(routed, e), 0, "sel_ready")
                slot_features(n, 0, 2)
                slots(lambda i: over_rank[:, i, :], column(gate, e), 0, "gated_ready")
                expert(n, moe_y[0:CAP, 1:2, 0:512])
                for q, (i, h) in enumerate(order):
                    rows_ = TILES[i][2]
                    dve.wait_ge(sem("back_mm"), 6 * w + 7 + q)
                    v = x[0:rows_, i, 512 * h:512 * h + 512]
                    ins = dve.tensor_tensor(v, v, bank(2 + q)[0:rows_, :], ALU.add)
                    ins.then_inc(sem("y_out_ready"), 1)

            while_overflow(dve, overflow)


INS = ['x_prompt', 'x_sample', 'state_conv_a', 'state_ssm', 'state_conv_b', 'cache_k', 'cache_v', 'cache_kidx',
       'state_conv_d', 'page_table', 'e_norm_mix', 'e_w_in', 'e_conv_a_w', 'e_conv_a_b', 'e_ln_a_g', 'e_ln_a_b',
       'e_conv_b_w', 'e_conv_b_b', 'e_dt_bias', 'e_a_log', 'e_d_skip', 'e_ssm_norm', 'e_w_out', 'e_norm_ffn',
       'e_w_gate', 'e_w_up', 'e_w_down', 'o_norm_mix', 'o_w_in', 'o_q_norm', 'o_k_norm', 'o_kidx_g', 'o_kidx_b',
       'o_conv_d_w', 'o_w_out', 'o_norm_ffn', 'o_w_router', 'o_b_router', 'o_we_gate', 'o_we_up', 'o_we_down']
OUTS = [("y_prompt", (1, SEQ, D)), ("y_sample", (NB, NT, D)), ("p_conv_a", (1, 1, WA - 1, DA)),
        ("p_ssm", (1, 1, NH, HP, NST)), ("p_conv_b", (1, 1, WB - 1, XC * P)), ("p_k", (1, 1, SEQ, 2, HD)),
        ("p_v", (1, 1, SEQ, 2, HD)), ("p_kidx", (1, 1, SEQ, HD)), ("p_conv_d", (1, 1, 2, DA)),
        ("s_conv_a", (1, NB, WA - 1, DA)), ("s_ssm", (1, NB, NH, HP, NST)), ("s_conv_b", (1, NB, WB - 1, XC * P)),
        ("s_k", (1, NB, NT, 2, HD)), ("s_v", (1, NB, NT, 2, HD)), ("s_kidx", (1, NB, NT, HD)),
        ("s_conv_d", (1, NB, 2, DA))]


def kernel(**inputs):
    import numpy as np
    from concourse import bacc
    from concourse.bass_utils import run_bass_kernel_spmd

    nc = bacc.Bacc("TRN2", target_bir_lowering=False, num_devices=1)
    arrays = {"constants": constants()}
    for name in INS:
        arrays[name] = np.ascontiguousarray(inputs[name])
    inp = {n: nc.dram_tensor(n, a.shape, mybir.dt.from_np(a.dtype), kind="ExternalInput").ap()
           for n, a in arrays.items()}
    out = {n: nc.dram_tensor(n, s, F32, kind="ExternalOutput").ap() for n, s in OUTS}
    step_program(nc, inp, out)
    r = run_bass_kernel_spmd(nc, [arrays], core_ids=[0])
    return tuple(r.results[0][n] for n, _ in OUTS)
```
